# Optimizing a Trainium2 kernel written in Bass

```python
import jax, jax.numpy as jnp
from jax import lax
import numpy as np

D_MODEL = 1024
BATCH = 1
SEQ = 2048
DEPTH = 1

HEAD_DIM = D_MODEL // 16
CONV_HEADS = 8
FFT_GROUPS = 8
CONV_CH = CONV_HEADS * HEAD_DIM
FFT_CH = FFT_GROUPS * HEAD_DIM
MIX_WIDTH = CONV_CH + FFT_CH
MIX_HEADS = CONV_HEADS + FFT_GROUPS
IN_COLS = 3 * CONV_CH + FFT_CH
CONV_K = 3
MEM_LEN = 256
XA_HEADS = 4
XA_HEAD_DIM = D_MODEL // XA_HEADS
N_GROUPS = 4
EXPERTS_PER_GROUP = 8
N_EXPERTS = N_GROUPS * EXPERTS_PER_GROUP
TOP_K = 2
D_EXPERT = D_MODEL // 2
ROUTE_BLOCK = 128
EPS = 1e-6

kernel_name = "hybrid_conv_fourier_xattn_hmoe_encoder"

def rmsnorm(x, g):
    xf = x.astype(jnp.float32)
    y = xf * lax.rsqrt(jnp.mean(xf * xf, axis=-1, keepdims=True) + EPS)
    return (y * g.astype(jnp.float32)).astype(x.dtype)

def parallel_mixer(h, w_in, conv_w, conv_b, head_norm_g, w_out):
    B, S, _ = h.shape
    u = h @ w_in
    b_gate, c_gate, v, u_f = jnp.split(u, [CONV_CH, 2 * CONV_CH, 3 * CONV_CH], axis=-1)
    z = lax.conv_general_dilated(
        c_gate * v, conv_w[:, None, :], window_strides=(1,),
        padding=[(CONV_K // 2, CONV_K // 2)],
        dimension_numbers=("NWC", "WIO", "NWC"),
        feature_group_count=CONV_CH) + conv_b
    y_conv = (b_gate * z).reshape(B, S, CONV_HEADS, HEAD_DIM)
    uf = u_f.reshape(B, S, FFT_GROUPS, HEAD_DIM).astype(jnp.float32)
    y_fft = jnp.fft.fftn(uf, axes=(1, 3), norm="ortho").real.astype(h.dtype)
    heads = jnp.concatenate([y_conv, y_fft], axis=2)
    heads = rmsnorm(heads, head_norm_g)
    return heads.reshape(B, S, MIX_WIDTH) @ w_out

def memory_cross_attention(h, m, w_q, w_kv, w_o):
    B, S, _ = h.shape
    q = (h @ w_q).reshape(B, S, XA_HEADS, XA_HEAD_DIM)
    k, v = jnp.split(m @ w_kv, 2, axis=-1)
    k = k.reshape(B, -1, XA_HEADS, XA_HEAD_DIM)
    v = v.reshape(B, -1, XA_HEADS, XA_HEAD_DIM)
    s = jnp.einsum("bqhd,bkhd->bhqk", q, k).astype(jnp.float32) * (XA_HEAD_DIM ** -0.5)
    p = jax.nn.softmax(s, axis=-1).astype(v.dtype)
    o = jnp.einsum("bhqk,bkhd->bqhd", p, v).reshape(B, S, D_MODEL)
    return o @ w_o

def hierarchical_moe(h, w_rg, b_rg, w_re, b_re, w_gate, w_up, w_down):
    B, S, D = h.shape
    T = B * S
    hf = h.reshape(T, D)
    g_prob = jax.nn.softmax((hf @ w_rg).astype(jnp.float32) + b_rg.astype(jnp.float32), axis=-1)
    g_idx = jnp.argmax(g_prob, axis=-1).astype(jnp.int32)
    g_w = jnp.take_along_axis(g_prob, g_idx[:, None], axis=-1)
    e_logits = ((hf @ w_re).astype(jnp.float32) + b_re.astype(jnp.float32)).reshape(T, N_GROUPS, EXPERTS_PER_GROUP)
    e_logits = jnp.take_along_axis(e_logits, g_idx[:, None, None], axis=1)[:, 0]
    e_prob = jax.nn.softmax(e_logits, axis=-1)
    top_p, top_e = lax.top_k(e_prob, TOP_K)
    gate = (g_w * top_p / jnp.sum(top_p, axis=-1, keepdims=True)).reshape(-1)
    eid = (g_idx[:, None] * EXPERTS_PER_GROUP + top_e.astype(jnp.int32)).reshape(-1)
    tok = jnp.arange(T * TOP_K, dtype=jnp.int32) // TOP_K
    order = jnp.argsort(eid)
    se = eid[order]
    counts = jnp.bincount(eid, length=N_EXPERTS)
    starts = jnp.cumsum(counts) - counts
    padded = (counts + ROUTE_BLOCK - 1) // ROUTE_BLOCK * ROUTE_BLOCK
    pend = jnp.cumsum(padded)
    pstart = pend - padded
    dest = pstart[se] + jnp.arange(T * TOP_K, dtype=jnp.int32) - starts[se]
    n_blk = -(-(T * TOP_K + N_EXPERTS * ROUTE_BLOCK) // ROUTE_BLOCK)
    P = n_blk * ROUTE_BLOCK
    slot_tok = jnp.zeros((P,), jnp.int32).at[dest].set(tok[order])
    slot_w = jnp.zeros((P,), jnp.float32).at[dest].set(gate[order])
    blk_start = jnp.arange(n_blk, dtype=pend.dtype) * ROUTE_BLOCK
    blk_e = jnp.minimum(jnp.searchsorted(pend, blk_start, side="right"), N_EXPERTS - 1)
    xs = hf[slot_tok].reshape(n_blk, ROUTE_BLOCK, D)

    def expert_block(args):
        xb, e = args
        a = xb @ w_gate[e]
        b = xb @ w_up[e]
        return (jax.nn.silu(a) * b) @ w_down[e]

    ys = lax.map(expert_block, (xs, blk_e)).reshape(P, D)
    out = jnp.zeros((T, D), h.dtype).at[slot_tok].add(ys * slot_w[:, None].astype(ys.dtype))
    return out.reshape(B, S, D)

def setup_inputs(seed: int = 0) -> dict:
    key = jax.random.key(seed)
    ks = jax.random.split(key, 24)
    L, D = DEPTH, D_MODEL
    nrm = jax.random.normal
    f32 = jnp.float32

    def gain(k, shape):
        return jnp.ones(shape, f32) + 0.01 * nrm(k, shape, f32)

    return {
        "x": nrm(ks[0], (BATCH, SEQ, D), f32),
        "mem": nrm(ks[1], (BATCH, MEM_LEN, D), f32),
        "norm_mix_g": gain(ks[2], (L, D)),
        "w_in": nrm(ks[3], (L, D, IN_COLS), f32) * D ** -0.5,
        "conv_w": nrm(ks[4], (L, CONV_K, CONV_CH), f32) * CONV_K ** -0.5,
        "conv_b": 0.01 * nrm(ks[5], (L, CONV_CH), f32),
        "head_norm_g": gain(ks[6], (L, MIX_HEADS, HEAD_DIM)),
        "w_out": nrm(ks[7], (L, MIX_WIDTH, D), f32) * MIX_WIDTH ** -0.5,
        "norm_xa_g": gain(ks[8], (L, D)),
        "norm_mem_g": gain(ks[9], (L, D)),
        "w_q": nrm(ks[10], (L, D, D), f32) * D ** -0.5,
        "w_kv": nrm(ks[11], (L, D, 2 * D), f32) * D ** -0.5,
        "w_o": nrm(ks[12], (L, D, D), f32) * D ** -0.5,
        "norm_ffn_g": gain(ks[13], (L, D)),
        "w_route_group": nrm(ks[14], (L, D, N_GROUPS), f32) * D ** -0.5,
        "b_route_group": 0.01 * nrm(ks[15], (L, N_GROUPS), f32),
        "w_route_expert": nrm(ks[16], (L, D, N_EXPERTS), f32) * D ** -0.5,
        "b_route_expert": 0.01 * nrm(ks[17], (L, N_EXPERTS), f32),
        "w_gate": nrm(ks[18], (L, N_EXPERTS, D, D_EXPERT), f32) * D ** -0.5,
        "w_up": nrm(ks[19], (L, N_EXPERTS, D, D_EXPERT), f32) * D ** -0.5,
        "w_down": nrm(ks[20], (L, N_EXPERTS, D_EXPERT, D), f32) * D_EXPERT ** -0.5,
        "final_norm_g": gain(ks[21], (D,)),
    }

def reference(x, mem, norm_mix_g, w_in, conv_w, conv_b, head_norm_g, w_out,
              norm_xa_g, norm_mem_g, w_q, w_kv, w_o,
              norm_ffn_g, w_route_group, b_route_group, w_route_expert, b_route_expert,
              w_gate, w_up, w_down, final_norm_g):
    for l in range(DEPTH):
        x = x + parallel_mixer(rmsnorm(x, norm_mix_g[l]), w_in[l], conv_w[l], conv_b[l],
                               head_norm_g[l], w_out[l])
        x = x + memory_cross_attention(rmsnorm(x, norm_xa_g[l]), rmsnorm(mem, norm_mem_g[l]),
                                       w_q[l], w_kv[l], w_o[l])
        x = x + hierarchical_moe(rmsnorm(x, norm_ffn_g[l]), w_route_group[l], b_route_group[l],
                                 w_route_expert[l], b_route_expert[l],
                                 w_gate[l], w_up[l], w_down[l])
    return rmsnorm(x, final_norm_g)


_drawn_inputs = setup_inputs


def setup_inputs(seed=0):
    import zlib

    import numpy as np

    out = dict(_drawn_inputs(seed))
    spreads = {}
    factors = {'norm_mix_g': 3.113,
     'conv_b': 4.075,
     'head_norm_g': 3.75,
     'norm_xa_g': 8.0,
     'norm_mem_g': 8.0,
     'norm_ffn_g': 3.655,
     'b_route_group': 26.094,
     'b_route_expert': 5.471,
     'final_norm_g': 30.19}
    for name, (base, spread) in spreads.items():
        noise = np.random.default_rng([zlib.crc32(name.encode()), seed]).standard_normal(out[name].shape)
        drawn = base * np.exp(spread * noise) if base else spread * noise
        out[name] = __import__('jax').numpy.asarray(drawn.astype(out[name].dtype))
    for name, factor in factors.items():
        out[name] = (out[name] * factor).astype(out[name].dtype)
    return out
```

```python
from contextlib import ExitStack

import numpy as np

import concourse.bass as bass
from concourse import mybir

F32 = mybir.dt.float32
F32R = mybir.dt.float32r
BF16 = mybir.dt.bfloat16
I32 = mybir.dt.int32
U32 = mybir.dt.uint32
ALU = mybir.AluOpType
ACT = mybir.ActivationFunctionType
AX_X = mybir.AxisListType.X

P = 128
D = 1024
S = 2048
KT = D // P
NT = S // P
HD = 64
CONV = 512
CT = CONV // P
FFT = 512
FG = FFT // HD
NA = HD // 2 + 1
NB = HD // 2 - 1
WA, WB = FG * NA, FG * NB
R16 = S // P
MEM = 256
XH = 4
XD = D // XH
NG, EG = 4, 8
NE = NG * EG
DE = D // 2
EPS = 1e-6
NBLK = 64
NCOL = NBLK + S // P
BIG = 1e30
BANK = 512


class Steps:

    def __init__(self, eng, sem, base=0):
        self.eng, self.sem, self.base, self.n = eng, sem, base, 0

    def done(self, ins):
        ins.then_inc(self.sem, 1)
        self.n += 1
        self.eng.wait_ge(self.sem, self.base + self.n)


def mm3(pe, out, a_hi, a_lo, b_hi, b_lo, first, last):
    pe.matmul(out, lhsT=a_lo, rhs=b_hi, start=first, stop=False, skip_group_check=True)
    pe.matmul(out, lhsT=a_hi, rhs=b_lo, start=False, stop=False, skip_group_check=True)
    return pe.matmul(out, lhsT=a_hi, rhs=b_hi, start=False, stop=last, skip_group_check=True)


def tiles2(eng, n, body):
    body(0, 0)
    body(1, 1)
    with eng.Fori(1, n // 2) as i:
        for u in range(2):
            body(i * 2 + u, u)


def words(ap):
    return ap.bitcast(F32)


def landed(t, u):
    return (t - u) * 8 + 16


def is_first(t, n=1):
    return isinstance(t, int) and t < n


def fourier_front(nc, io, scratch):
    ctx = ExitStack()
    with ctx:
        sb = lambda name, shape, dt=F32: ctx.enter_context(nc.sbuf_tensor("ff_" + name, shape, dt))
        ps = lambda name, shape, dt=F32: ctx.enter_context(nc.psum_tensor("ff_" + name, shape, dt))
        sem = lambda name: nc.alloc_semaphore(name="ff_" + name)

        ident = sb("ident", [P, P])
        wraw = sb("wraw", [P, FFT // P, D])
        wt_hi = sb("wt_hi", [P, FFT // P, D], F32R)
        wt_lo = sb("wt_lo", [P, FFT // P, D], F32R)
        dft_hi = sb("dft_hi", [P, P], F32R)
        dft_lo = sb("dft_lo", [P, P], F32R)
        gain = sb("gain", [P, KT])
        wf_hi = sb("wf_hi", [P, KT, FFT], F32R)
        wf_lo = sb("wf_lo", [P, KT, FFT], F32R)
        xs = sb("xs", [P, 2, D])
        junk = sb("junk", [P, D])
        ss = sb("ss", [P, 2])
        ms = sb("ms", [P, 2])
        rstd = sb("rstd", [P, 2])
        eps = sb("eps", [P, 1])
        xT_hi = sb("xT_hi", [P, 2, KT, P], F32R)
        xT_lo = sb("xT_lo", [P, 2, KT, P], F32R)
        u_hi = sb("u_hi", [P, 2, FFT], F32R)
        u_lo = sb("u_lo", [P, 2, FFT], F32R)
        tw = sb("tw", [P, 2, 2, 2 * P], F32R)
        z = sb("z", [P, 2, 2, 2, FFT], F32R)

        pT = ps("pT", [P, 2, BANK])
        pU = ps("pU", [P, 2, BANK])
        pZ = ps("pZ", [P, 2, BANK])

        s_c = sem("const")
        s_w = sem("w")
        s_dft = sem("dft")
        s_wsh = sem("w_split_hi")
        s_wsl = sem("w_split_lo")
        s_fold = sem("folded")
        s_wfh = sem("folded_hi")
        s_wfl = sem("folded_lo")
        s_x = [sem("x0"), sem("x1")]
        s_tw = [sem("tw0"), sem("tw1")]
        s_sq = sem("squares")
        s_rs = sem("rstd")
        s_T = sem("transposed")
        s_xh = sem("xT_hi")
        s_xl = sem("xT_lo")
        s_u = sem("u")
        s_uh = sem("u_hi")
        s_ul = sem("u_lo")
        s_z = sem("z")
        s_zh = sem("z_hi")
        s_zl = sem("z_lo")
        s_o = [sem("zout0"), sem("zout1")]
        s_sd = sem("deviation")
        s_eps = sem("eps")

        x16 = io["x"].rearrange("(a b) d -> b a d", b=R16)
        zrows = scratch["z"].rearrange("(k s) c h f -> s k c h f", s=R16)
        block = ctx.enter_context(nc.Block())

        @block.sync
        def _(sp):
            sp.dma_start(ident[:], io["ident"]).then_inc(s_c, 16)
            sp.dma_start(gain[:], io["norm_mix_g"]).then_inc(s_c, 16)
            sp.dma_start(wraw[:], io["w_f_T"].rearrange("(c p) d -> p c d", p=P)).then_inc(s_w, 16)

            def tile(t, u):
                if not is_first(t, 2):
                    sp.wait_ge(s_xl, 2 * t - 2)
                sp.dma_start(xs[:, u], x16[bass.ds(t, 1)].rearrange("o a d -> (o a) d")).then_inc(s_x[u], 16)

            tiles2(sp, NT, tile)

        @block.gpsimd
        def _(pool):
            pool.dma_start(dft_hi[:], io["dft64"][0]).then_inc(s_dft, 16)
            pool.dma_start(dft_lo[:], io["dft64"][1]).then_inc(s_dft, 16)

            def tile(t, u):
                if not is_first(t, 2):
                    pool.wait_ge(s_z, 2 * t - 2)
                pool.dma_start(tw[:, u], io["tw128"][bass.ds(t, 1)].rearrange("o h p k -> p (o h) k")
                               ).then_inc(s_tw[u], 16)

            tiles2(pool, NT, tile)

        @block.scalar
        def _(act):
            act.wait_ge(s_eps, 1)
            act.wait_ge(s_w, 16)
            act.wait_ge(s_c, 32)
            for c in range(FFT // P):
                act.activation(wt_hi[:, c], wraw[:, c], ACT.Copy).then_inc(s_wsh, 1)
            for m in range(KT):
                act.wait_ge(s_fold, m + 1)
                src = pU[:, m % 2].rearrange("p (g c) -> p g c", c=HD)
                act.activation(wf_hi[:, m, 0:WA].rearrange("p (g c) -> p g c", c=NA), src[:, :, 0:NA],
                               ACT.Identity, scale=gain[:, m:m + 1])
                act.activation(wf_hi[:, m, WA:].rearrange("p (g c) -> p g c", c=NB), src[:, :, NA:],
                               ACT.Identity, scale=gain[:, m:m + 1]).then_inc(s_wfh, 1)

            def front(t, u):
                act.wait_ge(s_x[u], landed(t, u))
                if not is_first(t, 1):
                    act.wait_ge(s_rs, t)
                act.activation(junk[:], xs[:, u], ACT.Square, accum_out=ss[:, u:u + 1]).then_inc(s_sq, 1)
                act.wait_ge(s_sq, t + 1)
                act.activation(ms[:, u:u + 1], ss[:, u:u + 1], ACT.Sqrt, scale=1.0 / D, bias=eps[:]).then_inc(s_sd, 1)
                for h in range(2):
                    act.wait_ge(s_T, 2 * t + h + 1)
                    if not is_first(t, 2) and h == 0:
                        act.wait_ge(s_u, t - 1)
                    act.activation(xT_hi[:, u, 4 * h:4 * h + 4].rearrange("p k n -> p (k n)"), pT[:, h],
                                   ACT.Copy).then_inc(s_xh, 1)

            def back(t, u):
                act.wait_ge(s_u, t + 1)
                act.wait_ge(s_rs, t + 1)
                if not is_first(t, 2):
                    act.wait_ge(s_z, 2 * t - 2)
                act.activation(u_hi[:, u], pU[:, u], ACT.Identity, scale=rstd[:, u:u + 1]).then_inc(s_uh, 1)
                for c in range(2):
                    act.wait_ge(s_z, 2 * t + c + 1)
                    if not is_first(t, 2) and c == 0:
                        act.wait_ge(s_o[u], landed(t, u) - 16)
                    act.activation(z[:, u, c, 0], pZ[:, c], ACT.Copy).then_inc(s_zh, 1)
                act.wait_ge(s_zh, 2 * t + 2)
                act.wait_ge(s_zl, 2 * t + 2)
                act.dma_start(zrows[bass.ds(t, 1)].rearrange("o k c h f -> (o k) (c h f)"),
                              words(z[:, u].rearrange("p c h f -> p (c h f)"))).then_inc(s_o[u], 16)

            front(0, 0)
            front(1, 1)
            back(0, 0)
            with act.Fori(1, NT // 2) as i:
                front(2 * i, 0)
                back(2 * i - 1, 1)
                front(2 * i + 1, 1)
                back(2 * i, 0)
            back(NT - 1, 1)
            for u in range(2):
                act.wait_ge(s_o[u], 16 * NT // 2)

        @block.vector
        def _(dve):
            dve.memset(eps[:], EPS).then_inc(s_eps, 1)
            dve.wait_ge(s_c, 32)
            for c in range(FFT // P):
                dve.wait_ge(s_wsh, c + 1)
                dve.tensor_tensor(wt_lo[:, c], wraw[:, c], wt_hi[:, c], ALU.subtract).then_inc(s_wsl, 1)
            for m in range(KT):
                dve.wait_ge(s_wfh, m + 1)
                src = pU[:, m % 2].rearrange("p (g c) -> p g c", c=HD)
                for lo, w, at in ((0, WA, 0), (WA, WB, NA)):
                    c = NA if at == 0 else NB
                    hi = wf_hi[:, m, lo:lo + w].rearrange("p (g c) -> p g c", c=c)
                    dst = wf_lo[:, m, lo:lo + w].rearrange("p (g c) -> p g c", c=c)
                    last = dve.scalar_tensor_tensor(dst, src[:, :, at:at + c], gain[:, m:m + 1], hi,
                                                    ALU.mult, ALU.subtract)
                last.then_inc(s_wfl, 1)

            def front(t, u):
                dve.wait_ge(s_sd, t + 1)
                if not is_first(t, 2):
                    dve.wait_ge(s_uh, t - 1)
                    dve.wait_ge(s_ul, t - 1)
                dve.reciprocal(rstd[:, u:u + 1], ms[:, u:u + 1]).then_inc(s_rs, 1)
                for h in range(2):
                    dve.wait_ge(s_xh, 2 * t + h + 1)
                    dve.tensor_tensor(xT_lo[:, u, 4 * h:4 * h + 4].rearrange("p k n -> p (k n)"), pT[:, h],
                                      xT_hi[:, u, 4 * h:4 * h + 4].rearrange("p k n -> p (k n)"),
                                      ALU.subtract).then_inc(s_xl, 1)

            def back(t, u):
                dve.wait_ge(s_uh, t + 1)
                dve.wait_ge(s_rs, t + 1)
                dve.scalar_tensor_tensor(u_lo[:, u], pU[:, u], rstd[:, u:u + 1], u_hi[:, u],
                                         ALU.mult, ALU.subtract).then_inc(s_ul, 1)
                for c in range(2):
                    dve.wait_ge(s_zh, 2 * t + c + 1)
                    dve.tensor_tensor(z[:, u, c, 1], pZ[:, c], z[:, u, c, 0], ALU.subtract).then_inc(s_zl, 1)

            front(0, 0)
            front(1, 1)
            back(0, 0)
            with dve.Fori(1, NT // 2) as i:
                front(2 * i, 0)
                back(2 * i - 1, 1)
                front(2 * i + 1, 1)
                back(2 * i, 0)
            back(NT - 1, 1)

        @block.tensor
        def _(pe):
            pe.wait_ge(s_c, 32)
            pe.wait_ge(s_dft, 32)
            pe.wait_ge(s_wsl, FFT // P)
            for m in range(KT):
                if m >= 2:
                    pe.wait_ge(s_wfl, m - 1)
                for c in range(FFT // P):
                    last = mm3(pe, pU[:, m % 2, c * P:(c + 1) * P], wt_hi[:, c, m * P:(m + 1) * P],
                               wt_lo[:, c, m * P:(m + 1) * P], dft_hi[:], dft_lo[:], True, True)
                last.then_inc(s_fold, 1)
            pe.wait_ge(s_wfl, KT)

            def transposes(t, u):
                pe.wait_ge(s_x[u], landed(t, u))
                for h in range(2):
                    if not is_first(t, 1):
                        pe.wait_ge(s_xl, 2 * t + h - 1)
                    for k in range(4):
                        last = pe.transpose(pT[:, h, k * P:(k + 1) * P], xs[:, u, (4 * h + k) * P:(4 * h + k + 1) * P],
                                            ident[:])
                    last.then_inc(s_T, 1)

            def project(t, u):
                pe.wait_ge(s_xl, 2 * t + 2)
                if not is_first(t, 2):
                    pe.wait_ge(s_ul, t - 1)
                for k in range(KT):
                    last = mm3(pe, pU[:, u], xT_hi[:, u, k], xT_lo[:, u, k], wf_hi[:, k], wf_lo[:, k],
                               k == 0, k == KT - 1)
                last.then_inc(s_u, 1)

            def stage(t, u):
                pe.wait_ge(s_ul, t + 1)
                pe.wait_ge(s_tw[u], landed(t, u))
                for c in range(2):
                    if not is_first(t, 1):
                        pe.wait_ge(s_zl, 2 * t + c - 1)
                    last = mm3(pe, pZ[:, c], tw[:, u, 0, c * P:(c + 1) * P], tw[:, u, 1, c * P:(c + 1) * P],
                               u_hi[:, u], u_lo[:, u], True, True)
                    last.then_inc(s_z, 1)

            transposes(0, 0)
            project(0, 0)
            transposes(1, 1)
            project(1, 1)
            stage(0, 0)
            with pe.Fori(1, NT // 2) as i:
                transposes(2 * i, 0)
                project(2 * i, 0)
                stage(2 * i - 1, 1)
                transposes(2 * i + 1, 1)
                project(2 * i + 1, 1)
                stage(2 * i, 0)
            stage(NT - 1, 1)


def fourier_back(nc, io, scratch):
    ctx = ExitStack()
    with ctx:
        sb = lambda name, shape, dt=F32: ctx.enter_context(nc.sbuf_tensor("fb_" + name, shape, dt))
        ps = lambda name, shape, dt=F32: ctx.enter_context(nc.psum_tensor("fb_" + name, shape, dt))
        sem = lambda name: nc.alloc_semaphore(name="fb_" + name)
        ident = sb("ident", [P, P])
        dft = sb("dft", [P, 3, 2, P], F32R)
        z = sb("z", [P, 2, 2, 2, FFT], F32R)
        yb = sb("yb", [P, 2, WB])
        y = sb("y", [P, 2, FG, HD])
        sq = sb("sq", [P, FG, HD])
        ss = sb("ss", [P, 2, FG])
        ms = sb("ms", [P, 2, FG])
        eps = sb("eps", [P, 1])
        rs = sb("rs", [P, FG])
        yn = sb("yn", [P, 2, FG, HD])
        yT = sb("yT", [P, 2, CT, S], F32R)
        pY = ps("pY", [P, 2, BANK])
        pT = ps("pT", [P, 2, BANK])
        s_c = sem("const")
        s_d = sem("dft")
        s_zi = [sem("z0"), sem("z1")]
        s_Y = sem("Y")
        s_yb = sem("yb")
        s_ys = sem("y_sum")
        s_yn = sem("yn")
        s_T = sem("T")
        s_th = sem("T_hi")
        s_tl = sem("T_lo")
        s_st = sem("steps")
        s_o = sem("out")
        s_ss = sem("squares")
        s_sd = sem("deviation")
        s_eps = sem("eps")
        zt = scratch["z"].rearrange("(b q) c h f -> b q (c h f)", q=P)
        block = ctx.enter_context(nc.Block())

        @block.sync
        def _(sp):
            sp.dma_start(ident[:], io["ident"]).then_inc(s_c, 16)

            def tile(t, u):
                if not is_first(t, 2):
                    sp.wait_ge(s_Y, t - 1)
                sp.dma_start(words(z[:, u].rearrange("p c h f -> p (c h f)")),
                             zt[bass.ds(t, 1)].rearrange("o q n -> (o q) n")).then_inc(s_zi[u], 16)

            tiles2(sp, NT, tile)
            sp.wait_ge(s_th, NT)
            sp.wait_ge(s_tl, NT)
            for h in range(2):
                sp.dma_start(scratch["yT"][:, CT:, h, 1:S + 1], words(yT[:, h])).then_inc(s_o, 16)
            sp.wait_ge(s_o, 32)

        @block.gpsimd
        def _(pool):
            pool.dma_start(dft[:], io["dft16"].rearrange("c h p k -> p c h k")).then_inc(s_d, 16)

        @block.scalar
        def _(act):
            act.wait_ge(s_c, 16)
            act.wait_ge(s_eps, 1)

            def tile(t, u):
                act.wait_ge(s_Y, t + 1)
                if not is_first(t, 2):
                    act.wait_ge(s_yn, t - 1)
                act.activation(yb[:, u], pY[:, u, WA:], ACT.Copy)
                act.activation(y[:, u, :, 0:NA:NA - 1],
                               pY[:, u, 0:WA].rearrange("p (g c) -> p g c", c=NA)[:, :, 0:NA:NA - 1],
                               ACT.Copy).then_inc(s_yb, 1)
                act.wait_ge(s_ss, t + 1)
                act.activation(ms[:, u], ss[:, u], ACT.Sqrt, scale=1.0 / HD, bias=eps[:]).then_inc(s_sd, 1)

            def turned(t, u):
                act.wait_ge(s_T, t + 1)
                act.activation(yT[:, 0].rearrange("p j (k b a) -> p j k b a", b=NT, a=8)[:, :, :, bass.ds(t, 1), :]
                               .rearrange("p j k o a -> p j k (o a)"),
                               pT[:, u].rearrange("p (j a k) -> p j k a", j=CT, a=8), ACT.Copy).then_inc(s_th, 1)

            tile(0, 0)
            tile(1, 1)
            turned(0, 0)
            with act.Fori(1, NT // 2) as i:
                tile(2 * i, 0)
                turned(2 * i - 1, 1)
                tile(2 * i + 1, 1)
                turned(2 * i, 0)
            turned(NT - 1, 1)

        @block.vector
        def _(dve):
            dve.memset(eps[:], EPS).then_inc(s_eps, 1)
            def tile(t, u):
                st = Steps(dve, s_st, t * 3)
                ya = pY[:, u, 0:WA].rearrange("p (g c) -> p g c", c=NA)[:, :, 1:NA - 1]
                ybv = yb[:, u].rearrange("p (g c) -> p g c", c=NB)
                dve.wait_ge(s_yb, t + 1)
                dve.tensor_tensor(y[:, u, :, 1:NA - 1], ya, ybv, ALU.subtract)
                st.done(dve.tensor_tensor(y[:, u, :, NA:], ya, ybv, ALU.add))
                st.done(dve.tensor_tensor(sq[:], y[:, u], y[:, u], ALU.mult))
                dve.tensor_reduce(ss[:, u], sq[:], AX_X, ALU.add).then_inc(s_ss, 1)
                dve.wait_ge(s_sd, t + 1)
                st.done(dve.reciprocal(rs[:], ms[:, u]))
                if not is_first(t, 2):
                    dve.wait_ge(s_T, t - 1)
                dve.tensor_tensor(yn[:, u], y[:, u], rs[:].unsqueeze(2).to_broadcast([P, FG, HD]), ALU.mult
                                  ).then_inc(s_yn, 1)

            def turned(t, u):
                dve.wait_ge(s_th, t + 1)
                view = lambda h: yT[:, h].rearrange("p j (k b a) -> p j k b a", b=NT, a=8)[:, :, :, bass.ds(t, 1), :] \
                    .rearrange("p j k o a -> p j k (o a)")
                dve.tensor_tensor(view(1), pT[:, u].rearrange("p (j a k) -> p j k a", j=CT, a=8), view(0),
                                  ALU.subtract).then_inc(s_tl, 1)

            tile(0, 0)
            tile(1, 1)
            turned(0, 0)
            with dve.Fori(1, NT // 2) as i:
                tile(2 * i, 0)
                turned(2 * i - 1, 1)
                tile(2 * i + 1, 1)
                turned(2 * i, 0)
            turned(NT - 1, 1)

        @block.tensor
        def _(pe):
            pe.wait_ge(s_c, 16)
            pe.wait_ge(s_d, 16)

            def tile(t, u):
                pe.wait_ge(s_zi[u], landed(t, u))
                if not is_first(t, 2):
                    pe.wait_ge(s_yn, t - 1)
                zc = lambda c, h, a, b: z[:, u, c, h, a:b]
                for (lo, hi, terms) in ((0, WA, ((0, 0), (2, 1))), (WA, FFT, ((0, 1), (1, 0)))):
                    for n, (m, c) in enumerate(terms):
                        last = mm3(pe, pY[:, u, lo:hi], dft[:, m, 0], dft[:, m, 1], zc(c, 0, lo, hi), zc(c, 1, lo, hi),
                                   n == 0, n == 1)
                last.then_inc(s_Y, 1)

            def turned(t, u):
                pe.wait_ge(s_yn, t + 1)
                if not is_first(t, 2):
                    pe.wait_ge(s_tl, t - 1)
                for j in range(CT):
                    last = pe.transpose(pT[:, u, j * P:(j + 1) * P],
                                        yn[:, u].rearrange("p g c -> p (g c)")[:, j * P:(j + 1) * P], ident[:])
                last.then_inc(s_T, 1)

            tile(0, 0)
            tile(1, 1)
            turned(0, 0)
            with pe.Fori(1, NT // 2) as i:
                tile(2 * i, 0)
                turned(2 * i - 1, 1)
                tile(2 * i + 1, 1)
                turned(2 * i, 0)
            turned(NT - 1, 1)


def conv_half(nc, io, scratch):
    CH = BANK
    NCH = S // CH
    QT = CH // P
    ctx = ExitStack()
    with ctx:
        sb = lambda name, shape, dt=F32: ctx.enter_context(nc.sbuf_tensor("cv_" + name, shape, dt))
        ps = lambda name, shape, dt=F32: ctx.enter_context(nc.psum_tensor("cv_" + name, shape, dt))
        sem = lambda name: nc.alloc_semaphore(name="cv_" + name)
        ident = sb("ident", [P, P])
        ones = sb("ones", [P, P])
        gain = sb("gain", [P, KT])
        taps = sb("taps", [P, 3, CT])
        cbias = sb("cbias", [P, CT])
        eps = sb("eps", [P, 1])
        with nc.sbuf_tensor("cv_wraw", [P, 2, 3 * CONV], F32) as wraw:
            pass
        hN_hi = sb("hN_hi", [P, KT, CH], F32R)
        w_hi = sb("w_hi", [P, KT, 3 * CONV], F32R)
        w_lo = sb("w_lo", [P, KT, 3 * CONV], F32R)
        xs = sb("xs", [P, 2, D])
        junk = sb("junk", [P, D], BF16)
        ss = sb("ss", [P, 2])
        sd1 = sb("sd1", [P, 2])
        rstd = sb("rstd", [P, 2])
        hT_hi = sb("hT_hi", [P, KT, CH], F32R)
        hT_lo = sb("hT_lo", [P, KT, CH], F32R)
        hN_lo = sb("hN_lo", [P, KT, CH], F32R)
        pb = sb("pb", [P, CT, CH + 2])
        bb = sb("bb", [P, CT, CH + 1])
        cs = sb("cs", [P, CH])
        zc = sb("zc", [P, CH])
        yc = sb("yc", [P, 2, CH])
        sq = sb("sq", [P, CH])
        sd = sb("sd", [P, CH])
        yo = sb("yo", [P, 2, CH], F32R)
        pT = ps("pT", [P, 2, BANK])
        pC = ps("pC", [P, BANK])
        pV = ps("pV", [P, BANK])
        pB = ps("pB", [P, BANK])
        pM = ps("pM", [P, BANK])
        s_c, s_cst = sem("const"), sem("memsets")
        s_w = [sem("w0"), sem("w1")]
        s_wh, s_wl = sem("w_hi"), sem("w_lo")
        s_x = [sem("x0"), sem("x1")]
        s_sq1, s_sd1, s_rs, s_xn = sem("sq1"), sem("sd1"), sem("rstd"), sem("xn")
        s_T, s_Th, s_Tl = sem("T"), sem("T_hi"), sem("T_lo")
        s_C, s_V, s_B = sem("c"), sem("v"), sem("b")
        s_cs, s_bb, s_p, s_car = sem("c_copied"), sem("b_copied"), sem("p"), sem("carried")
        s_sq, s_M, s_sd, s_rd, s_yn, s_yh, s_yl = (sem(n) for n in
                                                   ("squares", "mean", "dev", "rdev", "yn", "y_hi", "y_lo"))
        s_st, s_st2 = sem("steps_conv"), sem("steps_end")
        s_o, s_e = sem("out"), sem("out_end")
        xt = io["x"].rearrange("(t p) d -> t p d", p=P)
        block = ctx.enter_context(nc.Block())

        H = [(hT_hi, hT_lo), (hN_hi, hN_lo)]

        @block.sync
        def _(sp):
            sp.dma_start(ident[:], io["ident"]).then_inc(s_c, 16)
            sp.dma_start(ones[:], io["head_mean"]).then_inc(s_c, 16)
            sp.dma_start(gain[:], io["norm_mix_g"]).then_inc(s_c, 16)
            sp.dma_start(taps[:], io["conv_w"]).then_inc(s_c, 16)
            sp.dma_start(cbias[:], io["conv_b"]).then_inc(s_c, 16)
            for t in range(2):
                sp.dma_start(xs[:, t], xt[t]).then_inc(s_x[t], 16)
            for k in range(KT):
                if k >= 2:
                    sp.wait_ge(s_wl, k - 1)
                sp.dma_start(wraw[:, k % 2], io["w_conv"][k * P:(k + 1) * P, :]).then_inc(s_w[k % 2], 16)
                if k in (1, 2):
                    sp.wait_ge(s_T, 2 * k)
                    sp.dma_start(xs[:, k - 1], xt[k + 1]).then_inc(s_x[k - 1], 16)
            with sp.Fori(2, NT // 2) as i:
                for u in range(2):
                    sp.wait_ge(s_T, 4 * i + 2 * u - 2)
                    sp.dma_start(xs[:, u], xt[bass.ds(2 * i + u, 1)].rearrange("o p d -> (o p) d")).then_inc(s_x[u], 16)

        @block.gpsimd
        def _(pool):
            for n in range(NCH):
                for j in range(CT):
                    idx = 4 * n + j
                    pool.wait_ge(s_yl, idx + 1)
                    pool.wait_ge(s_yh, idx + 1)
                    pool.dma_start(scratch["yT"][:, j, :, n * CH:(n + 1) * CH], words(yo[:])).then_inc(s_o, 16)
            pool.wait_ge(s_o, 16 * 4 * NCH)

        @block.scalar
        def _(act):
            act.wait_ge(s_c, 80)
            act.wait_ge(s_cst, 1)

            def statistics(t, u):
                act.wait_ge(s_x[u], landed(t, u))
                if t >= 2:
                    act.wait_ge(s_rs, t - 1)
                act.activation(junk[:], xs[:, u],
                               ACT.Square, accum_out=ss[:, u:u + 1]).then_inc(s_sq1, 1)
                act.wait_ge(s_sq1, t + 1)
                act.activation(sd1[:, u:u + 1], ss[:, u:u + 1], ACT.Sqrt, scale=1.0 / D, bias=eps[:]).then_inc(s_sd1, 1)

            def turned(t):
                n, q = t // QT, t % QT
                for h in range(2):
                    act.wait_ge(s_T, 2 * t + h + 1)
                    if n >= 2 and q == 0 and h == 0:
                        act.wait_ge(s_B, 4 * (n - 1))
                    act.activation(H[n % 2][0][:, 4 * h:4 * h + 4, q * P:(q + 1) * P],
                                   pT[:, h].rearrange("p (k n) -> p k n", k=4), ACT.Copy).then_inc(s_Th, 1)

            def weights(k):
                act.wait_ge(s_w[k % 2], 16 * (k // 2) + 16)
                act.activation(w_hi[:, k], wraw[:, k % 2], ACT.Identity, scale=gain[:, k:k + 1]).then_inc(s_wh, 1)

            def norm(idx):
                act.wait_ge(s_M, idx + 1)
                if idx >= 1:
                    act.wait_ge(s_rd, idx)
                act.activation(sd[:], pM[:], ACT.Sqrt, bias=eps[:]).then_inc(s_sd, 1)
                act.wait_ge(s_yn, idx + 1)
                if idx >= 1:
                    act.wait_ge(s_o, 16 * idx)
                act.activation(yo[:, 0], yc[:, idx % 2], ACT.Copy).then_inc(s_yh, 1)

            for k in range(KT):
                if k < QT:
                    statistics(k, k % 2)
                    turned(k)
                weights(k)
            for n in range(NCH):
                for j in range(CT):
                    idx = 4 * n + j
                    act.wait_ge(s_C, idx + 1)
                    if idx >= 1:
                        act.wait_ge(s_p, idx)
                    act.activation(cs[:], pC[:], ACT.Copy).then_inc(s_cs, 1)
                    if n + 1 < NCH:
                        statistics(4 * (n + 1) + j, j % 2)
                    act.wait_ge(s_B, idx + 1)
                    if n >= 1:
                        act.wait_ge(s_car, idx - 3)
                    act.activation(bb[:, j, 1:CH + 1], pB[:], ACT.Copy).then_inc(s_bb, 1)
                    if idx >= 1:
                        norm(idx - 1)
                    if n + 1 < NCH:
                        turned(4 * (n + 1) + j)
            norm(4 * NCH - 1)
            act.wait_ge(s_M, 4 * NCH + 1)
            act.wait_ge(s_rd, 4 * NCH)
            act.activation(sd[:, 0:CT], pM[:, 0:CT], ACT.Sqrt, bias=eps[:]).then_inc(s_sd, 1)
            act.wait_ge(s_yn, 4 * NCH + 1)
            act.wait_ge(s_o, 16 * 4 * NCH)
            act.activation(yo[:, 0, 0:CT], yc[:, 0, 0:CT], ACT.Copy).then_inc(s_yh, 1)
            act.wait_ge(s_yh, 4 * NCH + 1)
            act.wait_ge(s_yl, 4 * NCH + 1)
            for j in range(CT):
                act.dma_start(scratch["yT"][:, j, :, S:S + 1], words(yo[:, :, j:j + 1]),
                              allow_slow_non_contiguous=True).then_inc(s_e, 16)
            act.wait_ge(s_e, 16 * CT)

        @block.vector
        def _(dve):
            dve.memset(eps[:], EPS).then_inc(s_cst, 1)
            dve.memset(pb[:], 0.0)
            dve.memset(bb[:], 0.0).then_inc(s_cst, 1)
            dve.wait_ge(s_c, 80)
            st = Steps(dve, s_st)

            def statistics(t, u):
                dve.wait_ge(s_sd1, t + 1)
                dve.reciprocal(rstd[:, u:u + 1], sd1[:, u:u + 1]).then_inc(s_rs, 1)
                dve.wait_ge(s_rs, t + 1)
                dve.tensor_scalar(xs[:, u], xs[:, u], rstd[:, u:u + 1], None, ALU.mult).then_inc(s_xn, 1)

            def turned(t):
                n, q = t // QT, t % QT
                for h in range(2):
                    dve.wait_ge(s_Th, 2 * t + h + 1)
                    dve.tensor_tensor(H[n % 2][1][:, 4 * h:4 * h + 4, q * P:(q + 1) * P],
                                      pT[:, h].rearrange("p (k n) -> p k n", k=4),
                                      H[n % 2][0][:, 4 * h:4 * h + 4, q * P:(q + 1) * P],
                                      ALU.subtract).then_inc(s_Tl, 1)

            def weights(k):
                dve.wait_ge(s_wh, k + 1)
                dve.scalar_tensor_tensor(w_lo[:, k], wraw[:, k % 2], gain[:, k:k + 1], w_hi[:, k],
                                         ALU.mult, ALU.subtract).then_inc(s_wl, 1)

            def convolve(n, j):
                idx = 4 * n + j
                dve.wait_ge(s_V, idx + 1)
                dve.wait_ge(s_cs, idx + 1)
                if idx == 0:
                    dve.wait_ge(s_cst, 2)
                dve.tensor_tensor(pb[:, j, 2:CH + 2], cs[:], pV[:], ALU.mult).then_inc(s_p, 1)
                dve.wait_ge(s_p, idx + 1)
                st.done(dve.tensor_scalar(zc[:], pb[:, j, 0:CH], taps[:, 0, j:j + 1], cbias[:, j:j + 1], ALU.mult, ALU.add))
                st.done(dve.scalar_tensor_tensor(zc[:], pb[:, j, 1:CH + 1], taps[:, 1, j:j + 1], zc[:], ALU.mult, ALU.add))
                st.done(dve.scalar_tensor_tensor(zc[:], pb[:, j, 2:CH + 2], taps[:, 2, j:j + 1], zc[:], ALU.mult, ALU.add))
                dve.wait_ge(s_bb, idx + 1)
                if idx >= 2:
                    dve.wait_ge(s_yh, idx - 1)
                    dve.wait_ge(s_yl, idx - 1)
                st.done(dve.tensor_tensor(yc[:, idx % 2], zc[:], bb[:, j, 0:CH], ALU.mult))
                if idx >= 1:
                    dve.wait_ge(s_M, idx)
                dve.tensor_tensor(sq[:], yc[:, idx % 2], yc[:, idx % 2], ALU.mult).then_inc(s_sq, 1)
                st.done(dve.tensor_copy(pb[:, j, 0:2], pb[:, j, CH:CH + 2]))
                dve.tensor_copy(bb[:, j, 0:1], bb[:, j, CH:CH + 1]).then_inc(s_car, 1)

            def norm(idx):
                dve.wait_ge(s_sd, idx + 1)
                dve.reciprocal(sd[:], sd[:]).then_inc(s_st2, 1)
                dve.wait_ge(s_st2, idx + 1)
                ins = dve.tensor_tensor(yc[:, idx % 2], yc[:, idx % 2], sd[:], ALU.mult)
                ins.then_inc(s_yn, 1)
                dve.wait_ge(s_yn, idx + 1)
                dve.wait_ge(s_yh, idx + 1)
                dve.tensor_tensor(yo[:, 1], yc[:, idx % 2], yo[:, 0], ALU.subtract).then_inc(s_yl, 1)
                dve.sem_inc(s_rd, 1)

            for k in range(KT):
                if k < QT:
                    statistics(k, k % 2)
                    turned(k)
                weights(k)
            for n in range(NCH):
                for j in range(CT):
                    idx = 4 * n + j
                    if n + 1 < NCH:
                        statistics(4 * (n + 1) + j, j % 2)
                    convolve(n, j)
                    if idx >= 1:
                        norm(idx - 1)
                    if n + 1 < NCH:
                        turned(4 * (n + 1) + j)
            norm(4 * NCH - 1)
            w = slice(0, CT)
            dve.wait_ge(s_car, 4 * NCH)
            dve.wait_ge(s_yh, 4 * NCH)
            dve.wait_ge(s_yl, 4 * NCH)
            dve.tensor_tensor(zc[:, w], pb[:, :, 0], taps[:, 0, :], ALU.mult)
            st.done(dve.tensor_tensor(yc[:, 0, w], pb[:, :, 1], taps[:, 1, :], ALU.mult))
            st.done(dve.tensor_tensor(zc[:, w], zc[:, w], yc[:, 0, w], ALU.add))
            st.done(dve.tensor_tensor(zc[:, w], zc[:, w], cbias[:], ALU.add))
            st.done(dve.tensor_tensor(yc[:, 0, w], zc[:, w], bb[:, :, 0], ALU.mult))
            dve.wait_ge(s_M, 4 * NCH)
            dve.tensor_tensor(sq[:, w], yc[:, 0, w], yc[:, 0, w], ALU.mult).then_inc(s_sq, 1)
            dve.wait_ge(s_sd, 4 * NCH + 1)
            st.done(dve.reciprocal(sd[:, w], sd[:, w]))
            dve.tensor_tensor(yc[:, 0, w], yc[:, 0, w], sd[:, w], ALU.mult).then_inc(s_yn, 1)
            dve.wait_ge(s_yh, 4 * NCH + 1)
            dve.tensor_tensor(yo[:, 1, w], yc[:, 0, w], yo[:, 0, w], ALU.subtract).then_inc(s_yl, 1)

        @block.tensor
        def _(pe):
            pe.wait_ge(s_c, 80)

            def turned(t):
                pe.wait_ge(s_xn, t + 1)
                for h in range(2):
                    if t >= 1:
                        pe.wait_ge(s_Tl, 2 * t + h - 1)
                    for k in range(4):
                        last = pe.transpose(pT[:, h, k * P:(k + 1) * P],
                                            xs[:, t % 2, (4 * h + k) * P:(4 * h + k + 1) * P], ident[:])
                    last.then_inc(s_T, 1)

            def mean(idx, width=CH):
                pe.wait_ge(s_sq, idx + 1)
                if idx >= 1:
                    pe.wait_ge(s_sd, idx)
                pe.matmul(pM[:, 0:width], lhsT=ones[:], rhs=sq[:, 0:width], start=True, stop=True).then_inc(s_M, 1)

            for t in range(QT):
                turned(t)
            pe.wait_ge(s_wl, KT)
            for n in range(NCH):
                hh, hl = H[n % 2]
                pe.wait_ge(s_Tl, 8 * (n + 1))
                for j in range(CT):
                    idx = 4 * n + j
                    for g, bank, done in ((1, pC, s_C), (2, pV, s_V), (0, pB, s_B)):
                        if idx >= 1:
                            pe.wait_ge(*{0: (s_bb, idx), 1: (s_cs, idx), 2: (s_p, idx)}[g])
                        c0 = g * CONV + j * P
                        for k in range(KT):
                            last = mm3(pe, bank[:], w_hi[:, k, c0:c0 + P], w_lo[:, k, c0:c0 + P], hh[:, k], hl[:, k],
                                       k == 0, k == KT - 1)
                        last.then_inc(done, 1)
                        if g == 1 and idx >= 1:
                            mean(idx - 1)
                    if n + 1 < NCH:
                        turned(4 * (n + 1) + j)
            mean(4 * NCH - 1)
            mean(4 * NCH, CT)


def mixer_out(nc, io, scratch):
    ctx = ExitStack()
    with ctx:
        sb = lambda name, shape, dt=F32: ctx.enter_context(nc.sbuf_tensor("mo_" + name, shape, dt))
        ps = lambda name, shape, dt=F32: ctx.enter_context(nc.psum_tensor("mo_" + name, shape, dt))
        sem = lambda name: nc.alloc_semaphore(name="mo_" + name)
        gain = sb("gain", [P, KT])
        wraw = sb("wraw", [P, 2, D])
        w_hi = sb("w_hi", [P, KT, D], F32R)
        w_lo = sb("w_lo", [P, KT, D], F32R)
        yt = sb("yt", [P, 2, KT, 2, P], F32R)
        xs = sb("xs", [P, 2, D])
        x1 = sb("x1", [P, 2, D])
        pO = ps("pO", [P, 2, 2, BANK])
        s_c = sem("const")
        s_w = [sem("w0"), sem("w1")]
        s_wh, s_wl = sem("w_hi"), sem("w_lo")
        s_y = [sem("y0"), sem("y1")]
        s_x = [sem("x0"), sem("x1")]
        s_O, s_a = sem("product"), sem("added")
        s_o = [sem("o0"), sem("o1")]
        xt = io["x"].rearrange("(t p) d -> t p d", p=P)
        x1t = scratch["x1"].rearrange("(t p) d -> t p d", p=P)
        yTv = scratch["yT"].rearrange("p k h t -> p (k h) t")
        block = ctx.enter_context(nc.Block())

        @block.sync
        def _(sp):
            sp.dma_start(gain[:], io["head_norm_g"]).then_inc(s_c, 16)

            def tile(t, u):
                if not is_first(t, 2):
                    sp.wait_ge(s_O, t - 1)
                sp.dma_start(words(yt[:, u].rearrange("p k h t -> p (k h) t")),
                             yTv[:, :, bass.ds(t * P + 1, P)]).then_inc(s_y[u], 16)

            tiles2(sp, NT, tile)

        @block.scalar
        def _(act):
            for k in range(KT):
                if k >= 2:
                    act.wait_ge(s_wl, k - 1)
                act.dma_start(wraw[:, k % 2], io["w_out"][k * P:(k + 1) * P, :]).then_inc(s_w[k % 2], 16)
                act.wait_ge(s_w[k % 2], 16 * (k // 2) + 16)
                act.wait_ge(s_c, 16)
                act.activation(w_hi[:, k], wraw[:, k % 2], ACT.Identity, scale=gain[:, k:k + 1]).then_inc(s_wh, 1)

            def tile(t, u):
                act.wait_ge(s_a, t + 1)
                act.dma_start(x1t[bass.ds(t, 1)].rearrange("o p d -> (o p) d"), x1[:, u]).then_inc(s_o[u], 16)

            tiles2(act, NT, tile)
            for u in range(2):
                act.wait_ge(s_o[u], 16 * NT // 2)

        @block.gpsimd
        def _(pool):
            def tile(t, u):
                if not is_first(t, 2):
                    pool.wait_ge(s_a, t - 1)
                pool.dma_start(xs[:, u], xt[bass.ds(t, 1)].rearrange("o p d -> (o p) d")).then_inc(s_x[u], 16)

            tiles2(pool, NT, tile)

        @block.vector
        def _(dve):
            dve.wait_ge(s_c, 16)
            for k in range(KT):
                dve.wait_ge(s_wh, k + 1)
                dve.scalar_tensor_tensor(w_lo[:, k], wraw[:, k % 2], gain[:, k:k + 1], w_hi[:, k],
                                         ALU.mult, ALU.subtract).then_inc(s_wl, 1)

            def tile(t, u):
                dve.wait_ge(s_O, t + 1)
                dve.wait_ge(s_x[u], landed(t, u))
                if not is_first(t, 2):
                    dve.wait_ge(s_o[u], landed(t, u) - 16)
                dve.tensor_tensor(x1[:, u], pO[:, u].rearrange("p a b -> p (a b)"), xs[:, u], ALU.add).then_inc(s_a, 1)

            tiles2(dve, NT, tile)

        @block.tensor
        def _(pe):
            pe.wait_ge(s_wl, KT)

            def tile(t, u):
                pe.wait_ge(s_y[u], landed(t, u))
                if not is_first(t, 2):
                    pe.wait_ge(s_a, t - 1)
                for h in range(2):
                    for k in range(KT):
                        last = mm3(pe, pO[:, u, h], yt[:, u, k, 0], yt[:, u, k, 1], w_hi[:, k, h * BANK:(h + 1) * BANK],
                                   w_lo[:, k, h * BANK:(h + 1) * BANK], k == 0, k == KT - 1)
                last.then_inc(s_O, 1)

            tiles2(pe, NT, tile)


def attention_tables(nc, io, G, VW):
    ctx = ExitStack()
    with ctx:
        sb = lambda name, shape, dt=F32: ctx.enter_context(nc.sbuf_tensor("at_" + name, shape, dt))
        ps = lambda name, shape, dt=F32: ctx.enter_context(nc.psum_tensor("at_" + name, shape, dt))
        sem = lambda name: nc.alloc_semaphore(name="at_" + name)
        ident = sb("ident", [P, P])
        gain_m = sb("gain_m", [P, KT])
        gain_q = sb("gain_q", [P, KT])
        eps = sb("eps", [P, 1])
        junk = sb("junk", [P, D], BF16)
        ss, sd, rs = sb("ss", [P, 2]), sb("sd", [P, 2]), sb("rs", [P, 2])
        mT_hi = sb("mT_hi", [P, KT, MEM], F32R)
        mT_lo = sb("mT_lo", [P, KT, MEM], F32R)
        wraw = sb("wraw", [P, 2 * D])
        xs = wraw[:].rearrange("p (t d) -> p t d", t=2)
        w_hi = sb("w_hi", [P, 2 * D], F32R)
        w_lo = sb("w_lo", [P, 2 * D], F32R)
        kv_hi = sb("kv_hi", [P, 2 * KT, MEM], F32R)
        kv_lo = sb("kv_lo", [P, 2 * KT, MEM], F32R)
        pT = ps("pT", [P, 2, BANK])
        pA = ps("pA", [P, 2, BANK])
        pG = ps("pG", [P, 2, BANK])
        pW = ps("pW", [P, 2, BANK])
        s_c, s_eps, s_gq, s_x = sem("const"), sem("eps"), sem("gain_q"), [sem("x0"), sem("x1")]
        s_sq, s_sd, s_rs, s_xn = sem("sq"), sem("sd"), sem("rs"), sem("xn")
        s_T, s_Th, s_Tl = sem("T"), sem("T_hi"), sem("T_lo")
        s_w, s_wh, s_wl = sem("w"), sem("w_hi"), sem("w_lo")
        s_A, s_Ah, s_Al = sem("kv"), sem("kv_hi"), sem("kv_lo")
        s_G, s_Gh, s_Gl = sem("G"), sem("G_hi"), sem("G_lo")
        s_W, s_Wh, s_Wl = sem("VW"), sem("VW_hi"), sem("VW_lo")
        mt = io["mem"].rearrange("(t p) d -> t p d", p=P)
        LOTS = [("kv", i) for i in range(KT)] + [("q", h) for h in range(XH)] + [("o", h) for h in range(XH)]
        block = ctx.enter_context(nc.Block())

        @block.sync
        def _(sp):
            sp.dma_start(ident[:], io["ident"]).then_inc(s_c, 16)
            sp.dma_start(gain_m[:], io["norm_mem_g"]).then_inc(s_c, 16)
            sp.dma_start(gain_q[:], io["norm_xa_g"]).then_inc(s_c, 16)
            for t in range(2):
                sp.dma_start(xs[:, t], mt[t]).then_inc(s_x[t], 16)
            for n, (kind, i) in enumerate(LOTS):
                if n == 0:
                    sp.wait_ge(s_T, 4)
                else:
                    sp.wait_ge(s_wl, n)
                src = {"kv": io["w_kv"], "q": io["w_q"], "o": io["w_o"]}[kind][i]
                sp.dma_start(wraw[:], src).then_inc(s_w, 16)

        @block.scalar
        def _(act):
            act.wait_ge(s_eps, 1)
            act.wait_ge(s_c, 48)
            act.wait_ge(s_gq, 1)
            for t in range(2):
                act.wait_ge(s_x[t], 16)
                act.activation(junk[:], xs[:, t], ACT.Square, accum_out=ss[:, t:t + 1]).then_inc(s_sq, 1)
                act.wait_ge(s_sq, t + 1)
                act.activation(sd[:, t:t + 1], ss[:, t:t + 1], ACT.Sqrt, scale=1.0 / D, bias=eps[:]).then_inc(s_sd, 1)
                for h in range(2):
                    act.wait_ge(s_T, 2 * t + h + 1)
                    for k in range(4):
                        last = act.activation(mT_hi[:, 4 * h + k, t * P:(t + 1) * P], pT[:, h, k * P:(k + 1) * P],
                                              ACT.Identity, scale=gain_m[:, 4 * h + k:4 * h + k + 1])
                    last.then_inc(s_Th, 1)
            na = ng = nw = 0
            for n, (kind, i) in enumerate(LOTS):
                act.wait_ge(s_w, 16 * (n + 1))
                act.activation(w_hi[:], wraw[:], ACT.Copy).then_inc(s_wh, 1)
                if kind == "kv":
                    for m in range(2):
                        act.wait_ge(s_A, na + 1)
                        act.activation(kv_hi[:, na], pA[:, na % 2, 0:MEM], ACT.Copy).then_inc(s_Ah, 1)
                        na += 1
                elif kind == "q":
                    for m in range(KT):
                        act.wait_ge(s_G, ng + 1)
                        act.activation(G[0][:, m, i * MEM:(i + 1) * MEM], pG[:, ng % 2, 0:MEM], ACT.Identity,
                                       scale=gain_q[:, m:m + 1]).then_inc(s_Gh, 1)
                        ng += 1
                else:
                    for m in range(4):
                        act.wait_ge(s_W, nw + 1)
                        act.activation(VW[0][:, 2 * i + m // 2, (m % 2) * BANK:(m % 2 + 1) * BANK], pW[:, nw % 2],
                                       ACT.Copy).then_inc(s_Wh, 1)
                        nw += 1

        @block.vector
        def _(dve):
            dve.memset(eps[:], EPS).then_inc(s_eps, 1)
            dve.wait_ge(s_c, 48)
            dve.tensor_scalar(gain_q[:], gain_q[:], float(XD) ** -0.5, None, ALU.mult).then_inc(s_gq, 1)
            dve.wait_ge(s_gq, 1)
            for t in range(2):
                dve.wait_ge(s_sd, t + 1)
                dve.reciprocal(rs[:, t:t + 1], sd[:, t:t + 1]).then_inc(s_rs, 1)
                dve.wait_ge(s_rs, t + 1)
                dve.tensor_scalar(xs[:, t], xs[:, t], rs[:, t:t + 1], None, ALU.mult).then_inc(s_xn, 1)
                for h in range(2):
                    dve.wait_ge(s_Th, 2 * t + h + 1)
                    for k in range(4):
                        last = dve.scalar_tensor_tensor(mT_lo[:, 4 * h + k, t * P:(t + 1) * P], pT[:, h, k * P:(k + 1) * P],
                                                        gain_m[:, 4 * h + k:4 * h + k + 1],
                                                        mT_hi[:, 4 * h + k, t * P:(t + 1) * P], ALU.mult, ALU.subtract)
                    last.then_inc(s_Tl, 1)
            na = ng = nw = 0
            for n, (kind, i) in enumerate(LOTS):
                dve.wait_ge(s_wh, n + 1)
                dve.tensor_tensor(w_lo[:], wraw[:], w_hi[:], ALU.subtract).then_inc(s_wl, 1)
                if kind == "kv":
                    for m in range(2):
                        dve.wait_ge(s_Ah, na + 1)
                        dve.tensor_tensor(kv_lo[:, na], pA[:, na % 2, 0:MEM], kv_hi[:, na], ALU.subtract).then_inc(s_Al, 1)
                        na += 1
                elif kind == "q":
                    for m in range(KT):
                        dve.wait_ge(s_Gh, ng + 1)
                        cut = slice(i * MEM, (i + 1) * MEM)
                        dve.scalar_tensor_tensor(G[1][:, m, cut], pG[:, ng % 2, 0:MEM], gain_q[:, m:m + 1],
                                                 G[0][:, m, cut], ALU.mult, ALU.subtract).then_inc(s_Gl, 1)
                        ng += 1
                else:
                    for m in range(4):
                        dve.wait_ge(s_Wh, nw + 1)
                        cut = slice((m % 2) * BANK, (m % 2 + 1) * BANK)
                        dve.tensor_tensor(VW[1][:, 2 * i + m // 2, cut], pW[:, nw % 2], VW[0][:, 2 * i + m // 2, cut],
                                          ALU.subtract).then_inc(s_Wl, 1)
                        nw += 1

        @block.tensor
        def _(pe):
            pe.wait_ge(s_c, 48)
            for t in range(2):
                pe.wait_ge(s_xn, t + 1)
                for h in range(2):
                    if t:
                        pe.wait_ge(s_Tl, h + 1)
                    for k in range(4):
                        last = pe.transpose(pT[:, h, k * P:(k + 1) * P], xs[:, t, (4 * h + k) * P:(4 * h + k + 1) * P],
                                            ident[:])
                    last.then_inc(s_T, 1)
            pe.wait_ge(s_Tl, 4)
            na = ng = nw = 0
            for n, (kind, i) in enumerate(LOTS):
                pe.wait_ge(s_wl, n + 1)
                if kind == "kv":
                    wh, wl = (w[:].rearrange("p (m k c) -> p m k c", m=2, k=KT) for w in (w_hi, w_lo))
                    for m in range(2):
                        if na >= 2:
                            pe.wait_ge(s_Al, na - 1)
                        for k in range(KT):
                            last = mm3(pe, pA[:, na % 2, 0:MEM], wh[:, m, k], wl[:, m, k], mT_hi[:, k], mT_lo[:, k],
                                       k == 0, k == KT - 1)
                        last.then_inc(s_A, 1)
                        na += 1
                elif kind == "q":
                    wh, wl = (w[:].rearrange("p (k d) -> p k d", k=2) for w in (w_hi, w_lo))
                    pe.wait_ge(s_Al, 2 * KT)
                    for m in range(KT):
                        if ng >= 2:
                            pe.wait_ge(s_Gl, ng - 1)
                        for k in range(2):
                            last = mm3(pe, pG[:, ng % 2, 0:MEM], wh[:, k, m * P:(m + 1) * P], wl[:, k, m * P:(m + 1) * P],
                                       kv_hi[:, 2 * i + k], kv_lo[:, 2 * i + k], k == 0, k == 1)
                        last.then_inc(s_G, 1)
                        ng += 1
                else:
                    wh, wl = (w[:].rearrange("p (k d) -> p k d", k=2) for w in (w_hi, w_lo))
                    for m in range(4):
                        if nw >= 2:
                            pe.wait_ge(s_Wl, nw - 1)
                        mem, out = slice((m // 2) * P, (m // 2 + 1) * P), slice((m % 2) * BANK, (m % 2 + 1) * BANK)
                        for k in range(2):
                            last = mm3(pe, pW[:, nw % 2], kv_hi[:, KT + 2 * i + k, mem], kv_lo[:, KT + 2 * i + k, mem],
                                       wh[:, k, out], wl[:, k, out], k == 0, k == 1)
                        last.then_inc(s_W, 1)
                        nw += 1


def attention(nc, io, scratch, G, VW, logits):
    ctx = ExitStack()
    with ctx:
        sb = lambda name, shape, dt=F32: ctx.enter_context(nc.sbuf_tensor("xa_" + name, shape, dt))
        ps = lambda name, shape, dt=F32: ctx.enter_context(nc.psum_tensor("xa_" + name, shape, dt))
        sem = lambda name: nc.alloc_semaphore(name="xa_" + name)
        NR = NG + NE
        ident = sb("ident", [P, P])
        rraw = sb("rraw", [P, KT, NR])
        r_hi = sb("r_hi", [P, KT, NR], F32R)
        r_lo = sb("r_lo", [P, KT, NR], F32R)
        rbias = sb("rbias", [P, NR])
        gain = sb("gain", [P, D])
        eps = sb("eps", [P, 1])
        x1 = sb("x1", [P, 2, D])
        junk = sb("junk", [P, D], BF16)
        ssA, sdA, rsA = sb("ssA", [P, 2]), sb("sdA", [P, 2]), sb("rsA", [P, 2])
        ssB, sdB, rsB = sb("ssB", [P, 2]), sb("sdB", [P, 2]), sb("rsB", [P, 2])
        t_hi = sb("t_hi", [P, KT, P], F32R)
        t_lo = sb("t_lo", [P, KT, P], F32R)
        p_hi = sb("p_hi", [P, KT, P], F32R)
        p_lo = sb("p_lo", [P, KT, P], F32R)
        h_hi = sb("h_hi", [P, KT, P], F32R)
        h_lo = sb("h_lo", [P, KT, P], F32R)
        mx, nb = sb("mx", [P, XH]), sb("nb", [P, XH])
        es, re = sb("es", [P, XH]), sb("re", [P, XH])
        pr = sb("pr", [P, XH, MEM])
        x2 = sb("x2", [P, 2, D])
        h3 = sb("h3", [P, 2, D])
        pT = ps("pT", [P, 2, BANK])
        pS = ps("pS", [P, 2, BANK])
        pV = ps("pV", [P, 2, BANK])
        pR = ps("pR", [P, BANK])
        s_c, s_eps, s_rs0 = sem("const"), sem("eps"), sem("r_split")
        s_x = [sem("x0"), sem("x1")]
        s_sqA, s_sdA, s_rsA = sem("sqA"), sem("sdA"), sem("rsA")
        s_sqB, s_sdB, s_rsB = sem("sqB"), sem("sdB"), sem("rsB")
        s_T = [sem("T1"), sem("T2"), sem("T3")]
        s_h = [sem("T1_hi"), sem("T2_hi"), sem("T3_hi")]
        s_l = [sem("T1_lo"), sem("T2_lo"), sem("T3_lo")]
        s_S, s_nb, s_e, s_pn, s_V, s_x2, s_h3 = (sem(n) for n in ("scores", "negmax", "exp", "p", "pv", "x2", "h3"))
        s_R, s_L, s_st = sem("router"), sem("logits"), sem("steps")
        s_ox = [sem("x2out0"), sem("x2out1")]
        s_oh = [sem("h3out0"), sem("h3out1")]
        rows = lambda ap, t: ap.rearrange("(t p) d -> t p d", p=P)[bass.ds(t, 1)].rearrange("o p d -> (o p) d")
        block = ctx.enter_context(nc.Block())

        def pipeline(eng, A, B, C):
            for t in range(4):
                A(t, t % 2)
                if t >= 1:
                    B(t - 1, (t - 1) % 2)
                if t >= 2:
                    C(t - 2, t % 2)
            with eng.Fori(2, NT // 2) as i:
                for u in range(2):
                    A(2 * i + u, u)
                    B(2 * i + u - 1, 1 - u)
                    C(2 * i + u - 2, u)
            B(NT - 1, 1)
            C(NT - 2, 0)
            C(NT - 1, 1)

        def bank_free(eng, stage, t, h):
            if stage == 0:
                if is_first(t, 1):
                    return
                before = (0, 0) if is_first(t, 2) else (1, t - 2) if is_first(t, 3) else (2, t - 3)
            elif stage == 1:
                before = (2, t - 2) if isinstance(t, int) and t == NT - 1 else (0, t + 1)
            else:
                before = (2, t - 1) if isinstance(t, int) and t == NT - 1 else (1, t + 1)
            eng.wait_ge(s_l[before[0]], 2 * before[1] + h + 1)

        @block.sync
        def _(sp):
            sp.dma_start(ident[:], io["ident"]).then_inc(s_c, 16)
            sp.dma_start(rraw[:], io["w_router"]).then_inc(s_c, 16)
            sp.dma_start(rbias[:], io["b_router"]).then_inc(s_c, 16)
            sp.dma_start(gain[:], io["norm_ffn_g"]).then_inc(s_c, 16)

            def store_x2(t, u):
                sp.dma_start(rows(scratch["x2"], t), x2[:, u]).then_inc(s_ox[u], 16)

            def tile(t, u):
                if not is_first(t, 2):
                    sp.wait_ge(s_x2, t - 1)
                    store_x2(t - 2, u)
                sp.dma_start(x1[:, u], rows(scratch["x1"], t)).then_inc(s_x[u], 16)

            tiles2(sp, NT, tile)
            for u in range(2):
                sp.wait_ge(s_x2, NT - 1 + u)
                store_x2(NT - 2 + u, u)
            for u in range(2):
                sp.wait_ge(s_ox[u], 16 * NT // 2)

        @block.gpsimd
        def _(pool):
            def tile(t, u):
                pool.wait_ge(s_h3, t + 1)
                pool.dma_start(rows(scratch["h3"], t), h3[:, u]).then_inc(s_oh[u], 16)

            tiles2(pool, NT, tile)
            for u in range(2):
                pool.wait_ge(s_oh[u], 16 * NT // 2)

        @block.scalar
        def _(act):
            act.wait_ge(s_c, 64)
            act.wait_ge(s_eps, 1)
            act.activation(r_hi[:], rraw[:], ACT.Copy).then_inc(s_rs0, 1)

            def high(stage, t, dst, used):
                for h in range(2):
                    act.wait_ge(s_T[stage], 2 * t + h + 1)
                    if h == 0 and not is_first(t, 1):
                        act.wait_ge(used, t)
                    act.activation(dst[:, 4 * h:4 * h + 4].rearrange("p k n -> p (k n)"), pT[:, h],
                                   ACT.Copy).then_inc(s_h[stage], 1)

            def A(t, u):
                act.wait_ge(s_x[u], landed(t, u))
                act.activation(junk[:], x1[:, u], ACT.Square, accum_out=ssA[:, u:u + 1]).then_inc(s_sqA, 1)
                act.wait_ge(s_sqA, t + 1)
                act.activation(sdA[:, u:u + 1], ssA[:, u:u + 1], ACT.Sqrt, scale=1.0 / D, bias=eps[:]).then_inc(s_sdA, 1)
                high(0, t, t_hi, s_S)

            def B(t, u):
                act.wait_ge(s_nb, t + 1)
                act.wait_ge(s_rsA, t + 1)
                for h in range(XH):
                    last = act.activation(pr[:, h], pS[:, h // 2, (h % 2) * MEM:(h % 2 + 1) * MEM], ACT.Exp,
                                          scale=rsA[:, u:u + 1], bias=nb[:, h:h + 1], accum_out=es[:, h:h + 1])
                last.then_inc(s_e, 1)
                high(1, t, p_hi, s_V)
                act.wait_ge(s_x2, t + 1)
                act.activation(junk[:], x2[:, u], ACT.Square, accum_out=ssB[:, u:u + 1]).then_inc(s_sqB, 1)
                act.wait_ge(s_sqB, t + 1)
                act.activation(sdB[:, u:u + 1], ssB[:, u:u + 1], ACT.Sqrt, scale=1.0 / D, bias=eps[:]).then_inc(s_sdB, 1)

            def C(t, u):
                high(2, t, h_hi, s_R)

            pipeline(act, A, B, C)

        @block.vector
        def _(dve):
            dve.memset(eps[:], EPS).then_inc(s_eps, 1)
            dve.wait_ge(s_c, 64)
            dve.wait_ge(s_rs0, 1)
            dve.tensor_tensor(r_lo[:], rraw[:], r_hi[:], ALU.subtract).then_inc(s_rs0, 1)

            def low(stage, t, hi, lo):
                for h in range(2):
                    dve.wait_ge(s_h[stage], 2 * t + h + 1)
                    cut = lambda x: x[:, 4 * h:4 * h + 4].rearrange("p k n -> p (k n)")
                    dve.tensor_tensor(cut(lo), pT[:, h], cut(hi), ALU.subtract).then_inc(s_l[stage], 1)

            def A(t, u):
                dve.wait_ge(s_sdA, t + 1)
                dve.reciprocal(rsA[:, u:u + 1], sdA[:, u:u + 1]).then_inc(s_rsA, 1)
                low(0, t, t_hi, t_lo)

            def B(t, u):
                st = Steps(dve, s_st, 2 * t)
                dve.wait_ge(s_S, t + 1)
                dve.wait_ge(s_rsA, t + 1)
                st.done(dve.tensor_reduce(mx[:].rearrange("p (a b) -> p a b", a=2),
                                          pS[:].rearrange("p a (b m) -> p a b m", b=2), AX_X, ALU.max))
                dve.tensor_scalar(nb[:], mx[:], rsA[:, u:u + 1], -1.0, ALU.mult, ALU.mult).then_inc(s_nb, 1)
                dve.wait_ge(s_e, t + 1)
                st.done(dve.reciprocal(re[:], es[:]))
                dve.tensor_tensor(pr[:], pr[:], re[:].unsqueeze(2).to_broadcast([P, XH, MEM]), ALU.mult
                                  ).then_inc(s_pn, 1)
                low(1, t, p_hi, p_lo)
                dve.wait_ge(s_V, t + 1)
                if not is_first(t, 2):
                    dve.wait_ge(s_ox[u], landed(t, u) - 16)
                dve.tensor_tensor(x2[:, u], pV[:].rearrange("p a b -> p (a b)"), x1[:, u], ALU.add).then_inc(s_x2, 1)
                dve.wait_ge(s_sdB, t + 1)
                dve.reciprocal(rsB[:, u:u + 1], sdB[:, u:u + 1]).then_inc(s_rsB, 1)
                dve.wait_ge(s_rsB, t + 1)
                if not is_first(t, 2):
                    dve.wait_ge(s_T[2], 2 * t - 2)
                    dve.wait_ge(s_oh[u], landed(t, u) - 16)
                dve.scalar_tensor_tensor(h3[:, u], x2[:, u], rsB[:, u:u + 1], gain[:], ALU.mult, ALU.mult
                                         ).then_inc(s_h3, 1)

            def C(t, u):
                low(2, t, h_hi, h_lo)
                dve.wait_ge(s_R, t + 1)
                dve.tensor_tensor(logits[:, bass.ds(t, 1)].rearrange("p o n -> p (o n)"), pR[:, 0:NR], rbias[:],
                                  ALU.add).then_inc(s_L, 1)

            pipeline(dve, A, B, C)

        @block.tensor
        def _(pe):
            pe.wait_ge(s_c, 64)
            pe.wait_ge(s_rs0, 2)

            def turn(stage, t, src):
                for h in range(2):
                    bank_free(pe, stage, t, h)
                    for k in range(4):
                        last = pe.transpose(pT[:, h, k * P:(k + 1) * P], src[:, (4 * h + k) * P:(4 * h + k + 1) * P],
                                            ident[:])
                    last.then_inc(s_T[stage], 1)

            def product(t, out, hi, lo, W):
                for n in range(2):
                    for k in range(KT):
                        last = mm3(pe, out[:, n], hi[:, k], lo[:, k], W[0][:, k, n * BANK:(n + 1) * BANK],
                                   W[1][:, k, n * BANK:(n + 1) * BANK], k == 0, k == KT - 1)
                return last

            def A(t, u):
                pe.wait_ge(s_x[u], landed(t, u))
                turn(0, t, x1[:, u])
                pe.wait_ge(s_l[0], 2 * t + 2)
                if not is_first(t, 1):
                    pe.wait_ge(s_e, t)
                product(t, pS, t_hi, t_lo, G).then_inc(s_S, 1)

            def B(t, u):
                pe.wait_ge(s_pn, t + 1)
                turn(1, t, pr[:].rearrange("p h m -> p (h m)"))
                pe.wait_ge(s_l[1], 2 * t + 2)
                if not is_first(t, 1):
                    pe.wait_ge(s_x2, t)
                product(t, pV, p_hi, p_lo, VW).then_inc(s_V, 1)

            def C(t, u):
                pe.wait_ge(s_h3, t + 1)
                turn(2, t, h3[:, u])
                pe.wait_ge(s_l[2], 2 * t + 2)
                if not is_first(t, 1):
                    pe.wait_ge(s_L, t)
                for k in range(KT):
                    last = mm3(pe, pR[:, 0:NR], h_hi[:, k], h_lo[:, k], r_hi[:, k], r_lo[:, k], k == 0, k == KT - 1)
                last.then_inc(s_R, 1)

            pipeline(pe, A, B, C)


def routing(nc, io, logits, slot_tok, slot_w, slot_of, first_block, n_blocks, all_blocks):
    ctx = ExitStack()
    with ctx:
        sb = lambda name, shape, dt=F32: ctx.enter_context(nc.sbuf_tensor("ro_" + name, shape, dt))
        ps = lambda name, shape, dt=F32: ctx.enter_context(nc.psum_tensor("ro_" + name, shape, dt))
        sem = lambda name: nc.alloc_semaphore(name="ro_" + name)
        NP = 2 * NT
        count = sb("count", [P, P])
        tri = sb("tri", [P, P])
        ones = sb("ones", [P, P])
        before = sb("before", [P, NE, NE])
        token = sb("token", [P, NT])
        tg, te = sb("tg", [P, NT, NG]), sb("te", [P, NT, NE])
        d4, ex4 = sb("d4", [P, NT, NG]), sb("ex4", [P, NT, NG])
        gm, gw, gi = sb("gm", [P, NT]), sb("gw", [P, NT]), sb("gi", [P, NT])
        le = sb("le", [P, NT, NE])
        m1, m2, ei = sb("m1", [P, NT]), sb("m2", [P, NT]), sb("ei", [P, NT])
        oh = sb("oh", [P, 2, NT, NE])
        e2, w = sb("e2", [P, NT]), sb("w", [P, 2, NT])
        M, Mb = sb("M", [P, NT, NE]), sb("Mb", [P, NT + 1, NE])
        steps15 = sb("steps15", [P, NT - 1])
        steps63 = sb("steps63", [P, NBLK - 1])
        over = sb("over", [P, NE, NT - 1])
        nbf, pbf = sb("nbf", [P, NE]), sb("pbf", [P, NE])
        usedf = sb("usedf", [1, 1])
        prod = sb("prod", [P, NE, NE])
        slots = sb("slots", [P, NT, NE])
        sf, bf, rf = sb("sf", [P, NP]), sb("bf", [P, NP]), sb("rf", [P, NP])
        reach = sb("reach", [P, NP, NBLK - 1])
        ohr = sb("ohr", [P, NP, P])
        ohb = sb("ohb", [P, NP, NBLK])
        val = sb("val", [P, NP, 2, NBLK])
        pR, pN, pS = ps("pR", [P, BANK]), ps("pN", [P, BANK]), ps("pS", [P, BANK])
        s_c, s_st, s_d, s_ex = sem("const"), sem("steps"), sem("differences"), sem("exp")
        s_M, s_R, s_oh, s_S = sem("M"), sem("ranks"), sem("onehots"), sem("slots")
        block = ctx.enter_context(nc.Block())

        @block.sync
        def _(sp):
            for dst, src in ((count, "count"), (tri, "tri"), (ones, "ones"), (before, "before"), (token, "token")):
                sp.dma_start(dst[:], io[src]).then_inc(s_c, 16)

        @block.scalar
        def _(act):
            act.wait_ge(s_d, 1)
            act.activation(ex4[:], d4[:], ACT.Exp).then_inc(s_ex, 1)
            act.wait_ge(s_d, 2)
            act.activation(e2[:], m2[:], ACT.Exp).then_inc(s_ex, 1)

        @block.tensor
        def _(pe):
            pe.wait_ge(s_c, 80)
            pe.wait_ge(s_M, 1)
            flat = lambda x: x.rearrange("p i e -> p (i e)")
            pe.matmul(pR[:], lhsT=tri[:], rhs=flat(M[:]), start=True, stop=False)
            pe.matmul(pR[:], lhsT=ones[:], rhs=flat(Mb[:, 0:NT]), start=False, stop=True)
            pe.matmul(pN[:, 0:NE], lhsT=ones[:], rhs=Mb[:, NT], start=True, stop=True).then_inc(s_R, 1)
            pe.wait_ge(s_oh, 1)
            for n in range(NP):
                last = pe.matmul(pS[:, 0:2 * NBLK], lhsT=ohr[:, n], rhs=val[:, n].rearrange("p v b -> p (v b)"),
                                 start=n == 0, stop=n == NP - 1)
            last.then_inc(s_S, 1)

        @block.vector
        def _(dve):
            dve.wait_ge(s_c, 80)
            st = Steps(dve, s_st)
            wide = lambda x, n: x.unsqueeze(2).to_broadcast([P, x.shape[1], n])
            deep = lambda x, n: x.unsqueeze(1).to_broadcast([P, n, x.shape[1]])

            def first_of(equal, n, index):
                st.done(dve.scalar_tensor_tensor(equal, deep(count[:, 0:n], NT), -float(P), equal, ALU.add, ALU.mult))
                st.done(dve.tensor_reduce(index, equal, AX_X, ALU.min))
                st.done(dve.scalar_tensor_tensor(equal, deep(count[:, 0:n], NT), -float(P), wide(index, n),
                                                 ALU.add, ALU.is_equal))

            lg = logits[:, :, 0:NG]
            st.done(dve.tensor_reduce(gm[:], lg, AX_X, ALU.max))
            dve.tensor_tensor(d4[:], lg, wide(gm[:], NG), ALU.subtract).then_inc(s_d, 1)
            st.done(dve.tensor_tensor(tg[:], lg, wide(gm[:], NG), ALU.is_equal))
            first_of(tg[:], NG, gi[:])
            dve.wait_ge(s_ex, 1)
            st.done(dve.tensor_reduce(gw[:], ex4[:], AX_X, ALU.add))
            st.done(dve.reciprocal(gw[:], gw[:]))
            st.done(dve.tensor_scalar(tg[:], tg[:], -1.0, BIG, ALU.add, ALU.mult))
            st.done(dve.tensor_copy(le[:], logits[:, :, NG:]))
            st.done(dve.tensor_tensor(le[:].rearrange("p i (g e) -> p (i g) e", g=NG),
                                      le[:].rearrange("p i (g e) -> p (i g) e", g=NG),
                                      wide(tg[:].rearrange("p i g -> p (i g)"), EG), ALU.add))
            st.done(dve.tensor_reduce(m1[:], le[:], AX_X, ALU.max))
            st.done(dve.tensor_tensor(oh[:, 0], le[:], wide(m1[:], NE), ALU.is_equal))
            first_of(oh[:, 0], NE, ei[:])
            st.done(dve.scalar_tensor_tensor(le[:], oh[:, 0], -2 * BIG, le[:], ALU.mult, ALU.add))
            st.done(dve.tensor_reduce(m2[:], le[:], AX_X, ALU.max))
            st.done(dve.tensor_tensor(oh[:, 1], le[:], wide(m2[:], NE), ALU.is_equal))
            first_of(oh[:, 1], NE, ei[:])
            dve.tensor_tensor(m2[:], m2[:], m1[:], ALU.subtract).then_inc(s_d, 1)
            st.done(dve.tensor_tensor(M[:], oh[:, 0], oh[:, 1], ALU.add))
            st.done(dve.memset(Mb[:, 0], 0.0))
            for i in range(NT):
                last = dve.tensor_tensor(Mb[:, i + 1], Mb[:, i], M[:, i], ALU.add)
                if i + 1 < NT:
                    st.done(last)
            last.then_inc(s_M, 1)
            dve.wait_ge(s_ex, 2)
            st.done(dve.tensor_scalar(w[:, 0], e2[:], 1.0, None, ALU.add))
            st.done(dve.reciprocal(w[:, 0], w[:, 0]))
            st.done(dve.tensor_tensor(w[:, 0], w[:, 0], gw[:], ALU.mult))
            st.done(dve.tensor_tensor(w[:, 1], w[:, 0], e2[:], ALU.mult))
            dve.tensor_scalar(steps15[:], count[:, 1:NT], float(P), None, ALU.mult)
            st.done(dve.tensor_scalar(steps63[:], count[:, 1:NBLK], float(P), None, ALU.mult))
            dve.wait_ge(s_R, 1)
            st.done(dve.tensor_tensor(over[:], wide(pN[:, 0:NE], NT - 1), deep(steps15[:], NE), ALU.is_gt))
            st.done(dve.tensor_reduce(nbf[:], over[:], AX_X, ALU.add))
            st.done(dve.tensor_scalar(nbf[:], nbf[:], 1.0, None, ALU.add))
            st.done(dve.tensor_tensor(prod[:], before[:], deep(nbf[:], NE), ALU.mult))
            st.done(dve.tensor_reduce(pbf[:], prod[:], AX_X, ALU.add))
            dve.tensor_copy(n_blocks[:], nbf[0:1])
            dve.tensor_copy(first_block[:], pbf[0:1])
            st.done(dve.tensor_tensor(usedf[:], pbf[0:1, NE - 1:NE], nbf[0:1, NE - 1:NE], ALU.add))
            dve.tensor_copy(all_blocks[:, 0:1], usedf[:])
            dve.tensor_scalar(all_blocks[:, 1:2], usedf[:], -1.0, float(NBLK), ALU.mult, ALU.add)
            st.done(dve.scalar_tensor_tensor(slots[:], deep(pbf[:], NT), float(P),
                                             pR[:].rearrange("p (i e) -> p i e", i=NT), ALU.mult, ALU.add))
            for k in range(2):
                st.done(dve.tensor_tensor(oh[:, k], oh[:, k], slots[:], ALU.mult))
            st.done(dve.tensor_reduce(sf[:], oh[:].rearrange("p k i e -> p (k i) e"), AX_X, ALU.add))
            dve.tensor_copy(slot_of[:], sf[:])
            st.done(dve.tensor_tensor(reach[:], wide(sf[:], NBLK - 1), deep(steps63[:], NP), ALU.is_ge))
            st.done(dve.tensor_reduce(bf[:], reach[:], AX_X, ALU.add))
            st.done(dve.scalar_tensor_tensor(rf[:], bf[:], -float(P), sf[:], ALU.mult, ALU.add))
            dve.tensor_tensor(ohr[:], wide(rf[:], P), deep(count[:], NP), ALU.is_equal)
            st.done(dve.tensor_tensor(ohb[:], wide(bf[:], NBLK), deep(count[:, 0:NBLK], NP), ALU.is_equal))
            for k in range(2):
                cut = slice(k * NT, (k + 1) * NT)
                dve.tensor_tensor(val[:, cut, 0], ohb[:, cut], wide(token[:], NBLK), ALU.mult)
                last = dve.tensor_tensor(val[:, cut, 1], ohb[:, cut], wide(w[:, k], NBLK), ALU.mult)
            last.then_inc(s_oh, 1)
            dve.wait_ge(s_S, 1)
            dve.tensor_copy(slot_tok[:, 0:NBLK], pS[:, 0:NBLK])
            dve.tensor_copy(slot_w[:, 0:NBLK], pS[:, NBLK:2 * NBLK])


def experts(nc, io, scratch, slot_tok, slot_w, first_block, n_blocks, all_blocks):
    ctx = ExitStack()
    with ctx:
        sb = lambda name, shape, dt=F32: ctx.enter_context(nc.sbuf_tensor("ex_" + name, shape, dt))
        ps = lambda name, shape, dt=F32: ctx.enter_context(nc.psum_tensor("ex_" + name, shape, dt))
        sem = lambda name: nc.alloc_semaphore(name="ex_" + name)
        NCK = 6
        CW = 4 * DE
        HT = DE // P
        ident = sb("ident", [P, P])
        raw = sb("raw", [P, NCK, CW])
        w_hi = sb("w_hi", [P, NCK, CW], F32R)
        w_lo = sb("w_lo", [P, NCK, CW], F32R)
        row = sb("row", [P, 1], I32)
        xg = sb("xg", [P, D])
        xT_hi = sb("xT_hi", [P, KT, P], F32R)
        xT_lo = sb("xT_lo", [P, KT, P], F32R)
        sil = sb("sil", [P, DE])
        hm = sb("hm", [P, DE])
        hT_hi = sb("hT_hi", [P, HT, P], F32R)
        hT_lo = sb("hT_lo", [P, HT, P], F32R)
        y = sb("y", [P, D])
        zero = sb("zero", [P, D])
        warm = sb("warm", [P, 1])
        pG, pU = ps("pG", [P, BANK]), ps("pU", [P, BANK])
        pT = ps("pT", [P, 2, BANK])
        pH = ps("pH", [P, BANK])
        pD = ps("pD", [P, 2, BANK])
        s_c, s_warm, s_zero, s_fill = sem("const"), sem("warm"), sem("zero"), sem("filled")
        s_w = [sem("w%d" % c) for c in range(NCK)]
        s_hi, s_lo = sem("w_hi"), sem("w_lo")
        s_row, s_asked, s_x = sem("row"), sem("asked"), sem("rows")
        s_T, s_xh, s_xl = sem("T"), sem("xT_hi"), sem("xT_lo")
        s_G, s_U, s_sil, s_hm = sem("gate"), sem("up"), sem("silu"), sem("hidden")
        s_TH, s_hh, s_hl = sem("TH"), sem("hT_hi"), sem("hT_lo")
        s_D, s_y, s_yo, s_stored = sem("down"), sem("y"), sem("y_out"), sem("all_stored")
        up_in = lambda w, e, c: io[w][bass.ds(e, 1)].rearrange("o (p c) n -> (o p) (c n)", p=P)[:, c * CW:(c + 1) * CW]
        chunk = lambda e, c: up_in(("w_gate", "w_gate", "w_up", "w_up", "w_down", "w_down")[c], e, c % 2)
        ysr = scratch["ys"].rearrange("(b p) d -> b p d", p=P)
        block = ctx.enter_context(nc.Block())

        def each_block(eng, body):
            def expert(e, more):
                n = eng.value_load(n_blocks[0:1, bass.ds(e, 1)], min_val=1, max_val=NT)
                first = eng.value_load(first_block[0:1, bass.ds(e, 1)], min_val=0, max_val=NBLK - 2)
                with eng.If(n > 1):
                    with eng.Fori(0, n - 1) as j:
                        body(first + j, e, False, more)
                body(first + n - 1, e, True, more)

            with eng.Fori(0, NE - 1) as e:
                expert(e, True)
            expert(NE - 1, False)

        @block.sync
        def _(sp):
            sp.dma_start(ident[:], io["ident"]).then_inc(s_c, 16)
            for c in range(NCK):
                sp.dma_start(raw[:, c], chunk(0, c)).then_inc(s_w[c], 16)
            sp.wait_ge(s_zero, 1)
            used = sp.value_load(all_blocks[0:1, 0:1], min_val=NE, max_val=NBLK - 1)
            with sp.Fori(used, NBLK) as b:
                sp.dma_start(ysr[bass.ds(b, 1)].rearrange("o p d -> (o p) d"), zero[:]).then_inc(s_fill, 16)
            with sp.Fori(1, NE) as e:
                for c in range(NCK):
                    sp.wait_ge(s_lo, NCK * e - NCK + c + 1)
                    sp.dma_start(raw[:, c], chunk(e, c)).then_inc(s_w[c], 16)
            unused = sp.value_load(all_blocks[0:1, 1:2], min_val=1, max_val=NBLK - NE)
            sp.wait_ge(s_fill, 16 * unused)
            sp.sem_inc(s_stored, 1)

        @block.gpsimd
        def _(pool):
            def gather(b):
                pool.tensor_copy(row[:], slot_tok[:, bass.ds(b, 1)]).then_inc(s_row, 1)
                pool.wait_ge(s_row, b + 1)
                pool.sem_inc(s_asked, 1)
                pool.indirect_dma_start(out=xg[:], out_offset=None, in_=scratch["h3"],
                                        in_offset=bass.IndirectOffsetOnAxis(ap=row[:].bitcast(U32), axis=0)
                                        ).then_inc(s_x, 16)

            pool.memset(zero[:], 0.0).then_inc(s_zero, 1)
            gather(0)
            used = pool.value_load(all_blocks[0:1, 0:1], min_val=NE, max_val=NBLK - 1)
            with pool.Fori(0, used) as b:
                pool.wait_ge(s_T, 2 * b + 2)
                gather(b + 1)

        @block.scalar
        def _(act):
            def high(e, c):
                act.wait_ge(s_w[c], 16 * e + 16)
                act.activation(w_hi[:, c], raw[:, c], ACT.Copy).then_inc(s_hi, 1)

            def turned(b, h):
                act.wait_ge(s_T, 2 * b + h + 1)
                act.activation(xT_hi[:, 4 * h:4 * h + 4].rearrange("p k n -> p (k n)"), pT[:, h], ACT.Copy).then_inc(s_xh, 1)

            act.sem_inc(s_sil, 1)
            act.sem_inc(s_y, 1)
            act.dma_start(y[:, 0:P], io["ident"]).then_inc(s_yo, 16)
            act.wait_ge(s_c, 16)
            act.activation(warm[:], ident[:, 0:1], ACT.Silu).then_inc(s_warm, 1)
            for c in range(NCK):
                high(0, c)
            for h in range(2):
                turned(0, h)

            def body(b, e, last, more):
                act.wait_ge(s_G, b + 1)
                act.wait_ge(s_hm, b + 1)
                act.activation(sil[:], pG[:], ACT.Silu).then_inc(s_sil, 1)
                if last and more:
                    high(e + 1, 0)
                    high(e + 1, 1)
                act.wait_ge(s_U, b + 1)
                turned(b + 1, 0)
                act.wait_ge(s_TH, b + 1)
                act.wait_ge(s_D, b + 1)
                act.activation(hT_hi[:].rearrange("p k n -> p (k n)"), pH[:], ACT.Copy).then_inc(s_hh, 1)
                turned(b + 1, 1)
                if last and more:
                    high(e + 1, 2)
                    high(e + 1, 3)
                act.wait_ge(s_D, b + 2)
                act.wait_ge(s_yo, 16 * b + 16)
                act.activation(y[:], pD[:].rearrange("p a b -> p (a b)"), ACT.Identity,
                               scale=slot_w[:, bass.ds(b, 1)]).then_inc(s_y, 1)
                act.wait_ge(s_y, b + 2)
                act.dma_start(ysr[bass.ds(b, 1)].rearrange("o p d -> (o p) d"), y[:]).then_inc(s_yo, 16)
                if last and more:
                    high(e + 1, 4)
                    high(e + 1, 5)
                if last and not more:
                    act.wait_ge(s_yo, 16 * b + 32)
                    act.sem_inc(s_stored, 1)

            each_block(act, body)

        @block.vector
        def _(dve):
            def low(e, c):
                dve.wait_ge(s_hi, NCK * e + c + 1)
                dve.tensor_tensor(w_lo[:, c], raw[:, c], w_hi[:, c], ALU.subtract).then_inc(s_lo, 1)

            def turned(b, h):
                dve.wait_ge(s_xh, 2 * b + h + 1)
                cut = lambda x: x[:, 4 * h:4 * h + 4].rearrange("p k n -> p (k n)")
                dve.tensor_tensor(cut(xT_lo), pT[:, h], cut(xT_hi), ALU.subtract).then_inc(s_xl, 1)

            dve.sem_inc(s_hm, 1)
            dve.sem_inc(s_hl, 1)
            for c in range(NCK):
                low(0, c)
            for h in range(2):
                turned(0, h)

            def body(b, e, last, more):
                if last and more:
                    low(e + 1, 0)
                dve.wait_ge(s_sil, b + 2)
                dve.wait_ge(s_U, b + 1)
                dve.tensor_tensor(hm[:], sil[:], pU[:], ALU.mult).then_inc(s_hm, 1)
                turned(b + 1, 0)
                dve.wait_ge(s_hh, b + 1)
                flat = lambda x: x[:].rearrange("p k n -> p (k n)")
                dve.tensor_tensor(flat(hT_lo), pH[:], flat(hT_hi), ALU.subtract).then_inc(s_hl, 1)
                turned(b + 1, 1)
                if last and more:
                    for c in range(1, NCK):
                        low(e + 1, c)

            each_block(dve, body)

        @block.tensor
        def _(pe):
            pe.sem_inc(s_D, 1)
            pe.wait_ge(s_c, 16)

            def turn(b, h):
                pe.wait_ge(s_x, 16 * b + 16)
                rows = xg[:].rearrange("p (q c) -> p q c", c=KT)
                for k in range(4):
                    ins = pe.transpose(pT[:, h, k * P:(k + 1) * P], rows[:, :, 4 * h + k], ident[:])
                ins.then_inc(s_T, 1)

            for h in range(2):
                turn(0, h)

            def body(b, e, last, more):
                wh = w_hi[:].rearrange("p k (c n) -> p (k c) n", n=DE)
                wl = w_lo[:].rearrange("p k (c n) -> p (k c) n", n=DE)
                pe.wait_ge(s_xl, 2 * b + 2)
                pe.wait_ge(s_lo, NCK * e + 2)
                pe.wait_ge(s_sil, b + 1)
                for k in range(KT):
                    ins = mm3(pe, pG[:], xT_hi[:, k], xT_lo[:, k], wh[:, k], wl[:, k], k == 0, k == KT - 1)
                ins.then_inc(s_G, 1)
                pe.wait_ge(s_lo, NCK * e + 4)
                pe.wait_ge(s_hm, b + 1)
                for k in range(KT):
                    ins = mm3(pe, pU[:], xT_hi[:, k], xT_lo[:, k], wh[:, KT + k], wl[:, KT + k], k == 0, k == KT - 1)
                ins.then_inc(s_U, 1)
                turn(b + 1, 0)
                pe.wait_ge(s_hm, b + 2)
                pe.wait_ge(s_hl, b + 1)
                hc = hm[:].rearrange("p (q c) -> p q c", c=HT)
                for k in range(HT):
                    ins = pe.transpose(pH[:, k * P:(k + 1) * P], hc[:, :, k], ident[:])
                ins.then_inc(s_TH, 1)
                turn(b + 1, 1)
                pe.wait_ge(s_hl, b + 2)
                pe.wait_ge(s_lo, NCK * e + 6)
                pe.wait_ge(s_y, b + 1)
                wh = w_hi[:, 4:6].rearrange("p k (c n) -> p (k c) n", n=D)
                wl = w_lo[:, 4:6].rearrange("p k (c n) -> p (k c) n", n=D)
                for n in range(2):
                    cut = slice(n * BANK, (n + 1) * BANK)
                    for k in range(HT):
                        ins = mm3(pe, pD[:, n], hT_hi[:, k], hT_lo[:, k], wh[:, k, cut], wl[:, k, cut], k == 0, k == HT - 1)
                ins.then_inc(s_D, 1)

            each_block(pe, body)


def combine(nc, io, scratch, slot_of, out):
    ctx = ExitStack()
    with ctx:
        sb = lambda name, shape, dt=F32: ctx.enter_context(nc.sbuf_tensor("co_" + name, shape, dt))
        sem = lambda name: nc.alloc_semaphore(name="co_" + name)
        gain = sb("gain", [P, D])
        eps = sb("eps", [P, 1])
        x2 = sb("x2", [P, 2, D])
        row = sb("row", [P, 2, 2], I32)
        ya, yb = sb("ya", [P, 2, D]), sb("yb", [P, 2, D])
        acc = sb("acc", [P, 2, D])
        res = sb("res", [P, 2, D])
        junk = sb("junk", [P, D], BF16)
        ss, sd, rs = sb("ss", [P, 2]), sb("sd", [P, 2]), sb("rs", [P, 2])
        s_c, s_eps = sem("gain"), sem("eps")
        s_row, s_asked = sem("row"), sem("asked")
        s_x = [sem("x0"), sem("x1")]
        s_a = [sem("ya0"), sem("ya1")]
        s_b = [sem("yb0"), sem("yb1")]
        s_y, s_acc, s_sq, s_sd, s_rs, s_r = (sem(n) for n in ("pair", "sum", "squares", "deviation", "rstd", "result"))
        s_o = [sem("o0"), sem("o1")]
        rows = lambda ap, t: ap.rearrange("(t p) d -> t p d", p=P)[bass.ds(t, 1)].rearrange("o p d -> (o p) d")
        block = ctx.enter_context(nc.Block())

        @block.sync
        def _(sp):
            sp.dma_start(gain[:], io["final_norm_g"]).then_inc(s_c, 16)

            def tile(t, u):
                if not is_first(t, 2):
                    sp.wait_ge(s_acc, t - 1)
                sp.dma_start(x2[:, u], rows(scratch["x2"], t)).then_inc(s_x[u], 16)

            tiles2(sp, NT, tile)

        @block.gpsimd
        def _(pool):
            def tile(t, u):
                if not is_first(t, 2):
                    pool.wait_ge(s_acc, t - 1)
                for k in range(2):
                    last = pool.tensor_copy(row[:, u, k:k + 1], slot_of[:, bass.ds(t + k * NT, 1)])
                last.then_inc(s_row, 1)
                pool.wait_ge(s_row, t + 1)
                pool.sem_inc(s_asked, 1)
                for k, (dst, done) in enumerate(((ya, s_a), (yb, s_b))):
                    pool.indirect_dma_start(out=dst[:, u], out_offset=None, in_=scratch["ys"][0:NBLK * P],
                                            in_offset=bass.IndirectOffsetOnAxis(
                                                ap=row[:, u, k:k + 1].bitcast(U32), axis=0)
                                            ).then_inc(done[u], 16)

            tiles2(pool, NT, tile)

        @block.vector
        def _(dve):
            dve.memset(eps[:], EPS).then_inc(s_eps, 1)

            def add(t, u):
                dve.wait_ge(s_a[u], landed(t, u))
                dve.wait_ge(s_b[u], landed(t, u))
                if not is_first(t, 2):
                    dve.wait_ge(s_r, t - 1)
                dve.tensor_tensor(acc[:, u], ya[:, u], yb[:, u], ALU.add).then_inc(s_y, 1)
                dve.wait_ge(s_y, t + 1)
                dve.wait_ge(s_x[u], landed(t, u))
                dve.tensor_tensor(acc[:, u], acc[:, u], x2[:, u], ALU.add).then_inc(s_acc, 1)

            def scale(t, u):
                dve.wait_ge(s_sd, t + 1)
                dve.reciprocal(rs[:, u:u + 1], sd[:, u:u + 1]).then_inc(s_rs, 1)
                dve.wait_ge(s_rs, t + 1)
                if not is_first(t, 2):
                    dve.wait_ge(s_o[u], landed(t, u) - 16)
                dve.scalar_tensor_tensor(res[:, u], acc[:, u], rs[:, u:u + 1], gain[:], ALU.mult, ALU.mult).then_inc(s_r, 1)

            add(0, 0)
            add(1, 1)
            dve.wait_ge(s_c, 16)
            scale(0, 0)
            add(2, 0)
            scale(1, 1)
            with dve.Fori(1, NT // 2 - 1) as i:
                add(2 * i + 1, 1)
                scale(2 * i, 0)
                add(2 * i + 2, 0)
                scale(2 * i + 1, 1)
            add(NT - 1, 1)
            scale(NT - 2, 0)
            scale(NT - 1, 1)

        @block.scalar
        def _(act):
            act.wait_ge(s_eps, 1)

            def square(t, u):
                act.wait_ge(s_acc, t + 1)
                act.activation(junk[:], acc[:, u], ACT.Square, accum_out=ss[:, u:u + 1]).then_inc(s_sq, 1)
                act.wait_ge(s_sq, t + 1)
                if not is_first(t, 2):
                    act.wait_ge(s_rs, t - 1)
                act.activation(sd[:, u:u + 1], ss[:, u:u + 1], ACT.Sqrt, scale=1.0 / D, bias=eps[:]).then_inc(s_sd, 1)

            def store(t, u):
                act.wait_ge(s_r, t + 1)
                act.dma_start(rows(out, t), res[:, u]).then_inc(s_o[u], 16)

            square(0, 0)
            square(1, 1)
            store(0, 0)
            square(2, 0)
            store(1, 1)
            with act.Fori(1, NT // 2 - 1) as i:
                square(2 * i + 1, 1)
                store(2 * i, 0)
                square(2 * i + 2, 0)
                store(2 * i + 1, 1)
            square(NT - 1, 1)
            store(NT - 2, 0)
            store(NT - 1, 1)
            for u in range(2):
                act.wait_ge(s_o[u], 16 * NT // 2)


def halves(a):
    a = np.asarray(a, np.float64)

    def round12(v):
        m, e = np.frexp(v)
        return np.ldexp(np.rint(m * 4096), e - 12)

    hi = round12(a)
    return np.stack([hi, round12(a - hi)]).astype(np.float32)


def tables():
    out = {"ident": np.eye(P, dtype=np.float32)}
    out["head_mean"] = np.kron(np.eye(2), np.full((HD, HD), 1.0 / HD)).astype(np.float32)
    d = np.arange(HD)
    cos = np.cos(2 * np.pi * np.outer(d, np.arange(NA)) / HD)
    sin = np.sin(2 * np.pi * np.outer(d, np.arange(1, NA - 1)) / HD)
    one = np.concatenate([cos, sin], 1) / np.sqrt(float(S * HD))
    out["dft64"] = halves(np.kron(np.eye(2), one))
    s1, k1, s2 = np.arange(P), np.arange(P), np.arange(R16)
    ang = 2 * np.pi * ((R16 * s1[None, :, None] + s2[:, None, None]) * k1[None, None, :] % S) / S
    tw = halves(np.concatenate([np.cos(ang), np.sin(ang)], 2))
    out["tw128"] = np.ascontiguousarray(tw.transpose(1, 0, 2, 3))
    ang = 2 * np.pi * (np.outer(np.arange(R16), np.arange(R16)) % R16) / R16
    c, s = (np.kron(np.eye(8), f(ang)) for f in (np.cos, np.sin))
    out["dft16"] = np.stack([halves(m) for m in (c, s, -s)])
    n = np.arange(P)
    out["count"] = np.broadcast_to(n, (P, P)).astype(np.float32)
    out["tri"] = (n[:, None] < n[None, :]).astype(np.float32)
    out["ones"] = np.ones((P, P), np.float32)
    e = np.arange(NE)
    out["before"] = np.broadcast_to(e[None, :] < e[:, None], (P, NE, NE)).astype(np.float32)
    out["token"] = (np.arange(NT)[None, :] * P + n[:, None]).astype(np.float32)
    return out


def laid_out(inputs):
    a = {k: np.asarray(v) for k, v in inputs.items()}
    cols = lambda v: np.ascontiguousarray(v.reshape(-1, P).T)
    order = np.arange(HD)
    order = np.concatenate([order[:NA], order[:NA - 1:-1]])
    perm = np.concatenate([np.arange(CONV), CONV + (np.arange(FG)[:, None] * HD + order).ravel()])
    out = tables()
    out["x"] = a["x"][0]
    out["mem"] = a["mem"][0]
    out["norm_mix_g"] = cols(a["norm_mix_g"][0])
    out["w_f_T"] = a["w_in"][0][:, 3 * CONV:].T
    out["w_conv"] = a["w_in"][0][:, :3 * CONV]
    out["conv_w"] = a["conv_w"][0].reshape(3, CT, P).transpose(2, 0, 1)
    out["conv_b"] = cols(a["conv_b"][0])
    out["head_norm_g"] = cols(a["head_norm_g"][0].reshape(-1)[perm])
    out["w_out"] = a["w_out"][0][perm]
    out["norm_mem_g"] = cols(a["norm_mem_g"][0])
    out["norm_xa_g"] = cols(a["norm_xa_g"][0])
    out["w_kv"] = a["w_kv"][0].reshape(KT, P, KT, 2, P).transpose(2, 1, 3, 0, 4).reshape(KT, P, 2 * D)
    out["w_q"] = a["w_q"][0].T.reshape(XH, 2, P, D).transpose(0, 2, 1, 3).reshape(XH, P, 2 * D)
    out["w_o"] = a["w_o"][0].reshape(XH, 2, P, D).transpose(0, 2, 1, 3).reshape(XH, P, 2 * D)
    router = np.concatenate([a["w_route_group"][0], a["w_route_expert"][0]], 1)
    out["w_router"] = router.reshape(KT, P, NG + NE).transpose(1, 0, 2)
    spread = lambda v: np.broadcast_to(v, (P, v.size))
    out["b_router"] = spread(np.concatenate([a["b_route_group"][0], a["b_route_expert"][0]]))
    out["norm_ffn_g"] = spread(a["norm_ffn_g"][0])
    out["final_norm_g"] = spread(a["final_norm_g"])
    for name in ("w_gate", "w_up", "w_down"):
        out[name] = a[name][0]
    return {k: np.ascontiguousarray(v) for k, v in out.items()}


def build(nc, io, out):
    dram = lambda name, *shape: nc.dram_tensor(name, shape, F32).ap()
    scratch = {"z": dram("z", S, 2, 2, FFT), "yT": dram("yT", P, 2 * CT, 2, S + 2), "x1": dram("x1", S, D),
               "x2": dram("x2", S, D), "h3": dram("h3", S, D), "ys": dram("ys", NCOL * P, D)}

    def phase(body, *args):
        with nc.cleanup_on_exit():
            body(nc, io, *args)

    phase(fourier_front, scratch)
    phase(conv_half, scratch)
    phase(fourier_back, scratch)
    phase(mixer_out, scratch)
    with ExitStack() as kept:
        sb = lambda ctx, name, shape, dt=F32: ctx.enter_context(nc.sbuf_tensor(name, shape, dt))
        logits = sb(kept, "logits", [P, NT, NG + NE])
        slot_tok = sb(kept, "slot_tok", [P, NCOL], I32)
        slot_w = sb(kept, "slot_w", [P, NCOL])
        slot_of = sb(kept, "slot_of", [P, 2 * NT], I32)
        first_block = sb(kept, "first_block", [1, NE], I32)
        n_blocks = sb(kept, "n_blocks", [1, NE], I32)
        all_blocks = sb(kept, "all_blocks", [1, 2], I32)
        with ExitStack() as ctx:
            G = [sb(ctx, "G_" + h, [P, KT, XH * MEM], F32R) for h in ("hi", "lo")]
            VW = [sb(ctx, "VW_" + h, [P, KT, D], F32R) for h in ("hi", "lo")]
            phase(attention_tables, G, VW)
            phase(attention, scratch, G, VW, logits)
        phase(routing, logits, slot_tok, slot_w, slot_of, first_block, n_blocks, all_blocks)
        phase(experts, scratch, slot_tok, slot_w, first_block, n_blocks, all_blocks)
        phase(combine, scratch, slot_of, out)


def kernel(**inputs):
    import concourse.bacc as bacc
    from concourse.bass_utils import run_bass_kernel_spmd

    arrays = laid_out(inputs)
    nc = bacc.Bacc("TRN2", target_bir_lowering=False, num_devices=1)
    io = {k: nc.dram_tensor("in_" + k, v.shape, mybir.dt.from_np(v.dtype), kind="ExternalInput").ap()
          for k, v in arrays.items()}
    out = nc.dram_tensor("out", (S, D), F32, kind="ExternalOutput").ap()
    build(nc, io, out)
    result = run_bass_kernel_spmd(nc, [{"in_" + k: v for k, v in arrays.items()}], core_ids=[0])
    return np.asarray(result.results[0]["out"]).reshape(1, S, D)
```

```python
from contextlib import ExitStack

import numpy as np

import concourse.bass as bass
from concourse import mybir

F32 = mybir.dt.float32
F32R = mybir.dt.float32r
BF16 = mybir.dt.bfloat16
I32 = mybir.dt.int32
U32 = mybir.dt.uint32
ALU = mybir.AluOpType
ACT = mybir.ActivationFunctionType
AX_X = mybir.AxisListType.X

P = 128
D = 1024
S = 2048
KT = D // P
NT = S // P
HD = 64
CONV = 512
CT = CONV // P
FFT = 512
FG = FFT // HD
NA = HD // 2 + 1
NB = HD // 2 - 1
WA, WB = FG * NA, FG * NB
R16 = S // P
MEM = 256
XH = 4
XD = D // XH
NG, EG = 4, 8
NE = NG * EG
DE = D // 2
EPS = 1e-6
NBLK = 64
NCOL = NBLK + S // P
BIG = 1e30
BANK = 512


class Steps:

    def __init__(self, eng, sem, base=0):
        self.eng, self.sem, self.base, self.n = eng, sem, base, 0

    def done(self, ins):
        ins.then_inc(self.sem, 1)
        self.n += 1
        self.eng.wait_ge(self.sem, self.base + self.n)


def mm3(pe, out, a_hi, a_lo, b_hi, b_lo, first, last):
    pe.matmul(out, lhsT=a_lo, rhs=b_hi, start=first, stop=False, skip_group_check=True)
    pe.matmul(out, lhsT=a_hi, rhs=b_lo, start=False, stop=False, skip_group_check=True)
    return pe.matmul(out, lhsT=a_hi, rhs=b_hi, start=False, stop=last, skip_group_check=True)


def tiles2(eng, n, body):
    body(0, 0)
    body(1, 1)
    with eng.Fori(1, n // 2) as i:
        for u in range(2):
            body(i * 2 + u, u)


def words(ap):
    return ap.bitcast(F32)


def landed(t, u):
    return (t - u) * 8 + 16


def is_first(t, n=1):
    return isinstance(t, int) and t < n


def fourier_front(nc, io, scratch):
    ctx = ExitStack()
    with ctx:
        sb = lambda name, shape, dt=F32: ctx.enter_context(nc.sbuf_tensor("ff_" + name, shape, dt))
        ps = lambda name, shape, dt=F32: ctx.enter_context(nc.psum_tensor("ff_" + name, shape, dt))
        sem = lambda name: nc.alloc_semaphore(name="ff_" + name)

        ident = sb("ident", [P, P])
        wraw = sb("wraw", [P, FFT // P, D])
        wt_hi = sb("wt_hi", [P, FFT // P, D], F32R)
        wt_lo = sb("wt_lo", [P, FFT // P, D], F32R)
        dft_hi = sb("dft_hi", [P, P], F32R)
        dft_lo = sb("dft_lo", [P, P], F32R)
        gain = sb("gain", [P, KT])
        wf_hi = sb("wf_hi", [P, KT, FFT], F32R)
        wf_lo = sb("wf_lo", [P, KT, FFT], F32R)
        xs = sb("xs", [P, 2, D])
        junk = sb("junk", [P, D])
        ss = sb("ss", [P, 2])
        ms = sb("ms", [P, 2])
        rstd = sb("rstd", [P, 2])
        eps = sb("eps", [P, 1])
        xT_hi = sb("xT_hi", [P, 2, KT, P], F32R)
        xT_lo = sb("xT_lo", [P, 2, KT, P], F32R)
        u_hi = sb("u_hi", [P, 2, FFT], F32R)
        u_lo = sb("u_lo", [P, 2, FFT], F32R)
        tw = sb("tw", [P, 2, 2, 2 * P], F32R)
        z = sb("z", [P, 2, 2, 2, FFT], F32R)

        pT = ps("pT", [P, 2, BANK])
        pU = ps("pU", [P, 2, BANK])
        pZ = ps("pZ", [P, 2, BANK])

        s_c = sem("const")
        s_w = [sem("w%d" % c) for c in range(FFT // P)]
        s_dft = sem("dft")
        s_wsh = sem("w_split_hi")
        s_wsl = sem("w_split_lo")
        s_fold = sem("folded")
        s_wfh = sem("folded_hi")
        s_wfl = sem("folded_lo")
        s_x = [sem("x0"), sem("x1")]
        s_tw = [sem("tw0"), sem("tw1")]
        s_sq = sem("squares")
        s_rs = sem("rstd")
        s_T = sem("transposed")
        s_xh = sem("xT_hi")
        s_xl = sem("xT_lo")
        s_u = sem("u")
        s_uh = sem("u_hi")
        s_ul = sem("u_lo")
        s_z = sem("z")
        s_zh = sem("z_hi")
        s_zl = sem("z_lo")
        s_o = [sem("zout0"), sem("zout1")]
        s_sd = sem("deviation")
        s_eps = sem("eps")

        x16 = io["x"].rearrange("(a b) d -> b a d", b=R16)
        zrows = scratch["z"].rearrange("(k s) c h f -> s k c h f", s=R16)
        block = ctx.enter_context(nc.Block())

        def schedule(eng, step):
            for i in range(4):
                step(i, i % 2)
            with eng.Fori(2, NT // 2 - 1) as j:
                for u in range(2):
                    step(2 * j + u, u)
            for i in range(NT - 2, NT + 1):
                step(i, i % 2)

        @block.sync
        def _(sp):
            sp.dma_start(ident[:], io["ident"]).then_inc(s_c, 16)
            sp.dma_start(gain[:], io["norm_mix_g"]).then_inc(s_c, 16)
            for c in range(FFT // P):
                sp.dma_start(wraw[:, c], io["w_f_T"][c * P:(c + 1) * P, :]).then_inc(s_w[c], 16)

            def tile(t, u):
                if not is_first(t, 2):
                    sp.wait_ge(s_xl, 2 * t - 2)
                sp.dma_start(xs[:, u], x16[bass.ds(t, 1)].rearrange("o a d -> (o a) d")).then_inc(s_x[u], 16)

            tiles2(sp, NT, tile)

        @block.gpsimd
        def _(pool):
            pool.dma_start(dft_hi[:], io["dft64"][0]).then_inc(s_dft, 16)
            pool.dma_start(dft_lo[:], io["dft64"][1]).then_inc(s_dft, 16)

            def tile(t, u):
                if not is_first(t, 2):
                    pool.wait_ge(s_z, 2 * t - 2)
                pool.dma_start(tw[:, u], io["tw128"][bass.ds(t, 1)].rearrange("o h p k -> p (o h) k")
                               ).then_inc(s_tw[u], 16)

            tiles2(pool, NT, tile)

        @block.scalar
        def _(act):
            act.wait_ge(s_eps, 1)
            act.wait_ge(s_c, 32)
            for c in range(FFT // P):
                act.wait_ge(s_w[c], 16)
                act.activation(wt_hi[:, c], wraw[:, c], ACT.Copy).then_inc(s_wsh, 1)
            for m in range(KT):
                act.wait_ge(s_fold, m + 1)
                src = pU[:, m % 2].rearrange("p (g c) -> p g c", c=HD)
                act.activation(wf_hi[:, m, 0:WA].rearrange("p (g c) -> p g c", c=NA), src[:, :, 0:NA],
                               ACT.Identity, scale=gain[:, m:m + 1])
                act.activation(wf_hi[:, m, WA:].rearrange("p (g c) -> p g c", c=NB), src[:, :, NA:],
                               ACT.Identity, scale=gain[:, m:m + 1]).then_inc(s_wfh, 1)

            def front(t, u):
                act.wait_ge(s_x[u], landed(t, u))
                if not is_first(t, 1):
                    act.wait_ge(s_rs, t)
                act.activation(junk[:], xs[:, u], ACT.Square, accum_out=ss[:, u:u + 1]).then_inc(s_sq, 1)
                act.wait_ge(s_sq, t + 1)
                act.activation(ms[:, u:u + 1], ss[:, u:u + 1], ACT.Sqrt, scale=1.0 / D, bias=eps[:]).then_inc(s_sd, 1)
                for h in range(2):
                    act.wait_ge(s_T, 2 * t + h + 1)
                    if not is_first(t, 2) and h == 0:
                        act.wait_ge(s_u, t - 1)
                    act.activation(xT_hi[:, u, 4 * h:4 * h + 4].rearrange("p k n -> p (k n)"), pT[:, h],
                                   ACT.Copy).then_inc(s_xh, 1)

            def back(t, u):
                act.wait_ge(s_u, t + 1)
                act.wait_ge(s_rs, t + 1)
                if not is_first(t, 2):
                    act.wait_ge(s_z, 2 * t - 2)
                act.activation(u_hi[:, u], pU[:, u], ACT.Identity, scale=rstd[:, u:u + 1]).then_inc(s_uh, 1)

            def ending(t, u):
                for c in range(2):
                    act.wait_ge(s_z, 2 * t + c + 1)
                    if not is_first(t, 2) and c == 0:
                        act.wait_ge(s_o[u], landed(t, u) - 16)
                    act.activation(z[:, u, c, 0], pZ[:, c], ACT.Copy).then_inc(s_zh, 1)
                act.wait_ge(s_zh, 2 * t + 2)
                act.wait_ge(s_zl, 2 * t + 2)
                act.dma_start(zrows[bass.ds(t, 1)].rearrange("o k c h f -> (o k) (c h f)"),
                              words(z[:, u].rearrange("p c h f -> p (c h f)"))).then_inc(s_o[u], 16)

            front(0, 0)

            def step(i, u):
                if not is_first(i, 1):
                    back(i - 1, 1 - u)
                if not (isinstance(i, int) and i + 1 >= NT):
                    front(i + 1, 1 - u)
                if not is_first(i, 1):
                    ending(i - 1, 1 - u)

            schedule(act, step)
            for u in range(2):
                act.wait_ge(s_o[u], 16 * NT // 2)

        @block.vector
        def _(dve):
            dve.memset(eps[:], EPS).then_inc(s_eps, 1)
            dve.wait_ge(s_c, 32)
            for c in range(FFT // P):
                dve.wait_ge(s_wsh, c + 1)
                dve.tensor_tensor(wt_lo[:, c], wraw[:, c], wt_hi[:, c], ALU.subtract).then_inc(s_wsl, 1)
            for m in range(KT):
                dve.wait_ge(s_wfh, m + 1)
                src = pU[:, m % 2].rearrange("p (g c) -> p g c", c=HD)
                for lo, w, at in ((0, WA, 0), (WA, WB, NA)):
                    c = NA if at == 0 else NB
                    hi = wf_hi[:, m, lo:lo + w].rearrange("p (g c) -> p g c", c=c)
                    dst = wf_lo[:, m, lo:lo + w].rearrange("p (g c) -> p g c", c=c)
                    last = dve.scalar_tensor_tensor(dst, src[:, :, at:at + c], gain[:, m:m + 1], hi,
                                                    ALU.mult, ALU.subtract)
                last.then_inc(s_wfl, 1)

            def front(t, u):
                dve.wait_ge(s_sd, t + 1)
                if not is_first(t, 2):
                    dve.wait_ge(s_uh, t - 1)
                    dve.wait_ge(s_ul, t - 1)
                dve.reciprocal(rstd[:, u:u + 1], ms[:, u:u + 1]).then_inc(s_rs, 1)
                for h in range(2):
                    dve.wait_ge(s_xh, 2 * t + h + 1)
                    dve.tensor_tensor(xT_lo[:, u, 4 * h:4 * h + 4].rearrange("p k n -> p (k n)"), pT[:, h],
                                      xT_hi[:, u, 4 * h:4 * h + 4].rearrange("p k n -> p (k n)"),
                                      ALU.subtract).then_inc(s_xl, 1)

            def back(t, u):
                dve.wait_ge(s_uh, t + 1)
                dve.wait_ge(s_rs, t + 1)
                dve.scalar_tensor_tensor(u_lo[:, u], pU[:, u], rstd[:, u:u + 1], u_hi[:, u],
                                         ALU.mult, ALU.subtract).then_inc(s_ul, 1)

            def ending(t, u):
                for c in range(2):
                    dve.wait_ge(s_zh, 2 * t + c + 1)
                    dve.tensor_tensor(z[:, u, c, 1], pZ[:, c], z[:, u, c, 0], ALU.subtract).then_inc(s_zl, 1)

            front(0, 0)

            def step(i, u):
                if not is_first(i, 1):
                    back(i - 1, 1 - u)
                if not (isinstance(i, int) and i + 1 >= NT):
                    front(i + 1, 1 - u)
                if not is_first(i, 1):
                    ending(i - 1, 1 - u)

            schedule(dve, step)

        @block.tensor
        def _(pe):
            pe.wait_ge(s_c, 32)
            pe.wait_ge(s_dft, 32)
            for m in range(KT):
                if m >= 2:
                    pe.wait_ge(s_wfl, m - 1)
                for c in range(FFT // P):
                    if m == 0:
                        pe.wait_ge(s_wsl, c + 1)
                    last = mm3(pe, pU[:, m % 2, c * P:(c + 1) * P], wt_hi[:, c, m * P:(m + 1) * P],
                               wt_lo[:, c, m * P:(m + 1) * P], dft_hi[:], dft_lo[:], True, True)
                last.then_inc(s_fold, 1)
            pe.wait_ge(s_wfl, KT)

            def transposes(t, u):
                pe.wait_ge(s_x[u], landed(t, u))
                for h in range(2):
                    if not is_first(t, 1):
                        pe.wait_ge(s_xl, 2 * t + h - 1)
                    for k in range(4):
                        last = pe.transpose(pT[:, h, k * P:(k + 1) * P], xs[:, u, (4 * h + k) * P:(4 * h + k + 1) * P],
                                            ident[:])
                    last.then_inc(s_T, 1)

            def project(t, u, half):
                if half == 0:
                    pe.wait_ge(s_xl, 2 * t + 2)
                    if not is_first(t, 2):
                        pe.wait_ge(s_ul, t - 1)
                for k in range(half * KT // 2, (half + 1) * KT // 2):
                    last = mm3(pe, pU[:, u], xT_hi[:, u, k], xT_lo[:, u, k], wf_hi[:, k], wf_lo[:, k],
                               k == 0, k == KT - 1)
                if half == 1:
                    last.then_inc(s_u, 1)

            def stage(t, u):
                pe.wait_ge(s_ul, t + 1)
                pe.wait_ge(s_tw[u], landed(t, u))
                for c in range(2):
                    if not is_first(t, 1):
                        pe.wait_ge(s_zl, 2 * t + c - 1)
                    last = mm3(pe, pZ[:, c], tw[:, u, 0, c * P:(c + 1) * P], tw[:, u, 1, c * P:(c + 1) * P],
                               u_hi[:, u], u_lo[:, u], True, True)
                    last.then_inc(s_z, 1)

            transposes(0, 0)

            def step(i, u):
                here = not (isinstance(i, int) and i >= NT)
                if here:
                    project(i, u, 0)
                if not (isinstance(i, int) and i + 1 >= NT):
                    transposes(i + 1, 1 - u)
                if here:
                    project(i, u, 1)
                if not is_first(i, 1):
                    stage(i - 1, 1 - u)

            schedule(pe, step)


def fourier_back(nc, io, scratch, yT, w_hi, w_lo):
    ctx = ExitStack()
    with ctx:
        sb = lambda name, shape, dt=F32: ctx.enter_context(nc.sbuf_tensor("fb_" + name, shape, dt))
        ps = lambda name, shape, dt=F32: ctx.enter_context(nc.psum_tensor("fb_" + name, shape, dt))
        sem = lambda name: nc.alloc_semaphore(name="fb_" + name)
        ident = sb("ident", [P, P])
        dft = sb("dft", [P, 3, 2, P], F32R)
        z = sb("z", [P, 2, 2, 2, FFT], F32R)
        yb = sb("yb", [P, 2, WB])
        y = sb("y", [P, 2, FG, HD])
        sq = sb("sq", [P, FG, HD])
        ss = sb("ss", [P, 2, FG])
        ms = sb("ms", [P, 2, FG])
        eps = sb("eps", [P, 1])
        rs = sb("rs", [P, FG])
        yn = sb("yn", [P, 2, FG, HD])
        wraw = sb("wraw", [P, KT, D])
        gain = sb("gain", [P, KT])
        pY = ps("pY", [P, 2, BANK])
        pT = ps("pT", [P, 2, BANK])
        s_c = sem("const")
        s_d = sem("dft")
        s_zi = [sem("z0"), sem("z1")]
        s_Y = sem("Y")
        s_yb = sem("yb")
        s_ys = sem("y_sum")
        s_yn = sem("yn")
        s_T = sem("T")
        s_th = sem("T_hi")
        s_tl = sem("T_lo")
        s_st = sem("steps")
        s_w, s_wh = sem("w"), sem("w_hi")
        s_ss = sem("squares")
        s_rs = sem("1/rms")
        s_sd = sem("deviation")
        s_eps = sem("eps")
        zt = scratch["z"].rearrange("(b q) c h f -> b q (c h f)", q=P)
        block = ctx.enter_context(nc.Block())

        @block.sync
        def _(sp):
            sp.dma_start(ident[:], io["ident"]).then_inc(s_c, 16)
            sp.dma_start(gain[:], io["head_norm_g"]).then_inc(s_c, 16)

            def tile(t, u):
                if not is_first(t, 2):
                    sp.wait_ge(s_Y, t - 1)
                sp.dma_start(words(z[:, u].rearrange("p c h f -> p (c h f)")),
                             zt[bass.ds(t, 1)].rearrange("o q n -> (o q) n")).then_inc(s_zi[u], 16)

            tiles2(sp, NT, tile)

        @block.gpsimd
        def _(pool):
            pool.dma_start(dft[:], io["dft16"].rearrange("c h p k -> p c h k")).then_inc(s_d, 16)
            for k in range(KT):
                pool.wait_ge(s_Y, 2 * k + 1)
                if k:
                    pool.wait_ge(s_w, 16 * k)
                pool.dma_start(wraw[:, k], io["w_out"][k * P:(k + 1) * P, :]).then_inc(s_w, 16)

        @block.scalar
        def _(act):
            act.wait_ge(s_c, 32)
            act.wait_ge(s_eps, 1)

            def tile(t, u):
                act.wait_ge(s_Y, t + 1)
                if not is_first(t, 2):
                    act.wait_ge(s_yn, t - 1)
                act.activation(yb[:, u], pY[:, u, WA:], ACT.Copy)
                act.activation(y[:, u, :, 0:NA:NA - 1],
                               pY[:, u, 0:WA].rearrange("p (g c) -> p g c", c=NA)[:, :, 0:NA:NA - 1],
                               ACT.Copy).then_inc(s_yb, 1)

            def deviation(t, u):
                act.wait_ge(s_ss, t + 1)
                act.activation(ms[:, u], ss[:, u], ACT.Sqrt, scale=1.0 / HD, bias=eps[:]).then_inc(s_sd, 1)

            def turned(t, u):
                act.wait_ge(s_T, t + 1)
                act.activation(yT[:, 0].rearrange("p j (k b a) -> p j k b a", b=NT, a=8)[:, :, :, bass.ds(t, 1), :]
                               .rearrange("p j k o a -> p j k (o a)"),
                               pT[:, u].rearrange("p (j a k) -> p j k a", j=CT, a=8), ACT.Copy).then_inc(s_th, 1)

            def weights(k):
                act.wait_ge(s_w, 16 * k + 16)
                one = lambda x: x[:, bass.ds(k, 1)].rearrange("p o d -> p (o d)")
                act.activation(one(w_hi), one(wraw), ACT.Identity, scale=gain[:, bass.ds(k, 1)]).then_inc(s_wh, 1)

            tile(0, 0)
            deviation(0, 0)
            tile(1, 1)
            turned(0, 0)
            deviation(1, 1)
            with act.Fori(1, NT // 2) as i:
                tile(2 * i, 0)
                turned(2 * i - 1, 1)
                deviation(2 * i, 0)
                weights(i - 1)
                tile(2 * i + 1, 1)
                turned(2 * i, 0)
                deviation(2 * i + 1, 1)
            turned(NT - 1, 1)
            weights(NT // 2 - 1)

        @block.vector
        def _(dve):
            dve.memset(eps[:], EPS).then_inc(s_eps, 1)
            def tile(t, u):
                st = Steps(dve, s_st, t * 2)
                ya = pY[:, u, 0:WA].rearrange("p (g c) -> p g c", c=NA)[:, :, 1:NA - 1]
                ybv = yb[:, u].rearrange("p (g c) -> p g c", c=NB)
                dve.wait_ge(s_yb, t + 1)
                dve.tensor_tensor(y[:, u, :, 1:NA - 1], ya, ybv, ALU.subtract)
                st.done(dve.tensor_tensor(y[:, u, :, NA:], ya, ybv, ALU.add))
                st.done(dve.tensor_tensor(sq[:], y[:, u], y[:, u], ALU.mult))
                dve.tensor_reduce(ss[:, u], sq[:], AX_X, ALU.add).then_inc(s_ss, 1)

            def norm(t, u):
                dve.wait_ge(s_sd, t + 1)
                dve.reciprocal(rs[:], ms[:, u]).then_inc(s_rs, 1)
                dve.wait_ge(s_rs, t + 1)
                if not is_first(t, 2):
                    dve.wait_ge(s_T, t - 1)
                dve.tensor_tensor(yn[:, u], y[:, u], rs[:].unsqueeze(2).to_broadcast([P, FG, HD]), ALU.mult
                                  ).then_inc(s_yn, 1)

            def turned(t, u):
                dve.wait_ge(s_th, t + 1)
                view = lambda h: yT[:, h].rearrange("p j (k b a) -> p j k b a", b=NT, a=8)[:, :, :, bass.ds(t, 1), :] \
                    .rearrange("p j k o a -> p j k (o a)")
                dve.tensor_tensor(view(1), pT[:, u].rearrange("p (j a k) -> p j k a", j=CT, a=8), view(0),
                                  ALU.subtract).then_inc(s_tl, 1)

            def weights(k):
                dve.wait_ge(s_wh, k + 1)
                one = lambda x: x[:, bass.ds(k, 1)].rearrange("p o d -> p (o d)")
                dve.scalar_tensor_tensor(one(w_lo), one(wraw), gain[:, bass.ds(k, 1)], one(w_hi), ALU.mult, ALU.subtract)

            tile(0, 0)
            norm(0, 0)
            tile(1, 1)
            turned(0, 0)
            norm(1, 1)
            dve.wait_ge(s_c, 32)
            with dve.Fori(1, NT // 2) as i:
                tile(2 * i, 0)
                turned(2 * i - 1, 1)
                norm(2 * i, 0)
                weights(i - 1)
                tile(2 * i + 1, 1)
                turned(2 * i, 0)
                norm(2 * i + 1, 1)
            turned(NT - 1, 1)
            weights(NT // 2 - 1)

        @block.tensor
        def _(pe):
            pe.wait_ge(s_c, 32)
            pe.wait_ge(s_d, 16)

            def tile(t, u):
                pe.wait_ge(s_zi[u], landed(t, u))
                if not is_first(t, 2):
                    pe.wait_ge(s_yn, t - 1)
                zc = lambda c, h, a, b: z[:, u, c, h, a:b]
                for (lo, hi, terms) in ((0, WA, ((0, 0), (2, 1))), (WA, FFT, ((0, 1), (1, 0)))):
                    for n, (m, c) in enumerate(terms):
                        last = mm3(pe, pY[:, u, lo:hi], dft[:, m, 0], dft[:, m, 1], zc(c, 0, lo, hi), zc(c, 1, lo, hi),
                                   n == 0, n == 1)
                last.then_inc(s_Y, 1)

            def turned(t, u):
                pe.wait_ge(s_yn, t + 1)
                if not is_first(t, 2):
                    pe.wait_ge(s_tl, t - 1)
                for j in range(CT):
                    last = pe.transpose(pT[:, u, j * P:(j + 1) * P],
                                        yn[:, u].rearrange("p g c -> p (g c)")[:, j * P:(j + 1) * P], ident[:])
                last.then_inc(s_T, 1)

            tile(0, 0)
            tile(1, 1)
            turned(0, 0)
            with pe.Fori(1, NT // 2) as i:
                tile(2 * i, 0)
                turned(2 * i - 1, 1)
                tile(2 * i + 1, 1)
                turned(2 * i, 0)
            turned(NT - 1, 1)


def conv_half(nc, io, scratch):
    CH = BANK
    NCH = S // CH
    QT = CH // P
    ctx = ExitStack()
    with ctx:
        sb = lambda name, shape, dt=F32: ctx.enter_context(nc.sbuf_tensor("cv_" + name, shape, dt))
        ps = lambda name, shape, dt=F32: ctx.enter_context(nc.psum_tensor("cv_" + name, shape, dt))
        sem = lambda name: nc.alloc_semaphore(name="cv_" + name)
        ident = sb("ident", [P, P])
        ones = sb("ones", [P, P])
        gain = sb("gain", [P, KT])
        taps = sb("taps", [P, 3, CT])
        cbias = sb("cbias", [P, CT])
        eps = sb("eps", [P, 1])
        with nc.sbuf_tensor("cv_wraw", [P, 2, 3 * CONV], F32) as wraw:
            pass
        hN_hi = sb("hN_hi", [P, KT, CH], F32R)
        w_hi = sb("w_hi", [P, KT, 3 * CONV], F32R)
        w_lo = sb("w_lo", [P, KT, 3 * CONV], F32R)
        xs = sb("xs", [P, 2, D])
        junk = sb("junk", [P, D], BF16)
        ss = sb("ss", [P, 2])
        sd1 = sb("sd1", [P, 2])
        rstd = sb("rstd", [P, 2])
        hT_hi = sb("hT_hi", [P, KT, CH], F32R)
        hT_lo = sb("hT_lo", [P, KT, CH], F32R)
        hN_lo = sb("hN_lo", [P, KT, CH], F32R)
        pb = sb("pb", [P, CT, CH + 2])
        bb = sb("bb", [P, CT, CH + 1])
        cs = sb("cs", [P, CH])
        zc = sb("zc", [P, CH])
        yc = sb("yc", [P, 2, CH])
        sq = sb("sq", [P, CH])
        sd = sb("sd", [P, CH])
        yo = sb("yo", [P, 2, CH], F32R)
        pT = ps("pT", [P, 2, BANK])
        pC = ps("pC", [P, BANK])
        pV = ps("pV", [P, BANK])
        pB = ps("pB", [P, BANK])
        pM = ps("pM", [P, BANK])
        s_c, s_cst = sem("const"), sem("memsets")
        s_w = [sem("w0"), sem("w1")]
        s_wh, s_wl = sem("w_hi"), sem("w_lo")
        s_x = [sem("x0"), sem("x1")]
        s_sq1, s_sd1, s_rs, s_xn = sem("sq1"), sem("sd1"), sem("rstd"), sem("xn")
        s_T, s_Th, s_Tl = sem("T"), sem("T_hi"), sem("T_lo")
        s_C, s_V, s_B = sem("c"), sem("v"), sem("b")
        s_cs, s_bb, s_p, s_car = sem("c_copied"), sem("b_copied"), sem("p"), sem("carried")
        s_sq, s_M, s_sd, s_rd, s_yn, s_yh, s_yl = (sem(n) for n in
                                                   ("squares", "mean", "dev", "rdev", "yn", "y_hi", "y_lo"))
        s_st, s_st2 = sem("steps_conv"), sem("steps_end")
        s_o, s_e = sem("out"), sem("out_end")
        xt = io["x"].rearrange("(t p) d -> t p d", p=P)
        block = ctx.enter_context(nc.Block())

        H = [(hT_hi, hT_lo), (hN_hi, hN_lo)]

        @block.sync
        def _(sp):
            sp.dma_start(ident[:], io["ident"]).then_inc(s_c, 16)
            sp.dma_start(ones[:], io["head_mean"]).then_inc(s_c, 16)
            sp.dma_start(gain[:], io["norm_mix_g"]).then_inc(s_c, 16)
            sp.dma_start(taps[:], io["conv_w"]).then_inc(s_c, 16)
            sp.dma_start(cbias[:], io["conv_b"]).then_inc(s_c, 16)
            for t in range(2):
                sp.dma_start(xs[:, t], xt[t]).then_inc(s_x[t], 16)
            for k in range(KT):
                if k >= 2:
                    sp.wait_ge(s_wl, k - 1)
                sp.dma_start(wraw[:, k % 2], io["w_conv"][k * P:(k + 1) * P, :]).then_inc(s_w[k % 2], 16)
                if k in (1, 2):
                    sp.wait_ge(s_T, 2 * k)
                    sp.dma_start(xs[:, k - 1], xt[k + 1]).then_inc(s_x[k - 1], 16)
            with sp.Fori(2, NT // 2) as i:
                for u in range(2):
                    sp.wait_ge(s_T, 4 * i + 2 * u - 2)
                    sp.dma_start(xs[:, u], xt[bass.ds(2 * i + u, 1)].rearrange("o p d -> (o p) d")).then_inc(s_x[u], 16)

        @block.gpsimd
        def _(pool):
            for n in range(NCH):
                for j in range(CT):
                    idx = 4 * n + j
                    pool.wait_ge(s_yl, idx + 1)
                    pool.wait_ge(s_yh, idx + 1)
                    pool.dma_start(scratch["yT"][:, j, :, n * CH:(n + 1) * CH], words(yo[:])).then_inc(s_o, 16)
            pool.wait_ge(s_o, 16 * 4 * NCH)

        @block.scalar
        def _(act):
            act.wait_ge(s_c, 80)
            act.wait_ge(s_cst, 1)

            def statistics(t, u):
                act.wait_ge(s_x[u], landed(t, u))
                if t >= 2:
                    act.wait_ge(s_rs, t - 1)
                act.activation(junk[:], xs[:, u],
                               ACT.Square, accum_out=ss[:, u:u + 1]).then_inc(s_sq1, 1)
                act.wait_ge(s_sq1, t + 1)
                act.activation(sd1[:, u:u + 1], ss[:, u:u + 1], ACT.Sqrt, scale=1.0 / D, bias=eps[:]).then_inc(s_sd1, 1)

            def turned(t):
                n, q = t // QT, t % QT
                for h in range(2):
                    act.wait_ge(s_T, 2 * t + h + 1)
                    if n >= 2 and q == 0 and h == 0:
                        act.wait_ge(s_B, 4 * (n - 1))
                    act.activation(H[n % 2][0][:, 4 * h:4 * h + 4, q * P:(q + 1) * P],
                                   pT[:, h].rearrange("p (k n) -> p k n", k=4), ACT.Copy).then_inc(s_Th, 1)

            def weights(k):
                act.wait_ge(s_w[k % 2], 16 * (k // 2) + 16)
                act.activation(w_hi[:, k], wraw[:, k % 2], ACT.Identity, scale=gain[:, k:k + 1]).then_inc(s_wh, 1)

            def norm(idx):
                act.wait_ge(s_M, idx + 1)
                if idx >= 1:
                    act.wait_ge(s_rd, idx)
                act.activation(sd[:], pM[:], ACT.Sqrt, bias=eps[:]).then_inc(s_sd, 1)
                act.wait_ge(s_yn, idx + 1)
                if idx >= 1:
                    act.wait_ge(s_o, 16 * idx)
                act.activation(yo[:, 0], yc[:, idx % 2], ACT.Copy).then_inc(s_yh, 1)

            statistics(0, 0)
            for k in range(KT):
                if k + 1 < QT:
                    statistics(k + 1, (k + 1) % 2)
                weights(k)
                if k < QT:
                    turned(k)
            for n in range(NCH):
                for j in range(CT):
                    idx = 4 * n + j
                    act.wait_ge(s_C, idx + 1)
                    if idx >= 1:
                        act.wait_ge(s_p, idx)
                    act.activation(cs[:], pC[:], ACT.Copy).then_inc(s_cs, 1)
                    if n + 1 < NCH:
                        statistics(4 * (n + 1) + j, j % 2)
                        turned(4 * (n + 1) + j)
                    act.wait_ge(s_B, idx + 1)
                    if n >= 1:
                        act.wait_ge(s_car, idx - 3)
                    act.activation(bb[:, j, 1:CH + 1], pB[:], ACT.Copy).then_inc(s_bb, 1)
                    if idx >= 1:
                        norm(idx - 1)
            norm(4 * NCH - 1)
            act.wait_ge(s_M, 4 * NCH + 1)
            act.wait_ge(s_rd, 4 * NCH)
            act.activation(sd[:, 0:CT], pM[:, 0:CT], ACT.Sqrt, bias=eps[:]).then_inc(s_sd, 1)
            act.wait_ge(s_yn, 4 * NCH + 1)
            act.wait_ge(s_o, 16 * 4 * NCH)
            act.activation(yo[:, 0, 0:CT], yc[:, 0, 0:CT], ACT.Copy).then_inc(s_yh, 1)
            act.wait_ge(s_yh, 4 * NCH + 1)
            act.wait_ge(s_yl, 4 * NCH + 1)
            for j in range(CT):
                act.dma_start(scratch["yT"][:, j, :, S:S + 1], words(yo[:, :, j:j + 1]),
                              allow_slow_non_contiguous=True).then_inc(s_e, 16)
            act.wait_ge(s_e, 16 * CT)

        @block.vector
        def _(dve):
            dve.memset(eps[:], EPS).then_inc(s_cst, 1)
            dve.memset(pb[:], 0.0)
            dve.memset(bb[:], 0.0).then_inc(s_cst, 1)
            dve.wait_ge(s_c, 80)
            st = Steps(dve, s_st)

            def statistics(t, u):
                dve.wait_ge(s_sd1, t + 1)
                dve.reciprocal(rstd[:, u:u + 1], sd1[:, u:u + 1]).then_inc(s_rs, 1)
                dve.wait_ge(s_rs, t + 1)
                dve.tensor_scalar(xs[:, u], xs[:, u], rstd[:, u:u + 1], None, ALU.mult).then_inc(s_xn, 1)

            def turned(t):
                n, q = t // QT, t % QT
                for h in range(2):
                    dve.wait_ge(s_Th, 2 * t + h + 1)
                    dve.tensor_tensor(H[n % 2][1][:, 4 * h:4 * h + 4, q * P:(q + 1) * P],
                                      pT[:, h].rearrange("p (k n) -> p k n", k=4),
                                      H[n % 2][0][:, 4 * h:4 * h + 4, q * P:(q + 1) * P],
                                      ALU.subtract).then_inc(s_Tl, 1)

            def weights(k):
                dve.wait_ge(s_wh, k + 1)
                dve.scalar_tensor_tensor(w_lo[:, k], wraw[:, k % 2], gain[:, k:k + 1], w_hi[:, k],
                                         ALU.mult, ALU.subtract).then_inc(s_wl, 1)

            def convolve(n, j):
                idx = 4 * n + j
                dve.wait_ge(s_V, idx + 1)
                dve.wait_ge(s_cs, idx + 1)
                if idx == 0:
                    dve.wait_ge(s_cst, 2)
                dve.tensor_tensor(pb[:, j, 2:CH + 2], cs[:], pV[:], ALU.mult).then_inc(s_p, 1)
                dve.wait_ge(s_p, idx + 1)
                st.done(dve.tensor_scalar(zc[:], pb[:, j, 0:CH], taps[:, 0, j:j + 1], cbias[:, j:j + 1], ALU.mult, ALU.add))
                st.done(dve.scalar_tensor_tensor(zc[:], pb[:, j, 1:CH + 1], taps[:, 1, j:j + 1], zc[:], ALU.mult, ALU.add))
                st.done(dve.scalar_tensor_tensor(zc[:], pb[:, j, 2:CH + 2], taps[:, 2, j:j + 1], zc[:], ALU.mult, ALU.add))
                dve.wait_ge(s_bb, idx + 1)
                if idx >= 2:
                    dve.wait_ge(s_yh, idx - 1)
                    dve.wait_ge(s_yl, idx - 1)
                st.done(dve.tensor_tensor(yc[:, idx % 2], zc[:], bb[:, j, 0:CH], ALU.mult))
                if idx >= 1:
                    dve.wait_ge(s_M, idx)
                dve.tensor_tensor(sq[:], yc[:, idx % 2], yc[:, idx % 2], ALU.mult).then_inc(s_sq, 1)
                st.done(dve.tensor_copy(pb[:, j, 0:2], pb[:, j, CH:CH + 2]))
                dve.tensor_copy(bb[:, j, 0:1], bb[:, j, CH:CH + 1]).then_inc(s_car, 1)

            def norm(idx):
                dve.wait_ge(s_sd, idx + 1)
                dve.reciprocal(sd[:], sd[:]).then_inc(s_st2, 1)
                dve.wait_ge(s_st2, idx + 1)
                ins = dve.tensor_tensor(yc[:, idx % 2], yc[:, idx % 2], sd[:], ALU.mult)
                ins.then_inc(s_yn, 1)
                dve.wait_ge(s_yn, idx + 1)
                dve.wait_ge(s_yh, idx + 1)
                dve.tensor_tensor(yo[:, 1], yc[:, idx % 2], yo[:, 0], ALU.subtract).then_inc(s_yl, 1)
                dve.sem_inc(s_rd, 1)

            statistics(0, 0)
            for k in range(KT):
                if k + 1 < QT:
                    statistics(k + 1, (k + 1) % 2)
                weights(k)
                if k < QT:
                    turned(k)
            for n in range(NCH):
                for j in range(CT):
                    idx = 4 * n + j
                    if n + 1 < NCH:
                        statistics(4 * (n + 1) + j, j % 2)
                        turned(4 * (n + 1) + j)
                    convolve(n, j)
                    if idx >= 1:
                        norm(idx - 1)
            norm(4 * NCH - 1)
            w = slice(0, CT)
            dve.wait_ge(s_car, 4 * NCH)
            dve.wait_ge(s_yh, 4 * NCH)
            dve.wait_ge(s_yl, 4 * NCH)
            dve.tensor_tensor(zc[:, w], pb[:, :, 0], taps[:, 0, :], ALU.mult)
            st.done(dve.tensor_tensor(yc[:, 0, w], pb[:, :, 1], taps[:, 1, :], ALU.mult))
            st.done(dve.tensor_tensor(zc[:, w], zc[:, w], yc[:, 0, w], ALU.add))
            st.done(dve.tensor_tensor(zc[:, w], zc[:, w], cbias[:], ALU.add))
            st.done(dve.tensor_tensor(yc[:, 0, w], zc[:, w], bb[:, :, 0], ALU.mult))
            dve.wait_ge(s_M, 4 * NCH)
            dve.tensor_tensor(sq[:, w], yc[:, 0, w], yc[:, 0, w], ALU.mult).then_inc(s_sq, 1)
            dve.wait_ge(s_sd, 4 * NCH + 1)
            st.done(dve.reciprocal(sd[:, w], sd[:, w]))
            dve.tensor_tensor(yc[:, 0, w], yc[:, 0, w], sd[:, w], ALU.mult).then_inc(s_yn, 1)
            dve.wait_ge(s_yh, 4 * NCH + 1)
            dve.tensor_tensor(yo[:, 1, w], yc[:, 0, w], yo[:, 0, w], ALU.subtract).then_inc(s_yl, 1)

        @block.tensor
        def _(pe):
            pe.wait_ge(s_c, 80)

            def turned(t):
                pe.wait_ge(s_xn, t + 1)
                for h in range(2):
                    if t >= 1:
                        pe.wait_ge(s_Tl, 2 * t + h - 1)
                    for k in range(4):
                        last = pe.transpose(pT[:, h, k * P:(k + 1) * P],
                                            xs[:, t % 2, (4 * h + k) * P:(4 * h + k + 1) * P], ident[:])
                    last.then_inc(s_T, 1)

            def mean(idx, width=CH):
                pe.wait_ge(s_sq, idx + 1)
                if idx >= 1:
                    pe.wait_ge(s_sd, idx)
                pe.matmul(pM[:, 0:width], lhsT=ones[:], rhs=sq[:, 0:width], start=True, stop=True).then_inc(s_M, 1)

            for t in range(QT):
                turned(t)
            for n in range(NCH):
                hh, hl = H[n % 2]
                pe.wait_ge(s_Tl, 8 * (n + 1))
                for j in range(CT):
                    idx = 4 * n + j
                    for g, bank, done in ((1, pC, s_C), (2, pV, s_V), (0, pB, s_B)):
                        if idx >= 1:
                            pe.wait_ge(*{0: (s_bb, idx), 1: (s_cs, idx), 2: (s_p, idx)}[g])
                        c0 = g * CONV + j * P
                        for k in range(KT):
                            if idx == 0 and g == 1:
                                pe.wait_ge(s_wl, k + 1)
                            last = mm3(pe, bank[:], w_hi[:, k, c0:c0 + P], w_lo[:, k, c0:c0 + P], hh[:, k], hl[:, k],
                                       k == 0, k == KT - 1)
                        last.then_inc(done, 1)
                        if g == 1 and idx >= 1:
                            mean(idx - 1)
                        if g == 2 and n + 1 < NCH:
                            turned(4 * (n + 1) + j)
            mean(4 * NCH - 1)
            mean(4 * NCH, CT)


def mixer_out(nc, io, scratch, yT, w_hi, w_lo):
    ctx = ExitStack()
    with ctx:
        sb = lambda name, shape, dt=F32: ctx.enter_context(nc.sbuf_tensor("mo_" + name, shape, dt))
        ps = lambda name, shape, dt=F32: ctx.enter_context(nc.psum_tensor("mo_" + name, shape, dt))
        sem = lambda name: nc.alloc_semaphore(name="mo_" + name)
        yt = sb("yt", [P, 2, CT, 2, P], F32R)
        ft = sb("ft", [P, 2, 2, CT, P], F32R)
        xs = sb("xs", [P, 2, D])
        x1 = sb("x1", [P, 2, D])
        pO = ps("pO", [P, 2, 2, BANK])
        s_f = sem("fourier_tile")
        s_y = [sem("y0"), sem("y1")]
        s_x = [sem("x0"), sem("x1")]
        s_O, s_a = sem("product"), sem("added")
        s_o = [sem("o0"), sem("o1")]
        xt = io["x"].rearrange("(t p) d -> t p d", p=P)
        x1t = scratch["x1"].rearrange("(t p) d -> t p d", p=P)
        yTv = scratch["yT"].rearrange("p k h t -> p (k h) t")
        block = ctx.enter_context(nc.Block())

        @block.sync
        def _(sp):
            def tile(t, u):
                if not is_first(t, 2):
                    sp.wait_ge(s_O, t - 1)
                sp.dma_start(words(yt[:, u].rearrange("p k h t -> p (k h) t")),
                             yTv[:, :, bass.ds(t * P + 1, P)]).then_inc(s_y[u], 16)

            tiles2(sp, NT, tile)

        @block.scalar
        def _(act):
            def take(t, u):
                act.activation(ft[:, u], yT[:, :, :, bass.ds(t * P, P)], ACT.Copy).then_inc(s_f, 1)

            def store(t, u):
                act.wait_ge(s_a, t + 1)
                act.dma_start(x1t[bass.ds(t, 1)].rearrange("o p d -> (o p) d"), x1[:, u]).then_inc(s_o[u], 16)

            take(0, 0)
            take(1, 1)
            with act.Fori(1, NT // 2) as i:
                for u in range(2):
                    act.wait_ge(s_O, 2 * i + u - 1)
                    take(2 * i + u, u)
                    store(2 * i + u - 2, u)
            store(NT - 2, 0)
            store(NT - 1, 1)
            for u in range(2):
                act.wait_ge(s_o[u], 16 * NT // 2)

        @block.gpsimd
        def _(pool):
            def tile(t, u):
                if not is_first(t, 2):
                    pool.wait_ge(s_a, t - 1)
                pool.dma_start(xs[:, u], xt[bass.ds(t, 1)].rearrange("o p d -> (o p) d")).then_inc(s_x[u], 16)

            tiles2(pool, NT, tile)

        @block.vector
        def _(dve):
            def tile(t, u):
                dve.wait_ge(s_O, t + 1)
                dve.wait_ge(s_x[u], landed(t, u))
                if not is_first(t, 2):
                    dve.wait_ge(s_o[u], landed(t, u) - 16)
                dve.tensor_tensor(x1[:, u], pO[:, u].rearrange("p a b -> p (a b)"), xs[:, u], ALU.add).then_inc(s_a, 1)

            tiles2(dve, NT, tile)

        @block.tensor
        def _(pe):
            def tile(t, u):
                pe.wait_ge(s_y[u], landed(t, u))
                pe.wait_ge(s_f, t + 1)
                if not is_first(t, 2):
                    pe.wait_ge(s_a, t - 1)
                for h in range(2):
                    for k in range(KT):
                        hi, lo = (yt[:, u, k, 0], yt[:, u, k, 1]) if k < CT else (ft[:, u, 0, k - CT], ft[:, u, 1, k - CT])
                        last = mm3(pe, pO[:, u, h], hi, lo, w_hi[:, k, h * BANK:(h + 1) * BANK],
                                   w_lo[:, k, h * BANK:(h + 1) * BANK], k == 0, k == KT - 1)
                last.then_inc(s_O, 1)

            tiles2(pe, NT, tile)


def attention_tables(nc, io, G, VW):
    ctx = ExitStack()
    with ctx:
        sb = lambda name, shape, dt=F32: ctx.enter_context(nc.sbuf_tensor("at_" + name, shape, dt))
        ps = lambda name, shape, dt=F32: ctx.enter_context(nc.psum_tensor("at_" + name, shape, dt))
        sem = lambda name: nc.alloc_semaphore(name="at_" + name)
        ident = sb("ident", [P, P])
        gain_m = sb("gain_m", [P, KT])
        gain_q = sb("gain_q", [P, KT])
        eps = sb("eps", [P, 1])
        junk = sb("junk", [P, D], BF16)
        ss, sd, rs = sb("ss", [P, 2]), sb("sd", [P, 2]), sb("rs", [P, 2])
        mT_hi = sb("mT_hi", [P, KT, MEM], F32R)
        mT_lo = sb("mT_lo", [P, KT, MEM], F32R)
        wraw = sb("wraw", [P, 2, D])
        xs = wraw
        w_hi = sb("w_hi", [P, 2, D], F32R)
        w_lo = sb("w_lo", [P, 2, D], F32R)
        kv_hi = sb("kv_hi", [P, 2 * KT, MEM], F32R)
        kv_lo = sb("kv_lo", [P, 2 * KT, MEM], F32R)
        pT = ps("pT", [P, 2, BANK])
        pA = ps("pA", [P, 2, BANK])
        pG = ps("pG", [P, 2, BANK])
        pW = ps("pW", [P, 2, BANK])
        s_c, s_eps, s_gq, s_x = sem("const"), sem("eps"), sem("gain_q"), [sem("x0"), sem("x1")]
        s_sq, s_sd, s_rs, s_xn = sem("sq"), sem("sd"), sem("rs"), sem("xn")
        s_T, s_Th, s_Tl = sem("T"), sem("T_hi"), sem("T_lo")
        s_w, s_wh, s_wl = [sem("w0"), sem("w1")], sem("w_hi"), sem("w_lo")
        s_A, s_Ah, s_Al = sem("kv"), sem("kv_hi"), sem("kv_lo")
        s_G, s_Gh, s_Gl = sem("G"), sem("G_hi"), sem("G_lo")
        s_W, s_Wh, s_Wl = sem("VW"), sem("VW_hi"), sem("VW_lo")
        mt = io["mem"].rearrange("(t p) d -> t p d", p=P)
        LOTS = [("w_kv", i) for i in range(2 * KT)] + [(w, i) for w in ("w_q", "w_o") for i in range(2 * XH)]
        NL = len(LOTS)
        block = ctx.enter_context(nc.Block())

        @block.sync
        def _(sp):
            sp.dma_start(ident[:], io["ident"]).then_inc(s_c, 16)
            sp.dma_start(gain_m[:], io["norm_mem_g"]).then_inc(s_c, 16)
            sp.dma_start(gain_q[:], io["norm_xa_g"]).then_inc(s_c, 16)
            for t in range(2):
                sp.dma_start(xs[:, t], mt[t]).then_inc(s_x[t], 16)
            for n, (w, i) in enumerate(LOTS):
                if n < 2:
                    sp.wait_ge(s_T, 2 * n + 2)
                else:
                    sp.wait_ge(s_wl, n - 1)
                sp.dma_start(wraw[:, n % 2], io[w][i]).then_inc(s_w[n % 2], 16)

        @block.scalar
        def _(act):
            act.wait_ge(s_eps, 1)
            act.wait_ge(s_c, 48)
            act.wait_ge(s_gq, 1)
            for t in range(2):
                act.wait_ge(s_x[t], 16)
                act.activation(junk[:], xs[:, t], ACT.Square, accum_out=ss[:, t:t + 1]).then_inc(s_sq, 1)
                act.wait_ge(s_sq, t + 1)
                act.activation(sd[:, t:t + 1], ss[:, t:t + 1], ACT.Sqrt, scale=1.0 / D, bias=eps[:]).then_inc(s_sd, 1)
                for h in range(2):
                    act.wait_ge(s_T, 2 * t + h + 1)
                    for k in range(4):
                        last = act.activation(mT_hi[:, 4 * h + k, t * P:(t + 1) * P], pT[:, h, k * P:(k + 1) * P],
                                              ACT.Identity, scale=gain_m[:, 4 * h + k:4 * h + k + 1])
                    last.then_inc(s_Th, 1)
            counts = dict.fromkeys(("w_kv", "w_q", "w_o"), 0)

            def split(n):
                act.wait_ge(s_w[n % 2], 16 * (n // 2 + 1))
                act.activation(w_hi[:, n % 2], wraw[:, n % 2], ACT.Copy).then_inc(s_wh, 1)

            split(0)
            for n, (w, i) in enumerate(LOTS):
                if n + 1 < NL:
                    split(n + 1)
                for m in range({"w_kv": 1, "w_q": 4, "w_o": 2}[w]):
                    c = counts[w]
                    counts[w] += 1
                    if w == "w_kv":
                        act.wait_ge(s_A, c + 1)
                        act.activation(kv_hi[:, c], pA[:, c % 2, 0:MEM], ACT.Copy).then_inc(s_Ah, 1)
                    elif w == "w_q":
                        act.wait_ge(s_G, c + 1)
                        k, h = 4 * (i % 2) + m, i // 2
                        act.activation(G[0][:, k, h * MEM:(h + 1) * MEM], pG[:, c % 2, 0:MEM], ACT.Identity,
                                       scale=gain_q[:, k:k + 1]).then_inc(s_Gh, 1)
                    else:
                        act.wait_ge(s_W, c + 1)
                        k, n2 = 2 * (i // 2) + m, i % 2
                        act.activation(VW[0][:, k, n2 * BANK:(n2 + 1) * BANK], pW[:, c % 2], ACT.Copy).then_inc(s_Wh, 1)

        @block.vector
        def _(dve):
            dve.memset(eps[:], EPS).then_inc(s_eps, 1)
            dve.wait_ge(s_c, 48)
            dve.tensor_scalar(gain_q[:], gain_q[:], float(XD) ** -0.5, None, ALU.mult).then_inc(s_gq, 1)
            dve.wait_ge(s_gq, 1)
            for t in range(2):
                dve.wait_ge(s_sd, t + 1)
                dve.reciprocal(rs[:, t:t + 1], sd[:, t:t + 1]).then_inc(s_rs, 1)
                dve.wait_ge(s_rs, t + 1)
                dve.tensor_scalar(xs[:, t], xs[:, t], rs[:, t:t + 1], None, ALU.mult).then_inc(s_xn, 1)
                for h in range(2):
                    dve.wait_ge(s_Th, 2 * t + h + 1)
                    for k in range(4):
                        last = dve.scalar_tensor_tensor(mT_lo[:, 4 * h + k, t * P:(t + 1) * P], pT[:, h, k * P:(k + 1) * P],
                                                        gain_m[:, 4 * h + k:4 * h + k + 1],
                                                        mT_hi[:, 4 * h + k, t * P:(t + 1) * P], ALU.mult, ALU.subtract)
                    last.then_inc(s_Tl, 1)
            counts = dict.fromkeys(("w_kv", "w_q", "w_o"), 0)

            def split(n):
                dve.wait_ge(s_wh, n + 1)
                dve.tensor_tensor(w_lo[:, n % 2], wraw[:, n % 2], w_hi[:, n % 2], ALU.subtract).then_inc(s_wl, 1)

            split(0)
            for n, (w, i) in enumerate(LOTS):
                if n + 1 < NL:
                    split(n + 1)
                for m in range({"w_kv": 1, "w_q": 4, "w_o": 2}[w]):
                    c = counts[w]
                    counts[w] += 1
                    if w == "w_kv":
                        dve.wait_ge(s_Ah, c + 1)
                        dve.tensor_tensor(kv_lo[:, c], pA[:, c % 2, 0:MEM], kv_hi[:, c], ALU.subtract).then_inc(s_Al, 1)
                    elif w == "w_q":
                        dve.wait_ge(s_Gh, c + 1)
                        k, h = 4 * (i % 2) + m, i // 2
                        cut = slice(h * MEM, (h + 1) * MEM)
                        dve.scalar_tensor_tensor(G[1][:, k, cut], pG[:, c % 2, 0:MEM], gain_q[:, k:k + 1],
                                                 G[0][:, k, cut], ALU.mult, ALU.subtract).then_inc(s_Gl, 1)
                    else:
                        dve.wait_ge(s_Wh, c + 1)
                        k, n2 = 2 * (i // 2) + m, i % 2
                        cut = slice(n2 * BANK, (n2 + 1) * BANK)
                        dve.tensor_tensor(VW[1][:, k, cut], pW[:, c % 2], VW[0][:, k, cut], ALU.subtract).then_inc(s_Wl, 1)

        @block.tensor
        def _(pe):
            pe.wait_ge(s_c, 48)
            for t in range(2):
                pe.wait_ge(s_xn, t + 1)
                for h in range(2):
                    if t:
                        pe.wait_ge(s_Tl, h + 1)
                    for k in range(4):
                        last = pe.transpose(pT[:, h, k * P:(k + 1) * P], xs[:, t, (4 * h + k) * P:(4 * h + k + 1) * P],
                                            ident[:])
                    last.then_inc(s_T, 1)
            pe.wait_ge(s_Tl, 4)
            counts = dict.fromkeys(("w_kv", "w_q", "w_o"), 0)
            for n, (w, i) in enumerate(LOTS):
                pe.wait_ge(s_wl, n + 1)
                wh, wl = (x[:, n % 2].rearrange("p (k c) -> p k c", k=KT if w == "w_kv" else 2)
                          for x in (w_hi, w_lo))
                for m in range({"w_kv": 1, "w_q": 4, "w_o": 2}[w]):
                    c = counts[w]
                    counts[w] += 1
                    if w == "w_kv":
                        if c >= 2:
                            pe.wait_ge(s_Al, c - 1)
                        for k in range(KT):
                            last = mm3(pe, pA[:, c % 2, 0:MEM], wh[:, k], wl[:, k], mT_hi[:, k], mT_lo[:, k],
                                       k == 0, k == KT - 1)
                        last.then_inc(s_A, 1)
                    elif w == "w_q":
                        pe.wait_ge(s_Al, 2 * KT)
                        if c >= 2:
                            pe.wait_ge(s_Gl, c - 1)
                        cut, h = slice(m * P, (m + 1) * P), i // 2
                        for k in range(2):
                            last = mm3(pe, pG[:, c % 2, 0:MEM], wh[:, k, cut], wl[:, k, cut],
                                       kv_hi[:, 2 * h + k], kv_lo[:, 2 * h + k], k == 0, k == 1)
                        last.then_inc(s_G, 1)
                    else:
                        if c >= 2:
                            pe.wait_ge(s_Wl, c - 1)
                        cut, h = slice(m * P, (m + 1) * P), i // 2
                        for k in range(2):
                            last = mm3(pe, pW[:, c % 2], kv_hi[:, KT + 2 * h + k, cut], kv_lo[:, KT + 2 * h + k, cut],
                                       wh[:, k], wl[:, k], k == 0, k == 1)
                        last.then_inc(s_W, 1)


def attention(nc, io, scratch, G, VW, logits):
    ctx = ExitStack()
    with ctx:
        sb = lambda name, shape, dt=F32: ctx.enter_context(nc.sbuf_tensor("xa_" + name, shape, dt))
        ps = lambda name, shape, dt=F32: ctx.enter_context(nc.psum_tensor("xa_" + name, shape, dt))
        sem = lambda name: nc.alloc_semaphore(name="xa_" + name)
        NR = NG + NE
        ident = sb("ident", [P, P])
        rraw = sb("rraw", [P, KT, NR])
        r_hi = sb("r_hi", [P, KT, NR], F32R)
        r_lo = sb("r_lo", [P, KT, NR], F32R)
        rbias = sb("rbias", [P, NR])
        gain = sb("gain", [P, D])
        eps = sb("eps", [P, 1])
        x1 = sb("x1", [P, 2, D])
        x1r = sb("x1r", [P, 2, D])
        junk = sb("junk", [P, D], BF16)
        ssA, sdA, rsA = sb("ssA", [P, 2]), sb("sdA", [P, 2]), sb("rsA", [P, 2])
        ssB, sdB, rsB = sb("ssB", [P, 2]), sb("sdB", [P, 2]), sb("rsB", [P, 2])
        t_hi = sb("t_hi", [P, KT, P], F32R)
        t_lo = sb("t_lo", [P, KT, P], F32R)
        p_hi = sb("p_hi", [P, KT, P], F32R)
        p_lo = sb("p_lo", [P, KT, P], F32R)
        h_hi = sb("h_hi", [P, KT, P], F32R)
        h_lo = sb("h_lo", [P, KT, P], F32R)
        mx, nb = sb("mx", [P, XH]), sb("nb", [P, XH])
        es, re = sb("es", [P, XH]), sb("re", [P, XH])
        pr = sb("pr", [P, XH, MEM])
        x2 = sb("x2", [P, 2, D])
        h3 = sb("h3", [P, D])
        pT = ps("pT", [P, 2, BANK])
        pS = ps("pS", [P, 2, BANK])
        pV = ps("pV", [P, 2, BANK])
        pR = ps("pR", [P, BANK])
        s_id, s_c, s_eps, s_rs0 = sem("ident"), sem("const"), sem("eps"), sem("r_split")
        s_x = [sem("x0"), sem("x1")]
        s_xr = [sem("xr0"), sem("xr1")]
        s_sqA, s_sdA, s_rsA = sem("sqA"), sem("sdA"), sem("rsA")
        s_sqB, s_sdB, s_rsB = sem("sqB"), sem("sdB"), sem("rsB")
        s_T = {k: sem("T_" + k) for k in "xph"}
        s_h = {k: sem("hi_" + k) for k in "xph"}
        s_l = {k: sem("lo_" + k) for k in "xph"}
        s_S, s_nb, s_e, s_pn, s_V, s_x2, s_h3 = (sem(n) for n in ("scores", "negmax", "exp", "p", "pv", "x2", "h3"))
        s_R, s_L, s_st = sem("router"), sem("logits"), sem("steps")
        s_ox = [sem("x2out0"), sem("x2out1")]
        s_oh = sem("h3out")
        rows = lambda ap, t: ap.rearrange("(t p) d -> t p d", p=P)[bass.ds(t, 1)].rearrange("o p d -> (o p) d")
        block = ctx.enter_context(nc.Block())

        def schedule(eng, step):
            peeled = lambda i: step(i, i % 2, lambda t: 0 <= t < NT)
            for i in range(-1, 6):
                peeled(i)
            with eng.Fori(3, NT // 2 - 1) as j:
                for u in range(2):
                    step(2 * j + u, u, lambda t: True)
            for i in range(NT - 2, NT + 3):
                peeled(i)

        @block.sync
        def _(sp):
            sp.dma_start(ident[:], io["ident"]).then_inc(s_id, 16)

            def tile(t, u):
                if is_first(t, 2) and t == 1:
                    sp.dma_start(rraw[:], io["w_router"]).then_inc(s_c, 16)
                    sp.dma_start(rbias[:], io["b_router"]).then_inc(s_c, 16)
                    sp.dma_start(gain[:], io["norm_ffn_g"]).then_inc(s_c, 16)
                if not is_first(t, 2):
                    sp.wait_ge(s_l["x"], 2 * t - 2)
                sp.dma_start(x1[:, u], rows(scratch["x1"], t)).then_inc(s_x[u], 16)

            tiles2(sp, NT, tile)

        @block.gpsimd
        def _(pool):
            def step(i, u, on):
                if on(i):
                    pool.wait_ge(s_x2, i + 1)
                if on(i + 2):
                    pool.dma_start(x1r[:, u], rows(scratch["x1"], i + 2)).then_inc(s_xr[u], 16)
                if on(i):
                    pool.dma_start(rows(scratch["x2"], i), x2[:, u]).then_inc(s_ox[u], 16)

            step(-2, 0, lambda t: 0 <= t < NT)
            step(-1, 1, lambda t: 0 <= t < NT)
            with pool.Fori(0, NT // 2 - 1) as j:
                for u in range(2):
                    step(2 * j + u, u, lambda t: True)
            for i in (NT - 2, NT - 1):
                step(i, i % 2, lambda t: 0 <= t < NT)
            for u in range(2):
                pool.wait_ge(s_ox[u], 16 * NT // 2)

        @block.scalar
        def _(act):
            act.wait_ge(s_eps, 1)

            def high(k, t, dst, used):
                for h in range(2):
                    act.wait_ge(s_T[k], 2 * t + h + 1)
                    if h == 0 and not is_first(t, 1):
                        act.wait_ge(used, t)
                    act.activation(dst[:, 4 * h:4 * h + 4].rearrange("p k n -> p (k n)"), pT[:, h],
                                   ACT.Copy).then_inc(s_h[k], 1)

            def statistics(t, u, src, ss, sd, s_sq, s_sd, s_rs):
                act.activation(junk[:], src[:, u], ACT.Square, accum_out=ss[:, u:u + 1]).then_inc(s_sq, 1)
                act.wait_ge(s_sq, t + 1)
                if not is_first(t, 2):
                    act.wait_ge(s_rs, t - 1)
                act.activation(sd[:, u:u + 1], ss[:, u:u + 1], ACT.Sqrt, scale=1.0 / D, bias=eps[:]).then_inc(s_sd, 1)

            def step(i, u, on):
                if is_first(i, 1) and i == 0:
                    act.wait_ge(s_c, 48)
                    act.activation(r_hi[:], rraw[:], ACT.Copy).then_inc(s_rs0, 1)
                if on(i - 2):
                    act.wait_ge(s_x2, i - 1)
                    statistics(i - 2, u, x2, ssB, sdB, s_sqB, s_sdB, s_rsB)
                if on(i - 1):
                    high("p", i - 1, p_hi, s_V)
                if on(i + 1):
                    act.wait_ge(s_x[1 - u], landed(i + 1, 1 - u))
                    statistics(i + 1, 1 - u, x1, ssA, sdA, s_sqA, s_sdA, s_rsA)
                if on(i):
                    act.wait_ge(s_nb, i + 1)
                    for h in range(XH):
                        last = act.activation(pr[:, h], pS[:, h // 2, (h % 2) * MEM:(h % 2 + 1) * MEM], ACT.Exp,
                                              scale=rsA[:, u:u + 1], bias=nb[:, h:h + 1], accum_out=es[:, h:h + 1])
                    last.then_inc(s_e, 1)
                if on(i - 2):
                    high("h", i - 2, h_hi, s_R)
                if on(i - 2):
                    act.wait_ge(s_h3, i - 1)
                    if not is_first(i - 2, 1):
                        act.wait_ge(s_oh, 16 * i - 32)
                    act.dma_start(rows(scratch["h3"], i - 2), h3[:]).then_inc(s_oh, 16)
                if on(i + 1):
                    high("x", i + 1, t_hi, s_S)

            schedule(act, step)
            act.wait_ge(s_oh, 16 * NT)

        @block.vector
        def _(dve):
            dve.memset(eps[:], EPS).then_inc(s_eps, 1)

            def low(k, t, hi, lo):
                for h in range(2):
                    dve.wait_ge(s_h[k], 2 * t + h + 1)
                    cut = lambda x: x[:, 4 * h:4 * h + 4].rearrange("p k n -> p (k n)")
                    dve.tensor_tensor(cut(lo), pT[:, h], cut(hi), ALU.subtract).then_inc(s_l[k], 1)

            def step(i, u, on):
                if is_first(i, 1) and i == 0:
                    dve.wait_ge(s_c, 48)
                    dve.wait_ge(s_rs0, 1)
                    dve.tensor_tensor(r_lo[:], rraw[:], r_hi[:], ALU.subtract).then_inc(s_rs0, 1)
                if on(i - 2):
                    t = i - 2
                    dve.wait_ge(s_V, t + 1)
                    dve.wait_ge(s_xr[u], landed(t, u))
                    if not is_first(t, 2):
                        dve.wait_ge(s_ox[u], landed(t, u) - 16)
                    dve.tensor_tensor(x2[:, u], pV[:].rearrange("p a b -> p (a b)"), x1r[:, u], ALU.add).then_inc(s_x2, 1)
                if on(i - 3):
                    t = i - 3
                    dve.wait_ge(s_R, t + 1)
                    dve.tensor_tensor(logits[:, bass.ds(t, 1)].rearrange("p o n -> p (o n)"), pR[:, 0:NR], rbias[:],
                                      ALU.add).then_inc(s_L, 1)
                if on(i - 2):
                    t = i - 2
                    dve.wait_ge(s_sdB, t + 1)
                    dve.reciprocal(rsB[:, u:u + 1], sdB[:, u:u + 1]).then_inc(s_rsB, 1)
                    dve.wait_ge(s_rsB, t + 1)
                    if not is_first(t, 1):
                        dve.wait_ge(s_T["h"], 2 * t)
                        dve.wait_ge(s_oh, 16 * t)
                    dve.scalar_tensor_tensor(h3[:], x2[:, u], rsB[:, u:u + 1], gain[:], ALU.mult, ALU.mult
                                             ).then_inc(s_h3, 1)
                if on(i - 1):
                    low("p", i - 1, p_hi, p_lo)
                if on(i + 1):
                    dve.wait_ge(s_sdA, i + 2)
                    if not is_first(i + 1, 2):
                        dve.wait_ge(s_e, i)
                    dve.reciprocal(rsA[:, 1 - u:2 - u], sdA[:, 1 - u:2 - u]).then_inc(s_rsA, 1)
                if on(i):
                    st = Steps(dve, s_st, 2 * i)
                    dve.wait_ge(s_S, i + 1)
                    dve.wait_ge(s_rsA, i + 1)
                    st.done(dve.tensor_reduce(mx[:].rearrange("p (a b) -> p a b", a=2),
                                              pS[:].rearrange("p a (b m) -> p a b m", b=2), AX_X, ALU.max))
                    dve.tensor_scalar(nb[:], mx[:], rsA[:, u:u + 1], -1.0, ALU.mult, ALU.mult).then_inc(s_nb, 1)
                    dve.wait_ge(s_e, i + 1)
                    st.done(dve.reciprocal(re[:], es[:]))
                    dve.tensor_tensor(pr[:], pr[:], re[:].unsqueeze(2).to_broadcast([P, XH, MEM]), ALU.mult
                                      ).then_inc(s_pn, 1)
                if on(i - 2):
                    low("h", i - 2, h_hi, h_lo)
                if on(i + 1):
                    low("x", i + 1, t_hi, t_lo)

            schedule(dve, step)

        @block.tensor
        def _(pe):
            pe.wait_ge(s_id, 16)

            def turn(k, t, src, before):
                for h in range(2):
                    if before:
                        pe.wait_ge(s_l[before[0]], 2 * before[1] + h + 1)
                    for c in range(4):
                        last = pe.transpose(pT[:, h, c * P:(c + 1) * P], src[:, (4 * h + c) * P:(4 * h + c + 1) * P],
                                            ident[:])
                    last.then_inc(s_T[k], 1)

            def product(out, hi, lo, W, n):
                for k in range(KT):
                    last = mm3(pe, out[:, n], hi[:, k], lo[:, k], W[0][:, k, n * BANK:(n + 1) * BANK],
                               W[1][:, k, n * BANK:(n + 1) * BANK], k == 0, k == KT - 1)
                return last

            def step(i, u, on):
                if on(i - 1):
                    pe.wait_ge(s_pn, i)
                    turn("p", i - 1, pr[:].rearrange("p h m -> p (h m)"),
                         ("x", i) if on(i) else ("h", i - 3))
                if on(i):
                    pe.wait_ge(s_l["x"], 2 * i + 2)
                    if not is_first(i, 1):
                        pe.wait_ge(s_e, i)
                    product(pS, t_hi, t_lo, G, 0)
                    product(pS, t_hi, t_lo, G, 1).then_inc(s_S, 1)
                if on(i - 2):
                    pe.wait_ge(s_h3, i - 1)
                    turn("h", i - 2, h3, ("p", i - 1) if on(i - 1) else ("h", i - 3))
                if on(i - 1):
                    pe.wait_ge(s_l["p"], 2 * i)
                    if not is_first(i - 1, 1):
                        pe.wait_ge(s_x2, i - 1)
                    product(pV, p_hi, p_lo, VW, 0)
                if on(i + 1):
                    pe.wait_ge(s_x[1 - u], landed(i + 1, 1 - u))
                    turn("x", i + 1, x1[:, 1 - u],
                         ("h", i - 2) if on(i - 2) else ("p", i - 1) if on(i - 1) else None if i < 0 else ("x", i))
                if on(i - 1):
                    product(pV, p_hi, p_lo, VW, 1).then_inc(s_V, 1)
                if on(i - 2):
                    pe.wait_ge(s_l["h"], 2 * i - 2)
                    if is_first(i - 2, 1):
                        pe.wait_ge(s_rs0, 2)
                    else:
                        pe.wait_ge(s_L, i - 2)
                    for k in range(KT):
                        last = mm3(pe, pR[:, 0:NR], h_hi[:, k], h_lo[:, k], r_hi[:, k], r_lo[:, k], k == 0, k == KT - 1)
                    last.then_inc(s_R, 1)

            schedule(pe, step)


NCK = 6
CW = 4 * DE


def weight_chunk(io, e, c):
    w = io[("w_gate", "w_up", "w_down")[c // 2]][bass.ds(e, 1)]
    if c < 4:
        return w.rearrange("o (p k) n -> (o p) k n", p=P)[:, c % 2 * 4:(c % 2 + 1) * 4]
    return w.rearrange("o (k p) n -> (o p) k n", p=P)[:, c % 2 * 2:(c % 2 + 1) * 2]


def chunk_place(raw, c):
    return raw[:, c].rearrange("p (k n) -> p k n", k=4 if c < 4 else 2)


def routing(nc, io, logits, slot_tok, slot_w, slot_of, first_block, last_block, n_blocks, all_blocks, raw, w_hi, w_lo):
    ctx = ExitStack()
    with ctx:
        sb = lambda name, shape, dt=F32: ctx.enter_context(nc.sbuf_tensor("ro_" + name, shape, dt))
        ps = lambda name, shape, dt=F32: ctx.enter_context(nc.psum_tensor("ro_" + name, shape, dt))
        sem = lambda name: nc.alloc_semaphore(name="ro_" + name)
        NP = 2 * NT
        count = sb("count", [P, P])
        tri = sb("tri", [P, P])
        ones = sb("ones", [P, P])
        before = sb("before", [P, NE, NE])
        token = sb("token", [P, NT])
        tg = sb("tg", [P, NT, NG])
        d4, ex4 = sb("d4", [P, NT, NG]), sb("ex4", [P, NT, NG])
        gm, gw, gi = sb("gm", [P, NT]), sb("gw", [P, NT]), sb("gi", [P, NT])
        le = sb("le", [P, NT, NE])
        m1, m2, ei = sb("m1", [P, NT]), sb("m2", [P, NT]), sb("ei", [P, NT])
        oh = sb("oh", [P, 2, NT, NE])
        e2, w = sb("e2", [P, NT]), sb("w", [P, 2, NT])
        M, Mb = sb("M", [P, NT, NE]), sb("Mb", [P, NT + 1, NE])
        steps15 = sb("steps15", [P, NT - 1])
        steps63 = sb("steps63", [P, NBLK - 1])
        nbf, pbf = sb("nbf", [P, NE]), sb("pbf", [P, NE])
        lbf = sb("lbf", [P, NE])
        usedf = sb("usedf", [1, 1])
        slots = sb("slots", [P, NT, NE])
        sf, bf, rf = sb("sf", [P, NP]), sb("bf", [P, NP]), sb("rf", [P, NP])
        ohr = sb("ohr", [P, NP, P])
        ohb = sb("ohb", [P, NP, NBLK])
        reach = ohb[:, :, 0:NBLK - 1]
        over = ohr[:, 16:16 + NE * NT // P].rearrange("p a b -> p (a b)").rearrange("p (e f) -> p e f", e=NE)[:, :, 1:]
        prod = ohr[:, 0:NE * NE // P].rearrange("p a b -> p (a b)").rearrange("p (e f) -> p e f", e=NE)
        val = sb("val", [P, NP, 2, NBLK])
        pR, pN, pS = ps("pR", [P, BANK]), ps("pN", [P, BANK]), ps("pS", [P, BANK])
        s_c, s_st, s_d, s_ex = sem("const"), sem("steps"), sem("differences"), sem("exp")
        s_M, s_R, s_oh, s_S = sem("M"), sem("ranks"), sem("onehots"), sem("slots")
        s_wh, s_cnt = sem("w_hi"), sem("count")
        s_w = [sem("w%d" % c) for c in range(NCK)]
        block = ctx.enter_context(nc.Block())

        @block.sync
        def _(sp):
            sp.dma_start(count[:], io["count"]).then_inc(s_cnt, 16)
            for dst, src in ((tri, "tri"), (ones, "ones"), (before, "before"), (token, "token")):
                sp.dma_start(dst[:], io[src]).then_inc(s_c, 16)
            for c in range(NCK):
                sp.dma_start(chunk_place(raw, c), weight_chunk(io, 0, c)).then_inc(s_w[c], 16)

        @block.scalar
        def _(act):
            act.wait_ge(s_d, 1)
            act.activation(ex4[:], d4[:], ACT.Exp).then_inc(s_ex, 1)
            act.wait_ge(s_d, 2)
            act.activation(e2[:], m2[:], ACT.Exp).then_inc(s_ex, 1)
            for c in range(NCK):
                act.wait_ge(s_w[c], 16)
                act.activation(w_hi[:, c], raw[:, c], ACT.Copy).then_inc(s_wh, 1)

        @block.tensor
        def _(pe):
            pe.wait_ge(s_c, 64)
            pe.wait_ge(s_M, 1)
            flat = lambda x: x.rearrange("p i e -> p (i e)")
            pe.matmul(pR[:], lhsT=tri[:], rhs=flat(M[:]), start=True, stop=False)
            pe.matmul(pR[:], lhsT=ones[:], rhs=flat(Mb[:, 0:NT]), start=False, stop=True)
            pe.matmul(pN[:, 0:NE], lhsT=ones[:], rhs=Mb[:, NT], start=True, stop=True).then_inc(s_R, 1)
            pe.wait_ge(s_oh, 1)
            for n in range(NP):
                last = pe.matmul(pS[:, 0:2 * NBLK], lhsT=ohr[:, n], rhs=val[:, n].rearrange("p v b -> p (v b)"),
                                 start=n == 0, stop=n == NP - 1)
            last.then_inc(s_S, 1)

        @block.vector
        def _(dve):
            dve.wait_ge(s_cnt, 16)
            st = Steps(dve, s_st)
            wide = lambda x, n: x.unsqueeze(2).to_broadcast([P, x.shape[1], n])
            deep = lambda x, n: x.unsqueeze(1).to_broadcast([P, n, x.shape[1]])

            def first_of(equal, n, index):
                st.done(dve.scalar_tensor_tensor(equal, deep(count[:, 0:n], NT), -float(P), equal, ALU.add, ALU.mult))
                st.done(dve.tensor_reduce(index, equal, AX_X, ALU.min))
                st.done(dve.scalar_tensor_tensor(equal, deep(count[:, 0:n], NT), -float(P), wide(index, n),
                                                 ALU.add, ALU.is_equal))

            lg = logits[:, :, 0:NG]
            st.done(dve.tensor_reduce(gm[:], lg, AX_X, ALU.max))
            dve.tensor_tensor(d4[:], lg, wide(gm[:], NG), ALU.subtract).then_inc(s_d, 1)
            st.done(dve.tensor_tensor(tg[:], lg, wide(gm[:], NG), ALU.is_equal))
            first_of(tg[:], NG, gi[:])
            dve.wait_ge(s_ex, 1)
            st.done(dve.tensor_reduce(gw[:], ex4[:], AX_X, ALU.add))
            st.done(dve.reciprocal(gw[:], gw[:]))
            st.done(dve.tensor_scalar(tg[:], tg[:], -1.0, BIG, ALU.add, ALU.mult))
            st.done(dve.tensor_copy(le[:], logits[:, :, NG:]))
            st.done(dve.tensor_tensor(le[:].rearrange("p i (g e) -> p (i g) e", g=NG),
                                      le[:].rearrange("p i (g e) -> p (i g) e", g=NG),
                                      wide(tg[:].rearrange("p i g -> p (i g)"), EG), ALU.add))
            st.done(dve.tensor_reduce(m1[:], le[:], AX_X, ALU.max))
            st.done(dve.tensor_tensor(oh[:, 0], le[:], wide(m1[:], NE), ALU.is_equal))
            first_of(oh[:, 0], NE, ei[:])
            st.done(dve.scalar_tensor_tensor(le[:], oh[:, 0], -2 * BIG, le[:], ALU.mult, ALU.add))
            st.done(dve.tensor_reduce(m2[:], le[:], AX_X, ALU.max))
            st.done(dve.tensor_tensor(oh[:, 1], le[:], wide(m2[:], NE), ALU.is_equal))
            first_of(oh[:, 1], NE, ei[:])
            dve.tensor_tensor(m2[:], m2[:], m1[:], ALU.subtract).then_inc(s_d, 1)
            st.done(dve.tensor_tensor(M[:], oh[:, 0], oh[:, 1], ALU.add))
            st.done(dve.memset(Mb[:, 0], 0.0))
            for i in range(NT):
                last = dve.tensor_tensor(Mb[:, i + 1], Mb[:, i], M[:, i], ALU.add)
                if i + 1 < NT:
                    st.done(last)
            last.then_inc(s_M, 1)
            dve.wait_ge(s_ex, 2)
            st.done(dve.tensor_scalar(w[:, 0], e2[:], 1.0, None, ALU.add))
            st.done(dve.reciprocal(w[:, 0], w[:, 0]))
            st.done(dve.tensor_tensor(w[:, 0], w[:, 0], gw[:], ALU.mult))
            st.done(dve.tensor_tensor(w[:, 1], w[:, 0], e2[:], ALU.mult))
            dve.tensor_scalar(steps15[:], count[:, 1:NT], float(P), None, ALU.mult)
            st.done(dve.tensor_scalar(steps63[:], count[:, 1:NBLK], float(P), None, ALU.mult))
            dve.wait_ge(s_R, 1)
            st.done(dve.tensor_tensor(over, wide(pN[:, 0:NE], NT - 1), deep(steps15[:], NE), ALU.is_gt))
            st.done(dve.tensor_reduce(nbf[:], over, AX_X, ALU.add))
            st.done(dve.tensor_scalar(nbf[:], nbf[:], 1.0, None, ALU.add))
            dve.wait_ge(s_c, 64)
            st.done(dve.tensor_tensor(prod, before[:], deep(nbf[:], NE), ALU.mult))
            st.done(dve.tensor_reduce(pbf[:], prod, AX_X, ALU.add))
            dve.tensor_copy(n_blocks[:], nbf[0:1])
            dve.tensor_copy(first_block[:], pbf[0:1])
            st.done(dve.tensor_tensor(lbf[:], pbf[:], nbf[:], ALU.add))
            st.done(dve.tensor_scalar(lbf[:], lbf[:], -1.0, None, ALU.add))
            dve.tensor_copy(last_block[:], lbf[0:1])
            st.done(dve.tensor_tensor(usedf[:], pbf[0:1, NE - 1:NE], nbf[0:1, NE - 1:NE], ALU.add))
            dve.tensor_copy(all_blocks[:, 0:1], usedf[:])
            dve.tensor_scalar(all_blocks[:, 1:2], usedf[:], -1.0, float(NBLK), ALU.mult, ALU.add)
            st.done(dve.scalar_tensor_tensor(slots[:], deep(pbf[:], NT), float(P),
                                             pR[:].rearrange("p (i e) -> p i e", i=NT), ALU.mult, ALU.add))
            for k in range(2):
                st.done(dve.tensor_tensor(oh[:, k], oh[:, k], slots[:], ALU.mult))
            st.done(dve.tensor_reduce(sf[:], oh[:].rearrange("p k i e -> p (k i) e"), AX_X, ALU.add))
            dve.tensor_copy(slot_of[:], sf[:])
            st.done(dve.tensor_tensor(reach, wide(sf[:], NBLK - 1), deep(steps63[:], NP), ALU.is_ge))
            st.done(dve.tensor_reduce(bf[:], reach, AX_X, ALU.add))
            st.done(dve.scalar_tensor_tensor(rf[:], bf[:], -float(P), sf[:], ALU.mult, ALU.add))
            dve.tensor_tensor(ohr[:], wide(rf[:], P), deep(count[:], NP), ALU.is_equal)
            st.done(dve.tensor_tensor(ohb[:], wide(bf[:], NBLK), deep(count[:, 0:NBLK], NP), ALU.is_equal))
            for k in range(2):
                cut = slice(k * NT, (k + 1) * NT)
                dve.tensor_tensor(val[:, cut, 0], ohb[:, cut], wide(token[:], NBLK), ALU.mult)
                last = dve.tensor_tensor(val[:, cut, 1], ohb[:, cut], wide(w[:, k], NBLK), ALU.mult)
            last.then_inc(s_oh, 1)
            for c in range(4):
                dve.wait_ge(s_wh, c + 1)
                dve.tensor_tensor(w_lo[:, c], raw[:, c], w_hi[:, c], ALU.subtract)
            dve.wait_ge(s_S, 1)
            dve.tensor_copy(slot_tok[:, 0:NBLK], pS[:, 0:NBLK])
            dve.tensor_copy(slot_w[:, 0:NBLK], pS[:, NBLK:2 * NBLK])


def experts(nc, io, scratch, slot_tok, slot_w, first_block, last_block, n_blocks, all_blocks, raw, w_hi, w_lo):
    ctx = ExitStack()
    with ctx:
        sb = lambda name, shape, dt=F32: ctx.enter_context(nc.sbuf_tensor("ex_" + name, shape, dt))
        ps = lambda name, shape, dt=F32: ctx.enter_context(nc.psum_tensor("ex_" + name, shape, dt))
        sem = lambda name: nc.alloc_semaphore(name="ex_" + name)
        HT = DE // P
        ident = sb("ident", [P, P])
        row = sb("row", [P, 1], I32)
        xg = sb("xg", [P, D])
        xT_hi = sb("xT_hi", [P, KT, P], F32R)
        xT_lo = sb("xT_lo", [P, KT, P], F32R)
        sil = sb("sil", [P, DE])
        hm = sb("hm", [P, DE])
        hT_hi = sb("hT_hi", [P, HT, P], F32R)
        hT_lo = sb("hT_lo", [P, HT, P], F32R)
        y = sb("y", [P, D])
        zero = sb("zero", [P, D])
        warm = sb("warm", [P, 1])
        pG = ps("pG", [P, BANK])
        pU = [ps("pUa", [P, BANK]), ps("pUb", [P, BANK])]
        pT = ps("pT", [P, 2, BANK])
        pH = ps("pH", [P, BANK])
        pD = ps("pD", [P, 2, BANK])
        s_c, s_warm, s_zero, s_fill = sem("const"), sem("warm"), sem("zero"), sem("filled")
        s_w = [sem("w%d" % c) for c in range(NCK)]
        s_hi, s_lo = sem("w_hi"), sem("w_lo")
        s_row, s_asked, s_x = sem("row"), sem("asked"), sem("rows")
        s_T, s_xh, s_xl = sem("T"), sem("xT_hi"), sem("xT_lo")
        s_G, s_U, s_sil, s_hm = sem("gate"), sem("up"), sem("silu"), sem("hidden")
        s_TH, s_hh, s_hl = sem("TH"), sem("hT_hi"), sem("hT_lo")
        s_D, s_y, s_yo, s_stored = sem("down"), sem("y"), sem("y_out"), sem("all_stored")
        flat = lambda x, h: x[:, 2 * h:2 * h + 2].rearrange("p k n -> p (k n)")
        ysr = scratch["ys"].rearrange("(b p) d -> b p d", p=P)
        block = ctx.enter_context(nc.Block())

        def each_block(eng, body):
            def expert(e, more):
                n = eng.value_load(n_blocks[0:1, bass.ds(e, 1)], min_val=1, max_val=NT)
                first = eng.value_load(first_block[0:1, bass.ds(e, 1)], min_val=0, max_val=NBLK - 2)
                final = eng.value_load(last_block[0:1, bass.ds(e, 1)], min_val=0, max_val=NBLK - 2)
                with eng.If(n > 1):
                    with eng.Fori(0, n - 1) as j:
                        body(first + j, e, False, more)
                body(final, e, True, more)

            with eng.Fori(0, NE - 1) as e:
                expert(e, True)
            expert(NE - 1, False)

        @block.sync
        def _(sp):
            sp.dma_start(ident[:], io["ident"]).then_inc(s_c, 16)

            def load(e):
                for c in range(NCK):
                    sp.wait_ge(s_lo, NCK * e - NCK + c + 1)
                    sp.dma_start(chunk_place(raw, c), weight_chunk(io, e, c)).then_inc(s_w[c], 16)

            with sp.Fori(1, NE) as e:
                load(e)
            sp.wait_ge(s_zero, 1)
            used = sp.value_load(all_blocks[0:1, 0:1], min_val=NE, max_val=NBLK - 1)
            with sp.Fori(used, NBLK) as b:
                sp.dma_start(ysr[bass.ds(b, 1)].rearrange("o p d -> (o p) d"), zero[:]).then_inc(s_fill, 16)
            unused = sp.value_load(all_blocks[0:1, 1:2], min_val=1, max_val=NBLK - NE)
            sp.wait_ge(s_fill, 16 * unused)
            sp.sem_inc(s_stored, 1)

        @block.gpsimd
        def _(pool):
            def gather(b):
                pool.tensor_copy(row[:], slot_tok[:, bass.ds(b, 1)]).then_inc(s_row, 1)
                pool.wait_ge(s_row, b + 1)
                pool.sem_inc(s_asked, 1)
                pool.indirect_dma_start(out=xg[:], out_offset=None, in_=scratch["h3"],
                                        in_offset=bass.IndirectOffsetOnAxis(ap=row[:].bitcast(U32), axis=0)
                                        ).then_inc(s_x, 16)

            pool.memset(zero[:], 0.0).then_inc(s_zero, 1)
            gather(0)
            used = pool.value_load(all_blocks[0:1, 0:1], min_val=NE, max_val=NBLK - 1)
            with pool.Fori(0, used) as b:
                pool.wait_ge(s_T, 2 * b + 2)
                gather(b + 1)

        @block.scalar
        def _(act):
            def high(e, c):
                act.wait_ge(s_w[c], 16 * e)
                act.activation(w_hi[:, c], raw[:, c], ACT.Copy).then_inc(s_hi, 1)

            def turned(b, h):
                act.wait_ge(s_T, 2 * b + h + 1)
                act.activation(xT_hi[:, 4 * h:4 * h + 4].rearrange("p k n -> p (k n)"), pT[:, h], ACT.Copy).then_inc(s_xh, 1)

            act.sem_inc(s_sil, 1)
            act.sem_inc(s_y, 1)
            act.dma_start(y[:, 0:P], io["ident"]).then_inc(s_yo, 16)
            act.wait_ge(s_c, 16)
            act.activation(warm[:], ident[:, 0:1], ACT.Silu).then_inc(s_warm, 1)
            for h in range(2):
                turned(0, h)

            def hidden(b, h):
                act.wait_ge(s_TH, 2 * b + h + 1)
                act.activation(flat(hT_hi, h), pH[:, 0:2 * P], ACT.Copy).then_inc(s_hh, 1)

            def body(b, e, last, more):
                act.wait_ge(s_G, b + 1)
                act.wait_ge(s_hm, 2 * b + 2)
                act.activation(sil[:], pG[:], ACT.Silu).then_inc(s_sil, 1)
                if last and more:
                    high(e + 1, 0)
                    high(e + 1, 1)
                act.wait_ge(s_D, b + 1)
                hidden(b, 0)
                act.wait_ge(s_U, 2 * b + 2)
                turned(b + 1, 0)
                hidden(b, 1)
                turned(b + 1, 1)
                if last and more:
                    high(e + 1, 2)
                    high(e + 1, 3)
                act.wait_ge(s_D, b + 2)
                act.wait_ge(s_yo, 16 * b + 16)
                act.activation(y[:], pD[:].rearrange("p a b -> p (a b)"), ACT.Identity,
                               scale=slot_w[:, bass.ds(b, 1)]).then_inc(s_y, 1)
                act.wait_ge(s_y, b + 2)
                act.dma_start(ysr[bass.ds(b, 1)].rearrange("o p d -> (o p) d"), y[:]).then_inc(s_yo, 16)
                if last and more:
                    high(e + 1, 4)
                    high(e + 1, 5)
                if last and not more:
                    act.wait_ge(s_yo, 16 * b + 32)
                    act.sem_inc(s_stored, 1)

            each_block(act, body)

        @block.vector
        def _(dve):
            def low(e, c):
                if not is_first(e, 1):
                    dve.wait_ge(s_hi, NCK * e - NCK + c + 1)
                dve.tensor_tensor(w_lo[:, c], raw[:, c], w_hi[:, c], ALU.subtract).then_inc(s_lo, 1)

            def turned(b, h):
                dve.wait_ge(s_xh, 2 * b + h + 1)
                cut = lambda x: x[:, 4 * h:4 * h + 4].rearrange("p k n -> p (k n)")
                dve.tensor_tensor(cut(xT_lo), pT[:, h], cut(xT_hi), ALU.subtract).then_inc(s_xl, 1)

            dve.sem_inc(s_hm, 2)
            dve.sem_inc(s_hl, 2)
            dve.sem_inc(s_lo, 4)
            for h in range(2):
                turned(0, h)
            low(0, 4)
            low(0, 5)

            def product(b, h):
                dve.wait_ge(s_U, 2 * b + h + 1)
                half = slice(h * 2 * P, (h + 1) * 2 * P)
                dve.tensor_tensor(hm[:, half], sil[:, half], pU[h][:, 0:2 * P], ALU.mult).then_inc(s_hm, 1)

            def hidden(b, h):
                dve.wait_ge(s_hh, 2 * b + h + 1)
                dve.tensor_tensor(flat(hT_lo, h), pH[:, 0:2 * P], flat(hT_hi, h), ALU.subtract).then_inc(s_hl, 1)

            def body(b, e, last, more):
                dve.wait_ge(s_sil, b + 2)
                product(b, 0)
                if last and more:
                    low(e + 1, 0)
                hidden(b, 0)
                product(b, 1)
                turned(b + 1, 0)
                hidden(b, 1)
                turned(b + 1, 1)
                if last and more:
                    for c in range(1, NCK):
                        low(e + 1, c)

            each_block(dve, body)

        @block.tensor
        def _(pe):
            pe.sem_inc(s_D, 1)
            pe.wait_ge(s_c, 16)

            def turn(b, h):
                pe.wait_ge(s_x, 16 * b + 16)
                rows = xg[:].rearrange("p (q c) -> p q c", c=KT)
                for k in range(4):
                    ins = pe.transpose(pT[:, h, k * P:(k + 1) * P], rows[:, :, 4 * h + k], ident[:])
                ins.then_inc(s_T, 1)

            for h in range(2):
                turn(0, h)

            def body(b, e, last, more):
                wh = w_hi[:].rearrange("p k (c n) -> p (k c) n", n=DE)
                wl = w_lo[:].rearrange("p k (c n) -> p (k c) n", n=DE)
                pe.wait_ge(s_xl, 2 * b + 2)
                pe.wait_ge(s_lo, NCK * e + 2)
                pe.wait_ge(s_sil, b + 1)
                for k in range(KT):
                    ins = mm3(pe, pG[:], xT_hi[:, k], xT_lo[:, k], wh[:, k], wl[:, k], k == 0, k == KT - 1)
                ins.then_inc(s_G, 1)
                pe.wait_ge(s_lo, NCK * e + 4)

                def up(h, k):
                    cut = slice(h * 2 * P, (h + 1) * 2 * P)
                    return mm3(pe, pU[h][:, 0:2 * P], xT_hi[:, k], xT_lo[:, k], wh[:, KT + k, cut], wl[:, KT + k, cut],
                               k == 0, k == KT - 1)

                def turn_hidden(h):
                    pe.wait_ge(s_hm, 2 * b + h + 3)
                    pe.wait_ge(s_hl, 2 * b + h + 2)
                    for k in range(2):
                        ins = pe.transpose(pH[:, k * P:(k + 1) * P], hm[:, (2 * h + k) * P:(2 * h + k + 1) * P], ident[:])
                    ins.then_inc(s_TH, 1)

                for h in range(2):
                    pe.wait_ge(s_hm, 2 * b + h + 1)
                    for k in range(KT):
                        if h == 1 and k == KT // 2:
                            turn_hidden(0)
                        ins = up(h, k)
                    ins.then_inc(s_U, 1)
                turn(b + 1, 0)
                turn(b + 1, 1)
                turn_hidden(1)
                pe.wait_ge(s_lo, NCK * e + 6)
                pe.wait_ge(s_y, b + 1)
                wh = w_hi[:, 4:6].rearrange("p k (c n) -> p (k c) n", n=D)
                wl = w_lo[:, 4:6].rearrange("p k (c n) -> p (k c) n", n=D)
                for n in range(2):
                    cut = slice(n * BANK, (n + 1) * BANK)
                    for k in range(HT):
                        if n == 0 and k % 2 == 0:
                            pe.wait_ge(s_hl, 2 * b + k // 2 + 3)
                        ins = mm3(pe, pD[:, n], hT_hi[:, k], hT_lo[:, k], wh[:, k, cut], wl[:, k, cut], k == 0, k == HT - 1)
                ins.then_inc(s_D, 1)

            each_block(pe, body)


def combine(nc, io, scratch, slot_of, out):
    ctx = ExitStack()
    with ctx:
        sb = lambda name, shape, dt=F32: ctx.enter_context(nc.sbuf_tensor("co_" + name, shape, dt))
        sem = lambda name: nc.alloc_semaphore(name="co_" + name)
        gain = sb("gain", [P, D])
        eps = sb("eps", [P, 1])
        x2 = sb("x2", [P, 2, D])
        row = sb("row", [P, 2, 2], I32)
        ya, yb = sb("ya", [P, 2, D]), sb("yb", [P, 2, D])
        acc = sb("acc", [P, 2, D])
        res = sb("res", [P, 2, D])
        junk = sb("junk", [P, D], BF16)
        ss, sd, rs = sb("ss", [P, 2]), sb("sd", [P, 2]), sb("rs", [P, 2])
        s_c, s_eps = sem("gain"), sem("eps")
        s_row, s_asked = sem("row"), sem("asked")
        s_x = [sem("x0"), sem("x1")]
        s_a = [sem("ya0"), sem("ya1")]
        s_b = [sem("yb0"), sem("yb1")]
        s_y, s_acc, s_sq, s_sd, s_rs, s_r = (sem(n) for n in ("pair", "sum", "squares", "deviation", "rstd", "result"))
        s_o = [sem("o0"), sem("o1")]
        rows = lambda ap, t: ap.rearrange("(t p) d -> t p d", p=P)[bass.ds(t, 1)].rearrange("o p d -> (o p) d")
        block = ctx.enter_context(nc.Block())

        @block.sync
        def _(sp):
            sp.dma_start(gain[:], io["final_norm_g"]).then_inc(s_c, 16)

            def tile(t, u):
                if not is_first(t, 2):
                    sp.wait_ge(s_acc, t - 1)
                sp.dma_start(x2[:, u], rows(scratch["x2"], t)).then_inc(s_x[u], 16)

            tiles2(sp, NT, tile)

        @block.gpsimd
        def _(pool):
            def tile(t, u):
                if not is_first(t, 2):
                    pool.wait_ge(s_acc, t - 1)
                for k in range(2):
                    last = pool.tensor_copy(row[:, u, k:k + 1], slot_of[:, bass.ds(t + k * NT, 1)])
                last.then_inc(s_row, 1)
                pool.wait_ge(s_row, t + 1)
                pool.sem_inc(s_asked, 1)
                for k, (dst, done) in enumerate(((ya, s_a), (yb, s_b))):
                    pool.indirect_dma_start(out=dst[:, u], out_offset=None, in_=scratch["ys"][0:NBLK * P],
                                            in_offset=bass.IndirectOffsetOnAxis(
                                                ap=row[:, u, k:k + 1].bitcast(U32), axis=0)
                                            ).then_inc(done[u], 16)

            tiles2(pool, NT, tile)

        @block.vector
        def _(dve):
            dve.memset(eps[:], EPS).then_inc(s_eps, 1)

            def add(t, u):
                dve.wait_ge(s_a[u], landed(t, u))
                dve.wait_ge(s_b[u], landed(t, u))
                if not is_first(t, 2):
                    dve.wait_ge(s_r, t - 1)
                dve.tensor_tensor(acc[:, u], ya[:, u], yb[:, u], ALU.add).then_inc(s_y, 1)
                dve.wait_ge(s_y, t + 1)
                dve.wait_ge(s_x[u], landed(t, u))
                dve.tensor_tensor(acc[:, u], acc[:, u], x2[:, u], ALU.add).then_inc(s_acc, 1)

            def scale(t, u):
                dve.wait_ge(s_sd, t + 1)
                dve.reciprocal(rs[:, u:u + 1], sd[:, u:u + 1]).then_inc(s_rs, 1)
                dve.wait_ge(s_rs, t + 1)
                if not is_first(t, 2):
                    dve.wait_ge(s_o[u], landed(t, u) - 16)
                dve.scalar_tensor_tensor(res[:, u], acc[:, u], rs[:, u:u + 1], gain[:], ALU.mult, ALU.mult).then_inc(s_r, 1)

            add(0, 0)
            add(1, 1)
            dve.wait_ge(s_c, 16)
            scale(0, 0)
            add(2, 0)
            scale(1, 1)
            with dve.Fori(1, NT // 2 - 1) as i:
                add(2 * i + 1, 1)
                scale(2 * i, 0)
                add(2 * i + 2, 0)
                scale(2 * i + 1, 1)
            add(NT - 1, 1)
            scale(NT - 2, 0)
            scale(NT - 1, 1)

        @block.scalar
        def _(act):
            act.wait_ge(s_eps, 1)

            def square(t, u):
                act.wait_ge(s_acc, t + 1)
                act.activation(junk[:], acc[:, u], ACT.Square, accum_out=ss[:, u:u + 1]).then_inc(s_sq, 1)
                act.wait_ge(s_sq, t + 1)
                if not is_first(t, 2):
                    act.wait_ge(s_rs, t - 1)
                act.activation(sd[:, u:u + 1], ss[:, u:u + 1], ACT.Sqrt, scale=1.0 / D, bias=eps[:]).then_inc(s_sd, 1)

            def store(t, u):
                act.wait_ge(s_r, t + 1)
                act.dma_start(rows(out, t), res[:, u]).then_inc(s_o[u], 16)

            square(0, 0)
            square(1, 1)
            store(0, 0)
            square(2, 0)
            store(1, 1)
            with act.Fori(1, NT // 2 - 1) as i:
                square(2 * i + 1, 1)
                store(2 * i, 0)
                square(2 * i + 2, 0)
                store(2 * i + 1, 1)
            square(NT - 1, 1)
            store(NT - 2, 0)
            store(NT - 1, 1)
            for u in range(2):
                act.wait_ge(s_o[u], 16 * NT // 2)


def halves(a):
    a = np.asarray(a, np.float64)

    def round12(v):
        m, e = np.frexp(v)
        return np.ldexp(np.rint(m * 4096), e - 12)

    hi = round12(a)
    return np.stack([hi, round12(a - hi)]).astype(np.float32)


def tables():
    out = {"ident": np.eye(P, dtype=np.float32)}
    out["head_mean"] = np.kron(np.eye(2), np.full((HD, HD), 1.0 / HD)).astype(np.float32)
    d = np.arange(HD)
    cos = np.cos(2 * np.pi * np.outer(d, np.arange(NA)) / HD)
    sin = np.sin(2 * np.pi * np.outer(d, np.arange(1, NA - 1)) / HD)
    one = np.concatenate([cos, sin], 1) / np.sqrt(float(S * HD))
    out["dft64"] = halves(np.kron(np.eye(2), one))
    s1, k1, s2 = np.arange(P), np.arange(P), np.arange(R16)
    ang = 2 * np.pi * ((R16 * s1[None, :, None] + s2[:, None, None]) * k1[None, None, :] % S) / S
    tw = halves(np.concatenate([np.cos(ang), np.sin(ang)], 2))
    out["tw128"] = np.ascontiguousarray(tw.transpose(1, 0, 2, 3))
    ang = 2 * np.pi * (np.outer(np.arange(R16), np.arange(R16)) % R16) / R16
    c, s = (np.kron(np.eye(8), f(ang)) for f in (np.cos, np.sin))
    out["dft16"] = np.stack([halves(m) for m in (c, s, -s)])
    n = np.arange(P)
    out["count"] = np.broadcast_to(n, (P, P)).astype(np.float32)
    out["tri"] = (n[:, None] < n[None, :]).astype(np.float32)
    out["ones"] = np.ones((P, P), np.float32)
    e = np.arange(NE)
    out["before"] = np.broadcast_to(e[None, :] < e[:, None], (P, NE, NE)).astype(np.float32)
    out["token"] = (np.arange(NT)[None, :] * P + n[:, None]).astype(np.float32)
    return out


def laid_out(inputs):
    a = {k: np.asarray(v) for k, v in inputs.items()}
    cols = lambda v: np.ascontiguousarray(v.reshape(-1, P).T)
    order = np.arange(HD)
    order = np.concatenate([order[:NA], order[:NA - 1:-1]])
    perm = np.concatenate([np.arange(CONV), CONV + (np.arange(FG)[:, None] * HD + order).ravel()])
    out = tables()
    out["x"] = a["x"][0]
    out["mem"] = a["mem"][0]
    out["norm_mix_g"] = cols(a["norm_mix_g"][0])
    out["w_f_T"] = a["w_in"][0][:, 3 * CONV:].T
    out["w_conv"] = a["w_in"][0][:, :3 * CONV]
    out["conv_w"] = a["conv_w"][0].reshape(3, CT, P).transpose(2, 0, 1)
    out["conv_b"] = cols(a["conv_b"][0])
    out["head_norm_g"] = cols(a["head_norm_g"][0].reshape(-1)[perm])
    out["w_out"] = a["w_out"][0][perm]
    out["norm_mem_g"] = cols(a["norm_mem_g"][0])
    out["norm_xa_g"] = cols(a["norm_xa_g"][0])
    out["w_kv"] = a["w_kv"][0].reshape(KT, P, 2 * KT, P).transpose(2, 1, 0, 3).reshape(2 * KT, P, D)
    pair = lambda w: w.reshape(XH, 2, P, 2, D // 2).transpose(0, 3, 2, 1, 4).reshape(2 * XH, P, D)
    out["w_q"] = pair(a["w_q"][0].T)
    out["w_o"] = pair(a["w_o"][0])
    router = np.concatenate([a["w_route_group"][0], a["w_route_expert"][0]], 1)
    out["w_router"] = router.reshape(KT, P, NG + NE).transpose(1, 0, 2)
    spread = lambda v: np.broadcast_to(v, (P, v.size))
    out["b_router"] = spread(np.concatenate([a["b_route_group"][0], a["b_route_expert"][0]]))
    out["norm_ffn_g"] = spread(a["norm_ffn_g"][0])
    out["final_norm_g"] = spread(a["final_norm_g"])
    for name in ("w_gate", "w_up", "w_down"):
        out[name] = a[name][0]
    return {k: np.ascontiguousarray(v) for k, v in out.items()}


def build(nc, io, out):
    dram = lambda name, *shape: nc.dram_tensor(name, shape, F32).ap()
    scratch = {"z": dram("z", S, 2, 2, FFT), "yT": dram("yT", P, CT, 2, S + 2), "x1": dram("x1", S, D),
               "x2": dram("x2", S, D), "h3": dram("h3", S, D), "ys": dram("ys", NCOL * P, D)}

    def phase(body, *args):
        with nc.cleanup_on_exit():
            body(nc, io, *args)

    phase(fourier_front, scratch)
    phase(conv_half, scratch)
    sb = lambda ctx, name, shape, dt=F32: ctx.enter_context(nc.sbuf_tensor(name, shape, dt))
    with ExitStack() as ctx:
        yT = sb(ctx, "yT_fourier", [P, 2, CT, S], F32R)
        w_out = [sb(ctx, "w_out_" + h, [P, KT, D], F32R) for h in ("hi", "lo")]
        phase(fourier_back, scratch, yT, *w_out)
        phase(mixer_out, scratch, yT, *w_out)
    with ExitStack() as kept:
        logits = sb(kept, "logits", [P, NT, NG + NE])
        slot_tok = sb(kept, "slot_tok", [P, NCOL], I32)
        slot_w = sb(kept, "slot_w", [P, NCOL])
        slot_of = sb(kept, "slot_of", [P, 2 * NT], I32)
        first_block = sb(kept, "first_block", [1, NE], I32)
        last_block = sb(kept, "last_block", [1, NE], I32)
        n_blocks = sb(kept, "n_blocks", [1, NE], I32)
        all_blocks = sb(kept, "all_blocks", [1, 2], I32)
        with ExitStack() as ctx:
            G = [sb(ctx, "G_" + h, [P, KT, XH * MEM], F32R) for h in ("hi", "lo")]
            VW = [sb(ctx, "VW_" + h, [P, KT, D], F32R) for h in ("hi", "lo")]
            phase(attention_tables, G, VW)
            phase(attention, scratch, G, VW, logits)
        with ExitStack() as ctx:
            raw = sb(ctx, "expert_raw", [P, NCK, CW])
            w_hi = sb(ctx, "expert_hi", [P, NCK, CW], F32R)
            w_lo = sb(ctx, "expert_lo", [P, NCK, CW], F32R)
            phase(routing, logits, slot_tok, slot_w, slot_of, first_block, last_block, n_blocks, all_blocks, raw, w_hi, w_lo)
            phase(experts, scratch, slot_tok, slot_w, first_block, last_block, n_blocks, all_blocks, raw, w_hi, w_lo)
        phase(combine, scratch, slot_of, out)


def kernel(**inputs):
    import concourse.bacc as bacc
    from concourse.bass_utils import run_bass_kernel_spmd

    arrays = laid_out(inputs)
    nc = bacc.Bacc("TRN2", target_bir_lowering=False, num_devices=1)
    io = {k: nc.dram_tensor("in_" + k, v.shape, mybir.dt.from_np(v.dtype), kind="ExternalInput").ap()
          for k, v in arrays.items()}
    out = nc.dram_tensor("out", (S, D), F32, kind="ExternalOutput").ap()
    build(nc, io, out)
    result = run_bass_kernel_spmd(nc, [{"in_" + k: v for k, v in arrays.items()}], core_ids=[0])
    return np.asarray(result.results[0]["out"]).reshape(1, S, D)
```
